# Optimizing a Trainium2 kernel written in Bass

```python
import math
import jax, jax.numpy as jnp
from jax import lax
import numpy as np

D_MODEL = 1024
BATCH = 1
SEQ = 512
DEPTH = 2

N_A = DEPTH // 2
N_B = DEPTH - N_A

DIFF_HEADS = 8
DIFF_HEAD_DIM = 64
DIFF_V_DIM = 2 * DIFF_HEAD_DIM
DIFF_QK_WIDTH = DIFF_HEADS * 2 * DIFF_HEAD_DIM
DIFF_V_WIDTH = DIFF_HEADS * DIFF_V_DIM

MLA_HEADS = 8
MLA_NOPE = 128
MLA_ROPE = 64
MLA_V = 128
Q_LORA = 384
KV_LORA = 256

D_FF = 4 * D_MODEL

ROPE_THETA = 10000.0
EPS = 1e-6
SUBLN_EPS = 1e-5
Q_BLOCK = 128


def rms_norm(x, g, eps=EPS):
    xf = x.astype(jnp.float32)
    y = xf * lax.rsqrt(jnp.mean(xf * xf, axis=-1, keepdims=True) + eps)
    return (y * g.astype(jnp.float32)).astype(x.dtype)

def rope_tables(seq, dim):
    pos = jnp.arange(seq, dtype=jnp.float32)
    inv_freq = ROPE_THETA ** (-jnp.arange(0, dim, 2, dtype=jnp.float32) / dim)
    ang = pos[:, None] * inv_freq[None, :]
    return jnp.cos(ang), jnp.sin(ang)

def apply_rope(x, cos, sin):
    half = x.shape[-1] // 2
    x1, x2 = x[..., :half], x[..., half:]
    c = cos[None, :, None, :].astype(x.dtype)
    s = sin[None, :, None, :].astype(x.dtype)
    return jnp.concatenate([x1 * c - x2 * s, x2 * c + x1 * s], axis=-1)

def causal_mask(i, seq):
    q_pos = i * Q_BLOCK + jnp.arange(Q_BLOCK)
    k_pos = jnp.arange(seq)
    return k_pos[None, :] <= q_pos[:, None]

def diff_attention(hn, w_qkv, w_o, lq1, lk1, lq2, lk2, subln_g, lambda_init, cos, sin):
    B, S, _ = hn.shape
    H, d = DIFF_HEADS, DIFF_HEAD_DIM
    qkv = hn @ w_qkv
    q, k, v = jnp.split(qkv, [DIFF_QK_WIDTH, 2 * DIFF_QK_WIDTH], axis=-1)
    q = apply_rope(q.reshape(B, S, 2 * H, d), cos, sin).reshape(B, S, H, 2, d)
    k = apply_rope(k.reshape(B, S, 2 * H, d), cos, sin).reshape(B, S, H, 2, d)
    v = v.reshape(B, S, H, DIFF_V_DIM)
    lam = (jnp.exp(jnp.sum(lq1.astype(jnp.float32) * lk1.astype(jnp.float32)))
           - jnp.exp(jnp.sum(lq2.astype(jnp.float32) * lk2.astype(jnp.float32)))
           + lambda_init)
    scale = d ** -0.5
    nb = S // Q_BLOCK
    qb = q.reshape(B, nb, Q_BLOCK, H, 2, d).transpose(1, 0, 2, 3, 4, 5)

    def block(args):
        q_blk, i = args
        s = jnp.einsum('bqhcd,bkhcd->bhcqk', q_blk, k).astype(jnp.float32) * scale
        s = jnp.where(causal_mask(i, S)[None, None, None], s, -jnp.inf)
        p = jax.nn.softmax(s, axis=-1)
        a = p[:, :, 0] - lam * p[:, :, 1]
        return jnp.einsum('bhqk,bkhe->bqhe', a.astype(v.dtype), v)

    o = lax.map(block, (qb, jnp.arange(nb)))
    o = o.transpose(1, 0, 2, 3, 4).reshape(B, S, H, DIFF_V_DIM)
    o = rms_norm(o, subln_g, SUBLN_EPS) * (1.0 - lambda_init)
    return o.reshape(B, S, DIFF_V_WIDTH) @ w_o

def mla_shared_kv(h, kv_in_norm_g, w_dkv, kv_norm_g, w_ukv, cos, sin):
    B, S, _ = h.shape
    hn = rms_norm(h, kv_in_norm_g)
    ckv = hn @ w_dkv
    c, k_rope = ckv[..., :KV_LORA], ckv[..., KV_LORA:]
    c = rms_norm(c, kv_norm_g)
    kv = (c @ w_ukv).reshape(B, S, MLA_HEADS, MLA_NOPE + MLA_V)
    k_nope, v = kv[..., :MLA_NOPE], kv[..., MLA_NOPE:]
    k_rope = apply_rope(k_rope[:, :, None, :], cos, sin)[:, :, 0, :]
    return k_nope, k_rope, v

def mla_attention(hn, w_dq, q_norm_g, w_uq, w_o, k_nope, k_rope, v, cos, sin):
    B, S, _ = hn.shape
    H = MLA_HEADS
    cq = rms_norm(hn @ w_dq, q_norm_g)
    q = (cq @ w_uq).reshape(B, S, H, MLA_NOPE + MLA_ROPE)
    q_nope = q[..., :MLA_NOPE]
    q_rope = apply_rope(q[..., MLA_NOPE:], cos, sin)
    scale = (MLA_NOPE + MLA_ROPE) ** -0.5
    nb = S // Q_BLOCK
    qn_b = q_nope.reshape(B, nb, Q_BLOCK, H, MLA_NOPE).transpose(1, 0, 2, 3, 4)
    qr_b = q_rope.reshape(B, nb, Q_BLOCK, H, MLA_ROPE).transpose(1, 0, 2, 3, 4)

    def block(args):
        qn, qr, i = args
        s = (jnp.einsum('bqhd,bkhd->bhqk', qn, k_nope)
             + jnp.einsum('bqhr,bkr->bhqk', qr, k_rope)).astype(jnp.float32) * scale
        s = jnp.where(causal_mask(i, S)[None, None], s, -jnp.inf)
        p = jax.nn.softmax(s, axis=-1)
        return jnp.einsum('bhqk,bkhe->bqhe', p.astype(v.dtype), v)

    o = lax.map(block, (qn_b, qr_b, jnp.arange(nb)))
    o = o.transpose(1, 0, 2, 3, 4).reshape(B, S, H * MLA_V)
    return o @ w_o

def sq_relu_mlp(hn, w_up, w_down):
    return jnp.square(jax.nn.relu(hn @ w_up)) @ w_down

def _w(key, shape, fan_in):
    return jax.random.normal(key, shape, jnp.float32) * fan_in ** -0.5

def _g(key, shape):
    return 1.0 + 0.02 * jax.random.normal(key, shape, jnp.float32)

def first_inputs(seed: int = 0) -> dict:
    key = jax.random.key(seed)
    ks = jax.random.split(key, 24)
    return {
        "x": jax.random.normal(ks[0], (BATCH, SEQ, D_MODEL), jnp.float32),
        "attn_norm_g": _g(ks[1], (DEPTH, D_MODEL)),
        "w_qkv_a": _w(ks[2], (N_A, D_MODEL, 2 * DIFF_QK_WIDTH + DIFF_V_WIDTH), D_MODEL),
        "lambda_q1": 0.1 * jax.random.normal(ks[3], (N_A, DIFF_HEAD_DIM), jnp.float32),
        "lambda_k1": 0.1 * jax.random.normal(ks[4], (N_A, DIFF_HEAD_DIM), jnp.float32),
        "lambda_q2": 0.1 * jax.random.normal(ks[5], (N_A, DIFF_HEAD_DIM), jnp.float32),
        "lambda_k2": 0.1 * jax.random.normal(ks[6], (N_A, DIFF_HEAD_DIM), jnp.float32),
        "subln_g": _g(ks[7], (N_A, DIFF_V_DIM)),
        "w_o_a": _w(ks[8], (N_A, DIFF_V_WIDTH, D_MODEL), DIFF_V_WIDTH),
        "kv_in_norm_g": _g(ks[9], (D_MODEL,)),
        "w_dkv": _w(ks[10], (D_MODEL, KV_LORA + MLA_ROPE), D_MODEL),
        "kv_norm_g": _g(ks[11], (KV_LORA,)),
        "w_ukv": _w(ks[12], (KV_LORA, MLA_HEADS * (MLA_NOPE + MLA_V)), KV_LORA),
        "w_dq": _w(ks[13], (N_B, D_MODEL, Q_LORA), D_MODEL),
        "q_norm_g": _g(ks[14], (N_B, Q_LORA)),
        "w_uq": _w(ks[15], (N_B, Q_LORA, MLA_HEADS * (MLA_NOPE + MLA_ROPE)), Q_LORA),
        "w_o_b": _w(ks[16], (N_B, MLA_HEADS * MLA_V, D_MODEL), MLA_HEADS * MLA_V),
        "mlp_norm_g": _g(ks[17], (DEPTH, D_MODEL)),
        "w_up": _w(ks[18], (DEPTH, D_MODEL, D_FF), D_MODEL),
        "w_down": _w(ks[19], (DEPTH, D_FF, D_MODEL), D_FF),
        "final_norm_g": _g(ks[20], (D_MODEL,)),
    }

def first_block(x, attn_norm_g, w_qkv_a, lambda_q1, lambda_k1, lambda_q2, lambda_k2, subln_g, w_o_a,
              kv_in_norm_g, w_dkv, kv_norm_g, w_ukv, w_dq, q_norm_g, w_uq, w_o_b,
              mlp_norm_g, w_up, w_down, final_norm_g):
    S = x.shape[1]
    cos_a, sin_a = rope_tables(S, DIFF_HEAD_DIM)
    cos_b, sin_b = rope_tables(S, MLA_ROPE)
    h = x
    k_nope = k_rope = v = None
    for l in range(DEPTH):
        if l < N_A:
            lambda_init = 0.8 - 0.6 * math.exp(-0.3 * l)
            hn = rms_norm(h, attn_norm_g[l])
            h = h + diff_attention(hn, w_qkv_a[l], w_o_a[l], lambda_q1[l], lambda_k1[l],
                                   lambda_q2[l], lambda_k2[l], subln_g[l], lambda_init,
                                   cos_a, sin_a)
        else:
            if l == N_A:
                k_nope, k_rope, v = mla_shared_kv(h, kv_in_norm_g, w_dkv, kv_norm_g, w_ukv,
                                                  cos_b, sin_b)
            j = l - N_A
            hn = rms_norm(h, attn_norm_g[l])
            h = h + mla_attention(hn, w_dq[j], q_norm_g[j], w_uq[j], w_o_b[j],
                                  k_nope, k_rope, v, cos_b, sin_b)
        h = h + sq_relu_mlp(rms_norm(h, mlp_norm_g[l]), w_up[l], w_down[l])
    return rms_norm(h, final_norm_g)


DEPTH_2 = 1

HEAD_DIM = 64
MIX_WIDTH = D_MODEL
GROUP_WIDTH = MIX_WIDTH // 4
CONV_WIDTH = 3
POOL_WINDOWS = (2, 4, 8, 16)
POOL_GROUP = GROUP_WIDTH // len(POOL_WINDOWS)
DSA_HEADS = GROUP_WIDTH // HEAD_DIM
IDX_HEADS = 8
IDX_DIM = 64
DSA_TOPK_MAX = 256
MOBA_HEADS = GROUP_WIDTH // HEAD_DIM
MOBA_BLOCK = 256
MOBA_TOPB_MAX = 3
REL_BUCKETS = 32
REL_MAX_DIST = 128
N_ATTN_HEADS = DSA_HEADS + MOBA_HEADS
D_FF_2 = -(-8 * D_MODEL // (3 * 256)) * 256
PLE_DIM = 256
MOBA_Q_BLOCK = 64
RMS_EPS = 1e-6
SPLIT_SIZES = (GROUP_WIDTH, GROUP_WIDTH, GROUP_WIDTH,
               GROUP_WIDTH,
               GROUP_WIDTH, GROUP_WIDTH, GROUP_WIDTH, IDX_HEADS * IDX_DIM, IDX_DIM, IDX_HEADS,
               GROUP_WIDTH, GROUP_WIDTH, GROUP_WIDTH)
IN_COLS = sum(SPLIT_SIZES)


def rmsnorm(x, g):
    x32 = x.astype(jnp.float32)
    y = x32 * lax.rsqrt(jnp.mean(x32 * x32, axis=-1, keepdims=True) + RMS_EPS)
    return (y * g.astype(jnp.float32)).astype(x.dtype)

def rel_bucket(dist):
    n = jnp.maximum(dist, 0)
    max_exact = REL_BUCKETS // 2
    nf = jnp.maximum(n, 1).astype(jnp.float32)
    large = max_exact + (jnp.log(nf / max_exact) / math.log(REL_MAX_DIST / max_exact)
                         * (REL_BUCKETS - max_exact)).astype(jnp.int32)
    large = jnp.minimum(large, REL_BUCKETS - 1)
    return jnp.where(n < max_exact, n, large)

def short_conv_mixer(a_in, gate_c, gate_b, conv_w):
    h = gate_c * a_in
    y = lax.conv_general_dilated(h, conv_w[:, None, :].astype(h.dtype), window_strides=(1,),
                                 padding=[(CONV_WIDTH - 1, 0)],
                                 dimension_numbers=("NWC", "WIO", "NWC"),
                                 feature_group_count=h.shape[-1])
    return gate_b * y

def pool_mixer(v, pool_w, pool_scale):
    b, s, _ = v.shape
    v32 = v.astype(jnp.float32)
    cs = jnp.concatenate([jnp.zeros((b, 1, GROUP_WIDTH), jnp.float32), lax.cumsum(v32, axis=1)], axis=1)
    t = jnp.arange(s)
    outs = []
    for g, w in enumerate(POOL_WINDOWS):
        sl = slice(g * POOL_GROUP, (g + 1) * POOL_GROUP)
        c = cs[:, :, sl]
        upper = c[:, 1:]
        lower = jnp.concatenate([jnp.zeros((b, w - 1, POOL_GROUP), jnp.float32), c[:, :s + 1 - w]], axis=1)
        cnt = jnp.minimum(t + 1, w).astype(jnp.float32)[None, :, None]
        outs.append((upper - lower) / cnt - v32[:, :, sl])
    d = jnp.stack(outs, axis=2)
    y = jnp.einsum("bsgc,gcd->bsgd", d, pool_w.astype(jnp.float32)).reshape(b, s, GROUP_WIDTH)
    return (y * pool_scale.astype(jnp.float32)).astype(v.dtype)

def dsa_mixer(q, k, v, iq, ik, iw, bias_tab):
    b, s, nh, hd = q.shape
    topk = min(DSA_TOPK_MAX, s // 4)
    idx_scale = (IDX_HEADS ** -0.5) * (IDX_DIM ** -0.5)
    ik32 = ik.astype(jnp.float32)
    bidx = jnp.arange(b)[:, None, None]
    spos = jnp.arange(s)

    def chunk(c):
        t0 = c * Q_BLOCK
        tq = t0 + jnp.arange(Q_BLOCK)
        qc = lax.dynamic_slice_in_dim(q, t0, Q_BLOCK, axis=1).astype(jnp.float32)
        iqc = lax.dynamic_slice_in_dim(iq, t0, Q_BLOCK, axis=1).astype(jnp.float32)
        iwc = lax.dynamic_slice_in_dim(iw, t0, Q_BLOCK, axis=1).astype(jnp.float32)
        sc = jax.nn.relu(jnp.einsum("bqhd,bsd->bqhs", iqc, ik32))
        score = jnp.einsum("bqh,bqhs->bqs", iwc, sc) * idx_scale
        score = jnp.where(spos[None, None, :] <= tq[None, :, None], score, -jnp.inf)
        _, sel = lax.top_k(score, topk)
        valid = sel <= tq[None, :, None]
        kg = k[bidx, sel].astype(jnp.float32)
        vg = v[bidx, sel].astype(jnp.float32)
        logits = jnp.einsum("bqhd,bqkhd->bhqk", qc, kg) * (hd ** -0.5)
        bias = jnp.moveaxis(bias_tab.astype(jnp.float32)[:, rel_bucket(tq[None, :, None] - sel)], 0, 1)
        logits = jnp.where(valid[:, None], logits + bias, -jnp.inf)
        probs = jax.nn.softmax(logits, axis=-1)
        return jnp.einsum("bhqk,bqkhd->bqhd", probs, vg)

    out = lax.map(chunk, jnp.arange(s // Q_BLOCK))
    return out.transpose(1, 0, 2, 3, 4).reshape(b, s, nh * hd).astype(q.dtype)

def moba_mixer(q, k, v, bias_tab):
    b, s, nh, hd = q.shape
    nb = -(-s // MOBA_BLOCK)
    pad = nb * MOBA_BLOCK - s
    kp = jnp.pad(k, ((0, 0), (0, pad), (0, 0), (0, 0)))
    vp = jnp.pad(v, ((0, 0), (0, pad), (0, 0), (0, 0)))
    kblk = kp.reshape(b, nb, MOBA_BLOCK, nh, hd)
    kmean = jnp.mean(kblk.astype(jnp.float32), axis=2)
    kblk_t = kblk.transpose(0, 3, 1, 2, 4)
    vblk_t = vp.reshape(b, nb, MOBA_BLOCK, nh, hd).transpose(0, 3, 1, 2, 4)
    topb = min(MOBA_TOPB_MAX, nb - 1)
    scale = hd ** -0.5
    tab = bias_tab.astype(jnp.float32)
    bi = jnp.arange(b)[:, None, None, None]
    hi = jnp.arange(nh)[None, :, None, None]
    blk_off = jnp.arange(MOBA_BLOCK)

    def chunk(c):
        t0 = c * MOBA_Q_BLOCK
        tq = t0 + jnp.arange(MOBA_Q_BLOCK)
        ob = t0 // MOBA_BLOCK
        qc = lax.dynamic_slice_in_dim(q, t0, MOBA_Q_BLOCK, axis=1).astype(jnp.float32)
        ko = lax.dynamic_slice_in_dim(kp, ob * MOBA_BLOCK, MOBA_BLOCK, axis=1).astype(jnp.float32)
        vo = lax.dynamic_slice_in_dim(vp, ob * MOBA_BLOCK, MOBA_BLOCK, axis=1).astype(jnp.float32)
        spos_o = ob * MOBA_BLOCK + blk_off
        lo = jnp.einsum("bqhd,bshd->bhqs", qc, ko) * scale + tab[:, rel_bucket(tq[:, None] - spos_o[None, :])][None]
        lo = jnp.where((spos_o[None, :] <= tq[:, None])[None, None], lo, -jnp.inf)
        if topb == 0:
            po = jax.nn.softmax(lo, axis=-1)
            return jnp.einsum("bhqs,bshd->bqhd", po, vo)
        gate = jnp.einsum("bqhd,bnhd->bhqn", qc, kmean)
        gate = jnp.where(jnp.arange(nb)[None, None, None, :] < ob, gate, -jnp.inf)
        _, sel = lax.top_k(gate, topb)
        valid = sel < ob
        kg = kblk_t[bi, hi, sel].astype(jnp.float32)
        vg = vblk_t[bi, hi, sel].astype(jnp.float32)
        lp = jnp.einsum("bqhd,bhqnsd->bhqns", qc, kg) * scale
        spos_p = sel[..., None] * MOBA_BLOCK + blk_off
        lp = lp + tab[hi[..., None], rel_bucket(tq[None, None, :, None, None] - spos_p)]
        lp = jnp.where(valid[..., None], lp, -jnp.inf)
        npast = topb * MOBA_BLOCK
        logits = jnp.concatenate([lp.reshape(b, nh, MOBA_Q_BLOCK, npast), lo], axis=-1)
        probs = jax.nn.softmax(logits, axis=-1)
        pp = probs[..., :npast].reshape(b, nh, MOBA_Q_BLOCK, topb, MOBA_BLOCK)
        po = probs[..., npast:]
        return (jnp.einsum("bhqns,bhqnsd->bqhd", pp, vg) + jnp.einsum("bhqs,bshd->bqhd", po, vo))

    out = lax.map(chunk, jnp.arange(s // MOBA_Q_BLOCK))
    return out.transpose(1, 0, 2, 3, 4).reshape(b, s, nh * hd).astype(q.dtype)

def swiglu(h, w_gate_up, w_down):
    gu = h @ w_gate_up
    gate, up = jnp.split(gu, 2, axis=-1)
    return (jax.nn.silu(gate) * up) @ w_down

def second_inputs(seed: int = 0) -> dict:
    key = jax.random.key(seed)
    ks = jax.random.split(key, 20)
    f32 = jnp.float32

    def nrm(k, shape, scale):
        return jax.random.normal(k, shape, f32) * scale

    def gain(k, shape):
        return 1.0 + 0.05 * jax.random.normal(k, shape, f32)

    return {
        "x": nrm(ks[0], (BATCH, SEQ, D_MODEL), 1.0),
        "p": nrm(ks[1], (DEPTH_2, BATCH, SEQ, PLE_DIM), 1.0),
        "rel_bias": nrm(ks[2], (N_ATTN_HEADS, REL_BUCKETS), 0.5),
        "g_mix_pre": gain(ks[3], (DEPTH_2, D_MODEL)),
        "w_in": nrm(ks[4], (DEPTH_2, D_MODEL, IN_COLS), D_MODEL ** -0.5),
        "conv_w": nrm(ks[5], (DEPTH_2, CONV_WIDTH, GROUP_WIDTH), CONV_WIDTH ** -0.5),
        "pool_w": nrm(ks[6], (DEPTH_2, len(POOL_WINDOWS), POOL_GROUP, POOL_GROUP), POOL_GROUP ** -0.5),
        "pool_scale": gain(ks[7], (DEPTH_2, GROUP_WIDTH)),
        "w_out": nrm(ks[8], (DEPTH_2, MIX_WIDTH, D_MODEL), MIX_WIDTH ** -0.5),
        "g_mix_post": gain(ks[9], (DEPTH_2, D_MODEL)),
        "g_ffn_pre": gain(ks[10], (DEPTH_2, D_MODEL)),
        "w_gate_up": nrm(ks[11], (DEPTH_2, D_MODEL, 2 * D_FF_2), D_MODEL ** -0.5),
        "w_down": nrm(ks[12], (DEPTH_2, D_FF_2, D_MODEL), D_FF_2 ** -0.5),
        "g_ffn_post": gain(ks[13], (DEPTH_2, D_MODEL)),
        "g_ple": gain(ks[14], (DEPTH_2, D_MODEL)),
        "w_ple_gate": nrm(ks[15], (DEPTH_2, D_MODEL, D_MODEL), D_MODEL ** -0.5),
        "w_ple_proj": nrm(ks[16], (DEPTH_2, PLE_DIM, D_MODEL), PLE_DIM ** -0.5),
    }

def second_block(x, p, rel_bias, g_mix_pre, w_in, conv_w, pool_w, pool_scale, w_out, g_mix_post,
              g_ffn_pre, w_gate_up, w_down, g_ffn_post, g_ple, w_ple_gate, w_ple_proj):
    b, s, _ = x.shape
    split_at = tuple(int(o) for o in np.cumsum(SPLIT_SIZES)[:-1])

    def heads(t):
        return t.reshape(b, s, -1, HEAD_DIM)

    for i in range(DEPTH_2):
        h = rmsnorm(x, g_mix_pre[i])
        z = h @ w_in[i]
        (a_in, a_c, a_b, pv, cq, ck, cv, iq, ik, iw, dq, dk, dv) = jnp.split(z, split_at, axis=-1)
        ya = short_conv_mixer(a_in, a_c, a_b, conv_w[i])
        yb = pool_mixer(pv, pool_w[i], pool_scale[i])
        yc = dsa_mixer(heads(cq), heads(ck), heads(cv), iq.reshape(b, s, IDX_HEADS, IDX_DIM), ik, iw,
                       rel_bias[:DSA_HEADS])
        yd = moba_mixer(heads(dq), heads(dk), heads(dv), rel_bias[DSA_HEADS:])
        mix = jnp.concatenate([ya, yb, yc, yd], axis=-1) @ w_out[i]
        x = x + rmsnorm(mix, g_mix_post[i])
        f = swiglu(rmsnorm(x, g_ffn_pre[i]), w_gate_up[i], w_down[i])
        x = x + rmsnorm(f, g_ffn_post[i])
        gate = jax.nn.sigmoid(rmsnorm(x, g_ple[i]) @ w_ple_gate[i])
        x = x + gate * (p[i] @ w_ple_proj[i])
    return x


def setup_inputs(seed=0):
    out = dict(first_inputs(seed))
    for name, value in second_inputs(seed + 1).items():
        if name != "x":
            out[name + "_2"] = value
    return out


def reference(
    x, attn_norm_g, w_qkv_a, lambda_q1, lambda_k1, lambda_q2, lambda_k2, subln_g, w_o_a,
    kv_in_norm_g, w_dkv, kv_norm_g, w_ukv, w_dq, q_norm_g, w_uq, w_o_b, mlp_norm_g, w_up,
    w_down, final_norm_g, p_2, rel_bias_2, g_mix_pre_2, w_in_2, conv_w_2, pool_w_2,
    pool_scale_2, w_out_2, g_mix_post_2, g_ffn_pre_2, w_gate_up_2, w_down_2, g_ffn_post_2,
    g_ple_2, w_ple_gate_2, w_ple_proj_2,
):
    x = first_block(
        x, attn_norm_g, w_qkv_a, lambda_q1, lambda_k1, lambda_q2, lambda_k2, subln_g, w_o_a,
        kv_in_norm_g, w_dkv, kv_norm_g, w_ukv, w_dq, q_norm_g, w_uq, w_o_b, mlp_norm_g, w_up,
        w_down, final_norm_g,
    )
    return second_block(
        x, p_2, rel_bias_2, g_mix_pre_2, w_in_2, conv_w_2, pool_w_2, pool_scale_2, w_out_2,
        g_mix_post_2, g_ffn_pre_2, w_gate_up_2, w_down_2, g_ffn_post_2, g_ple_2, w_ple_gate_2,
        w_ple_proj_2,
    )


_drawn_inputs = setup_inputs


def setup_inputs(seed=0):
    import zlib

    import numpy as np

    out = dict(_drawn_inputs(seed))
    spreads = {}
    factors = {'lambda_q2': 8.0,
     'kv_in_norm_g': 7.063,
     'kv_norm_g': 7.062,
     'q_norm_g': 8.0,
     'pool_scale_2': 2.68,
     'g_ple_2': 23.573}
    for name, (base, spread) in spreads.items():
        noise = np.random.default_rng([zlib.crc32(name.encode()), seed]).standard_normal(out[name].shape)
        drawn = base * np.exp(spread * noise) if base else spread * noise
        out[name] = __import__('jax').numpy.asarray(drawn.astype(out[name].dtype))
    for name, factor in factors.items():
        out[name] = (out[name] * factor).astype(out[name].dtype)
    return out
```

```python
from contextlib import ExitStack

import numpy as np

import concourse.bass as bass
from concourse import mybir

F32 = mybir.dt.float32
F32R = mybir.dt.float32r
ALU = mybir.AluOpType
ACT = mybir.ActivationFunctionType
AX = mybir.AxisListType

P = 128
S = 512
QT = S // P
D = 1024
KD = D // P
CHUNK = 2048
HEADS = 8
FF = 4096
ROUNDS = FF // D
EPS = 1e-6
SUBLN_EPS = 1e-5
LAMBDA_INIT = 0.8 - 0.6
DIFF_SCALE = 64 ** -0.5
MLA_SCALE = (128 + 64) ** -0.5
BIG = 1e30

GAINS = {}


def _gain_columns():
    at = 0
    for name, n in (("attn0", 8), ("attn1", 8), ("kv_in", 8), ("mlp0", 8), ("mlp1", 8), ("final", 8),
                    ("mix_pre", 8), ("mix_post", 8), ("ffn_pre", 8), ("ffn_post", 8), ("ple", 8),
                    ("kv", 2), ("q", 3), ("subln", 1), ("pool_scale", 2), ("conv", 6)):
        GAINS[name] = (at, n)
        at += n
    return at


N_GAINS = _gain_columns()

STAGES = (
    ("qk", 8, 16), ("v", 4, 8), ("diff", 0, 64), ("wo_a", 4, 8), ("mlp0", 32, 64),
          ("dkv", 4, 7), ("ukv", 2, 16), ("uq", 3, 12), ("mla", 0, 32), ("wo_b", 4, 8), ("mlp1", 32, 64),
          ("w_in", 4, 8), ("idx", 0, 24), ("w_in2", 9, 18), ("att2a", 0, 12), ("pool", 0, 2), ("att2b", 0, 20),
          ("w_out", 4, 8), ("proj0", 1, 4), ("gu0", 8, 16), ("dn0", 4, 8), ("gu1", 8, 16), ("dn1", 4, 8),
          ("gu2", 6, 12), ("dn2", 4, 8), ("proj1", 1, 4), ("ple", 4, 8), ("end2", 0, 0))
C, T = {}, {}


def _plan():
    c = t = 0
    for name, n_chunks, n_tiles in STAGES:
        C[name], T[name] = c, t
        c, t = c + n_chunks, t + n_tiles
    return c, t


N_CHUNKS, N_TILES = _plan()

SQUARED = (8, 8, 8, 2, 3, 8, 8, 0, 8, 8, 8, 8)
ADDED = (7, 7, 7, 1, 2, 7, 0, 0, 7, 7, 7, 7)
N_NORMS = len(SQUARED)
SQ = [sum(SQUARED[:n]) for n in range(N_NORMS + 1)]
SSQ = [sum(ADDED[:n]) for n in range(N_NORMS + 1)]
STATS = [n if n < 7 else n - 1 for n in range(N_NORMS)]

IDX_HEADS, TOPK = 8, 128
IDX_SCALE = IDX_HEADS ** -0.5 * 64 ** -0.5
HEAD_SCALE = 64 ** -0.5
ROUNDS_TOP = TOPK // 8
TAKEN = -3e38
IDX_OFF = [0, 0, 2 * P, 5 * P]
BUCKETS, MAX_DIST = 32, 128
ROWS = 3 * P
PAD = 16
GU_TILES = (8, 8, 6)
HID2 = 2 * 8 * ROUNDS
N_SILU = sum(GU_TILES)
POOL_GROUPS = ((0, slice(0, 64), 0, 2), (0, slice(64, 128), 1, 4), (1, slice(0, 64), 2, 8), (1, slice(64, 128), 3, 16))
POOL_STEPS = (2, 2, 6, 6)
T_JOB = [T["att2a"] + 4 * j if j < 3 else T["att2b"] + 4 * (j - 3) for j in range(8)]
Q_TILES = ([T["w_in2"] + 4, T["w_in2"] + 5, T["w_in2"] + 6, T["w_in2"] + 7],
           [T["w_in"] + 6, T["w_in"] + 7, T["w_in2"], T["w_in2"] + 1])
NB_HEAD = (4, 5, 6, 7, 0, 1, 2, 3)

OFF = [P * i * (i + 1) // 2 for i in range(QT)]
ROWLEN = P * QT * (QT + 1) // 2


def build(nc, wst, xT, gains, cos, sin, ident_in, mask_in, lam, pT_in, tab_in, buckets_in, pool_w_in, pool_fix_in, outT):
    ctx = ExitStack()
    with ctx:
        def sem(name):
            return ctx.enter_context(nc.semaphore(name))

        base = [(nc.sbuf_base + 31) // 32 * 32]
        top = nc.sbuf_usable_end

        def at(name, shape, dt, offset):
            return nc.alloc_sbuf_tensor_at(name, shape, dt, offset=offset)

        def sb(name, shape, dt=F32):
            n = 4 * int(np.prod(shape[1:]))
            t = at(name, shape, dt, base[0])
            base[0] += (n + 31) // 32 * 32
            assert base[0] <= top, (name, base[0], top)
            return t

        h = sb("h", [P, KD, S])
        raw = [sb(f"raw{s}", [P, CHUNK]) for s in range(2)]
        whi = [sb(f"whi{s}", [P, CHUNK], F32R) for s in range(2)]
        wlo = [sb(f"wlo{s}", [P, CHUNK], F32R) for s in range(2)]
        xa_at = base[0]
        xa_hi, xa_lo = sb("xa_hi", [P, KD, S], F32R), sb("xa_lo", [P, KD, S], F32R)
        xb_at = base[0]
        xb_hi, xb_lo = sb("xb_hi", [P, KD, S], F32R), sb("xb_lo", [P, KD, S], F32R)
        cos_t, sin_t = sb("cos_t", [P, S]), sb("sin_t", [P, S])
        rstd_f = sb("rstd_f", [P, S])
        sq_tmp, ssq = sb("sq_tmp", [P, S]), sb("ssq", [P, S])
        gain = sb("gain", [P, N_GAINS])
        ident = sb("ident", [P, P])
        mask = sb("mask", [P, P])
        ones = sb("ones", [P, 1])
        ms_t, rstd_t = sb("ms_t", [P, QT * N_NORMS]), sb("rstd_t", [P, QT * N_NORMS])
        r1_sq, r1_ms, r12 = (sb(n, [P, QT]) for n in ("r1_sq", "r1_ms", "r12"))
        gain_sq = sb("gain_sq", [P, KD, 2])
        tab = sb("tab", [P, HEADS])
        iw = sb("iw", [P, QT, IDX_HEADS])
        top8 = sb("top8", [P, 8])
        pool_fix = sb("pool_fix", [P, 2, PAD])
        g_x2 = sb("g_x2", [P, KD])
        half_neg = sb("half_neg", [P, QT])
        lam_ab = sb("lam_ab", [P, 4])
        neg_lam = sb("neg_lam", [P, 1])
        gsub = sb("gsub", [P, 1])
        negmin = sb("negmin", [P, 2, 8])
        rowsum, rinv = sb("rowsum", [P, 2, 8]), sb("rinv", [P, 2, 8])
        coef2 = sb("coef2", [P, 2, QT])
        o_ss, o_ms, o_rstd = (sb(n, [P, QT]) for n in ("o_ss", "o_ms", "o_rstd"))
        G = base[0]
        K = 1024

        qk = at("qk", [P, 2, 2, 4, S], F32, G)
        v_tok = at("v_tok", [P, QT, D], F32, G + 32 * K)
        stage = [at(f"stage{s}", [P, 2, S], F32, G + 48 * K + 4 * K * s) for s in range(2)]
        probs = [at(f"probs{s}", [P, 2, ROWLEN], F32, xa_at + 10 * K * s) for s in range(2)]
        pT = [at(f"pT{s}", [P, ROWLEN], F32, xa_at + 20 * K + 5 * K * s) for s in range(2)]
        cq, sq_, ck, sk = (at(n, [P, S], F32, xb_at + 2 * K * j) for j, n in enumerate(("cq", "sq_", "ck", "sk")))
        rope_tmp = at("rope_tmp", [P, 2, S], F32, xb_at + 8 * K)
        o_raw = [at(f"o_raw{s}", [P, QT, P], F32, G + 56 * K + 2 * K * s) for s in range(2)]
        o_sq = sq_tmp
        lam_in = at("lam_in", [P, 4, 64], F32, G)
        bias_rows = at("bias_rows", [P, HEADS, ROWS], F32, G + 1 * K)
        buckets = at("buckets", [P, ROWS], F32, G + 13 * K)
        iq = at("iq", [P, 4, S], F32, G)
        ik = at("ik", [P, S], F32, G + 8 * K)
        idx_score = at("idx_score", [P, 9 * P], F32, G + 10 * K)
        idx_relu = at("idx_relu", [P, 2, S], F32, G + 15 * K)
        cq2, ck2 = (at(n, [P, 2, S], F32, G + (19 + 4 * j) * K) for j, n in enumerate(("cq2", "ck2")))
        cv = at("cv", [P, QT, 256], F32, G + 27 * K)
        dq2, dk2 = (at(n, [P, 2, S], F32, G + (31 + 4 * j) * K) for j, n in enumerate(("dq2", "dk2")))
        dv = at("dv", [P, QT, 256], F32, G + 39 * K)
        nbias = at("nbias", [P, HEADS, 2 * P], F32, G + 43 * K)
        conv_in, conv_gate, conv_y = (at(n, [P, 2, S], F32, G + (51 + 4 * j) * K)
                                      for j, n in enumerate(("conv_in", "conv_gate", "conv_y")))
        r1_f = at("r1_f", [P, S], F32, G + 64 * K)
        squares = at("squares", [P, KD, S], F32, G + 48 * K)
        pool_v = at("pool_v", [P, 2, PAD + S], F32, G)
        pool_s = [at(f"pool_s{j}", [P, PAD + S], F32, G + 4224 + 2112 * (j % 2) if j < 2 else xb_at + 24 * K + 2112 * (j - 2))
                  for j in range(4)]
        pool_d = at("pool_d", [P, 2, S], F32, G + 15 * K)
        conv_gate2 = at("conv_gate2", [P, 2, S], F32, G + 15 * K)
        probs2 = [at(f"probs2{s}", [P, ROWLEN], F32, xb_at + 5 * K * s) for s in range(2)]
        pT2 = [at(f"pT2{s}", [P, ROWLEN], F32, xb_at + 10 * K + 5 * K * s) for s in range(2)]
        o2 = [at(f"o2{s}", [P, QT, P], F32, xb_at + 20 * K + 2 * K * s) for s in range(2)]
        pool_w = at("pool_w", [P, 2, P], F32, xb_at + 30 * K)
        gate_t, silu_t, up_t, hid_t = (at(n, [P, 2, S], F32, G + 4 * K * j)
                                       for j, n in enumerate(("gate_t", "silu_t", "up_t", "hid_t")))
        branch_t = at("branch_t", [P, 2, S], F32, G + 16 * K)
        p_raw = at("p_raw", [P, 2, S], F32, G + 20 * K)
        p_hi, p_lo = (at(n, [P, 2, S], F32R, G + (24 + 4 * j) * K) for j, n in enumerate(("p_hi", "p_lo")))
        branch = at("branch", [P, KD, S], F32, G + 32 * K)
        projected = at("projected", [P, KD, S], F32, G + 48 * K)
        JOBS = [(dq2, dk2, dv, hd) for hd in range(4)] + [(cq2, ck2, cv, hd) for hd in range(4)]
        scratch = nc.dram_tensor("bias_scratch", (HEADS, P * ROWS), F32, kind="Internal").ap()
        rows_view = scratch.rearrange("h (p x) -> p h x", p=P)
        skewed = scratch[:, P - 1:P - 1 + P * (ROWS - 1)].rearrange("h (p x) -> p h x", p=P)[:, :, 0:2 * P]
        p_view = pT_in.rearrange("(k p) n -> p k n", p=P)
        out_view = outT.rearrange("(k p) n -> p k n", p=P)
        q_nope = at("q_nope", [P, HEADS, S], F32, xb_at)
        k_nope = at("k_nope", [P, HEADS, S], F32, xb_at + 16 * K)
        v_tok2 = at("v_tok2", [P, QT, D], F32, G)
        qr_eo = at("qr_eo", [P, 4, S], F32, G + 16 * K)
        k_eo = at("k_eo", [P, 2, S], F32, G + 24 * K)
        rope_tmp2 = at("rope_tmp2", [P, 2, S], F32, G + 28 * K)
        table2 = at("table2", [P, 2, S], F32, G + 32 * K)
        mla_qn = [at(f"mla_qn{s}", [P, S], F32, G + 28 * K + 2 * K * s) for s in range(2)]
        mla_qr = [at(f"mla_qr{s}", [P, S], F32, G + 32 * K + 2 * K * s) for s in range(2)]
        mla_kr = at("mla_kr", [P, S], F32, G + 36 * K)
        ckv = at("ckv", [P, 2, S], F32, G + 36 * K)
        ckv_hi, ckv_lo = (at(n, [P, 2, S], F32R, G + 40 * K + 4 * K * j) for j, n in enumerate(("ckv_hi", "ckv_lo")))
        cq_raw = at("cq_raw", [P, 3, S], F32, G + 48 * K)
        cq_hi, cq_lo = (at(n, [P, 3, S], F32R, G + 54 * K + 6 * K * j) for j, n in enumerate(("cq_hi", "cq_lo")))
        mla_probs = [at(f"mla_probs{s}", [P, ROWLEN], F32, G + 38 * K + 5 * K * s) for s in range(2)]
        mla_pT = [at(f"mla_pT{s}", [P, ROWLEN], F32, G + 48 * K + 5 * K * s) for s in range(2)]
        mla_o = [at(f"mla_o{s}", [P, QT, P], F32, G + 58 * K + 2 * K * s) for s in range(2)]
        u_tmp = at("u_tmp", [P, 2, S], F32, G)
        u_sq = at("u_sq", [P, 2, S], F32, G + 4 * K)
        assert G + 60 * K <= top, (G + 60 * K, top)

        ps = [ctx.enter_context(nc.psum_tensor(f"ps{b}", [P, S], F32)) for b in range(8)]
        STAT, BC, PT0, O_PS, OT = ps[6], ps[7], 4, ps[6], ps[7]

        raw_full = [sem(f"raw_full{s}") for s in range(2)]
        whi_done = sem("whi_done")
        wlo_done = sem("wlo_done")
        tile_done = sem("tile_done")
        bank_free = [sem(f"bank_free{b}") for b in range(4)]
        x_loaded = [sem(f"x_loaded{i}") for i in range(4)]
        const_loaded = sem("const_loaded")
        dve_const = sem("dve_const")
        xh_done = sem("xh_done")
        xl_done = sem("xl_done")
        hid_hi, hid_sq, hid_lo = sem("hid_hi"), sem("hid_sq"), sem("hid_lo")
        sq_done, ssq_done = sem("sq_done"), sem("ssq_done")
        stat_done, ms_done, rstd_t_done = sem("stat_done"), sem("ms_done"), sem("rstd_t_done")
        bc_done, rstd_f_done = sem("bc_done"), sem("rstd_f_done")
        table_done, rope_done = sem("table_done"), sem("rope_done")
        lam_done, lam_exp = sem("lam_done"), sem("lam_exp")
        kr_full = sem("kr_full")
        stage_full = [sem(f"stage_full{s}") for s in range(2)]
        mask_done, ri_done = sem("mask_done"), sem("ri_done")
        nm_done, rc_done, p2_done, a_done = sem("nm_done"), sem("rc_done"), sem("p2_done"), sem("a_done")
        tr_done, ptc_done = sem("tr_done"), sem("ptc_done")
        o_done, oc_done, sqo_done = sem("o_done"), sem("oc_done"), sem("sqo_done")
        oss_done, oms_done, orstd_done = sem("oss_done"), sem("oms_done"), sem("orstd_done")
        on_done, ot_done = sem("on_done"), sem("ot_done")
        rows_mm, rows_done, rows_stored, nbias_full = (sem(n) for n in ("rows_mm", "rows_done", "rows_stored", "nbias_full"))
        r12_done, small_done, idx_acc, top_done, sel_done = (sem(n) for n in ("r12_done", "small_done", "idx_acc", "top_done", "sel_done"))
        conv_x, conv_step, conv_out = sem("conv_x"), sem("conv_step"), sem("conv_out")
        pool_zero, pool_s_done, pool_fix_done, pool_d_done = (sem(n) for n in ("pool_zero", "pool_s_done", "pool_fix_done", "pool_d_done"))
        nb_masked, x2_done, p_full, poolw_full = sem("nb_masked"), sem("x2_done"), sem("p_full"), sem("poolw_full")
        res_done, branch_done, silu_done, gated_done, y_done = (sem(n) for n in ("res_done", "branch_done", "silu_done", "gated_done", "y_done"))
        out_done = sem("out_done")

        def gains_of(name):
            return lambda k: g(name, k)

        def gains_all(name):
            c0, n = GAINS[name]
            return gain[:, c0:c0 + n]

        def g(name, k):
            c0 = GAINS[name][0] + k
            return gain[:, c0:c0 + 1]

        X = dict(qkv=0, diff_o=8, mlp0=16, dkv=24, dq=32, ckv=40, cq=42, mla_o=45, mlp1=53, w_in=61, mix=69, p=77, ffn=79, ple=87)
        STAGE_DIFF = 64 * HEADS // 2
        NM_DIFF = 8 * HEADS
        NM_MLA = NM_DIFF + 4 * HEADS
        MASK2 = [NM_MLA + (4 * j if j < 4 else 16 + 7 * (j - 4)) for j in range(8)]

        x_view = xT.rearrange("(k p) n -> p k n", p=P)
        consts = [(gain[:, :], gains), (ident[:, :], ident_in), (cos_t[:, :], cos), (sin_t[:, :], sin),
                  (mask[:, :], mask_in), (lam_in[:, :, :].rearrange("p a b -> p (a b)"), lam.partition_broadcast(P)),
                  (tab[0:BUCKETS, :], tab_in), (buckets[0:BUCKETS, :], buckets_in),
                  (pool_fix[:, :, :].rearrange("p a b -> p (a b)"), pool_fix_in)]

        block = ctx.enter_context(nc.Block())

        @block.sync
        def _(sp):
            def load(c, slot):
                if not isinstance(c, int) or c >= 2:
                    sp.wait_ge(wlo_done, c - 1)
                sp.dma_start(raw[slot][:, :], wst[c]).then_inc(raw_full[slot], 16)

            def load_pairs(c0, c1):
                with sp.Fori(0, (c1 - c0) // 2) as i:
                    for s in range(2):
                        load(c0 + s + 2 * i, (c0 + s) % 2)
                if (c1 - c0) % 2:
                    load(c1 - 1, (c1 - 1) % 2)

            def stage_diff(par, half, first):
                if first:
                    sp.wait_ge(rope_done, 8)
                else:
                    sp.wait_ge(tile_done, T["diff"] + 8 * par + 16 * half - 8)
                for comp in range(2):
                    for hf in range(2):
                        src, dst = 32 * (2 * par + comp), 64 * comp + 32 * hf
                        sp.dma_start(stage[par][dst:dst + 32, :, :],
                                     qk[src:src + 32, hf, :, half, :]).then_inc(stage_full[par], 16)

            load(0, 0)
            load(1, 1)
            load_pairs(2, 14)
            stage_diff(0, 0, True)
            stage_diff(1, 0, True)
            with sp.Fori(1, HEADS // 2) as half:
                for par in range(2):
                    stage_diff(par, half, False)
            load_pairs(14, C["dkv"] + 2)
            load_pairs(C["dkv"] + 2, C["wo_b"] + 2)
            sp.wait_ge(rope_done, 9)
            for hf in range(2):
                sp.dma_start(mla_kr[32 * hf:32 * hf + 32, :], k_eo[0:32, hf, :]).then_inc(kr_full, 16)
            sp.wait_ge(rope_done, 11)
            for n in range(HEADS):
                par, rows = n % 2, slice(32 * (n % 4), 32 * (n % 4) + 32)
                if n >= 2:
                    sp.wait_ge(tile_done, T["mla"] + 4 * (n - 1))
                sp.dma_start(mla_qn[par][:, :], q_nope[:, n, :]).then_inc(stage_full[par], 16)
                for hf in range(2):
                    sp.dma_start(mla_qr[par][32 * hf:32 * hf + 32, :],
                                 qr_eo[rows, 2 * (n // 4) + hf, :]).then_inc(stage_full[par], 16)
            load_pairs(C["wo_b"] + 2, C["w_in"] + 4)
            sp.wait_ge(stat_done, STATS[6] + 1)
            sp.wait_ge(rows_stored, 16)
            sp.dma_start(nbias[:, :, :], skewed).then_inc(nbias_full, 16)
            load_pairs(C["w_in"] + 4, C["w_out"] + 1)
            sp.wait_ge(tile_done, T["att2a"])
            sp.dma_start(pool_w[:, :, :].rearrange("p a b -> p (a b)"), pool_w_in).then_inc(poolw_full, 16)
            load_pairs(C["w_out"] + 1, C["proj0"])
            sp.wait_ge(tile_done, T["w_out"] + 1)
            sp.dma_start(p_raw[:, :, :], p_view).then_inc(p_full, 16)
            load_pairs(C["proj0"], C["end2"])
            for k in range(KD):
                sp.wait_ge(y_done, k + 1)
                sp.dma_start(out_view[:, k, :], h[:, k, :]).then_inc(out_done, 16)

            sp.wait_ge(out_done, 16 * KD)

        @block.tensor
        def _(pe):
            def products(out, lhs_hi, lhs_lo, rhs_hi, rhs_lo, first, last):
                pe.matmul(out, lhs_hi, rhs_hi, start=first, stop=False)
                pe.matmul(out, lhs_hi, rhs_lo, start=False, stop=False)
                return pe.matmul(out, lhs_lo, rhs_hi, start=False, stop=last)

            def bank_ready(t, per=0, i=0):
                if not isinstance(i, int) or t // 4 + (per // 4) * i > 0:
                    pe.wait_ge(bank_free[t % 4], t // 4 + (per // 4) * i)

            def features(slot, c, t0, xhi, xlo, kt=KD, cols=256, n=2, per=0, i=0, ready=None, hook=None,
                         pair_hook=None):
                pe.wait_ge(wlo_done, c + 1)
                w_hi, w_lo = (w[slot][:, 0:kt * cols].rearrange("p (k m) -> p k m", k=kt) for w in (whi, wlo))
                for a0 in range(0, n, 2):
                    pair = range(a0, min(a0 + 2, n))
                    if pair_hook is not None:
                        pair_hook(a0)
                    for a in pair:
                        bank_ready(t0 + a, per, i)
                    for k in range(kt):
                        if hook is not None:
                            hook(k)
                        if ready is not None and a0 == 0:
                            pe.wait_ge(*ready(k))
                        for a in pair:
                            mm = products(ps[(t0 + a) % 4][:, :],
                                          w_hi[:, k, a * P:(a + 1) * P], w_lo[:, k, a * P:(a + 1) * P],
                                          xhi[:, k, :], xlo[:, k, :], k == 0, k == kt - 1)
                            if k == kt - 1:
                                mm.then_inc(tile_done, 1)

            def tokens(slot, c, t0, xhi, xlo, per=0, i=0):
                pe.wait_ge(wlo_done, c + 1)
                w_hi = whi[slot][:, :].rearrange("p (k m) -> p k m", k=KD)
                w_lo = wlo[slot][:, :].rearrange("p (k m) -> p k m", k=KD)
                for u in range(2):
                    bank_ready(t0 + u, per, i)
                    for half in range(2):
                        q = slice((2 * u + half) * P, (2 * u + half + 1) * P)
                        out = ps[(t0 + u) % 4][:, half * 256:half * 256 + 256]
                        for k in range(KD):
                            mm = products(out, xhi[:, k, q], xlo[:, k, q], w_hi[:, k, :], w_lo[:, k, :],
                                          k == 0, k == KD - 1)
                    mm.then_inc(tile_done, 1)

            def stat(n):
                pe.wait_ge(ssq_done, SSQ[n + 1])
                if n >= 8:
                    pe.wait_ge(on_done, 3 * HEADS)
                for q in range(QT):
                    mm = pe.matmul(STAT[:, q:q + 1], ssq[:, q * P:(q + 1) * P], ones[:, :], start=True, stop=True)
                mm.then_inc(stat_done, 1)

            def broadcast(n, src=None):
                if src is None:
                    pe.wait_ge(rstd_t_done, n + 1)
                    src = rstd_t[:, 4 * n:4 * n + 4]
                for q in range(QT):
                    mm = pe.matmul(BC[:, q * P:(q + 1) * P], src[:, q:q + 1].to_broadcast([P, P]), ident[:, :],
                                   start=True, stop=True)
                mm.then_inc(bc_done, 1)

            def linear(stage, pairs, xhi, xlo, ready, norm=None, hook=None):
                c, t = C[stage], T[stage]
                features(c % 2, c, t, xhi, xlo, ready=ready, hook=hook)
                if norm is not None:
                    stat(norm)
                features((c + 1) % 2, c + 1, t + 2, xhi, xlo,
                         hook=(lambda k: broadcast(norm) if k == 4 else None) if norm is not None else None)
                with pe.Fori(1, pairs) as i:
                    for s in range(2):
                        features((c + s) % 2, c + s + 2 * i, t + 2 * s, xhi, xlo, per=4, i=i)

            def mlp(stage, norm, xhi, xlo, hhi, hlo, x0, hid0):
                c, t = C[stage], T[stage]

                def one_round(r, first):
                    for u in range(4):
                        features((c + u) % 2, c + u + 8 * r, t + 2 * u, xhi, xlo, per=16, i=r,
                                 ready=(lambda k: (xl_done, x0 + k + 1)) if first and u == 0 else None,
                                 hook=(lambda k: broadcast(norm) if k == 4 else None) if first and u == 1 else None)
                        if first and u == 0:
                            stat(norm)
                    for d in range(4):
                        features((c + d) % 2, c + 4 + d + 8 * r, t + 8 + 2 * d, hhi, hlo, per=16, i=r,
                                 ready=(lambda k: (hid_lo, hid0 + 8 * r + k + 1)) if d == 0 else None)

                one_round(0, True)
                with pe.Fori(1, ROUNDS) as r:
                    one_round(r, False)

            pe.wait_ge(const_loaded, 16 * len(consts))
            pe.wait_ge(dve_const, 1)
            for hd in range(HEADS):
                b = 4 + hd % 4
                if hd >= 4:
                    pe.wait_ge(rows_done, hd - 3)
                pe.matmul(ps[b][:, 0:ROWS], tab[0:BUCKETS, hd:hd + 1].to_broadcast([BUCKETS, P]), buckets[0:BUCKETS, :],
                          start=True, stop=True).then_inc(rows_mm, 1)
            pe.wait_ge(rows_done, HEADS)
            linear("qk", 4, xa_hi, xa_lo, lambda k: (xl_done, X["qkv"] + k + 1), norm=0)
            with pe.Fori(0, 2) as i:
                for s in range(2):
                    tokens((C["v"] + s) % 2, C["v"] + s + 2 * i, T["v"] + 2 * s, xa_hi, xa_lo, per=4, i=i)

            def diff_scores(par, half):
                pe.wait_ge(stage_full[par], 64 * (half + 1))
                for i in range(QT):
                    for comp in range(2):
                        n = 8 * par + 2 * i + comp
                        bank_ready(T["diff"] + n, 16, half)
                        rows = slice(64 * comp, 64 * comp + 64)
                        pe.matmul(ps[(T["diff"] + n) % 4][:, 0:P * (i + 1)],
                                  stage[par][rows, 0, P * i:P * (i + 1)],
                                  stage[par][rows, 1, 0:P * (i + 1)], start=True, stop=True).then_inc(tile_done, 1)

            def transposes(src, ready, n):
                for i in range(QT):
                    pe.wait_ge(*ready(i))
                    if not (isinstance(n, int) and 4 * n + i < 2):
                        pe.wait_ge(ptc_done, 4 * n + i - 1)
                    for kt in range(i + 1):
                        mm = pe.transpose(ps[PT0 + i % 2][:, kt * P:(kt + 1) * P],
                                          src[:, OFF[i] + kt * P:OFF[i] + (kt + 1) * P], ident[:, :])
                    mm.then_inc(tr_done, 1)

            def weighted(src, vals, head, n, taken):
                if not (isinstance(n, int) and n < 1):
                    pe.wait_ge(taken, n)
                for i in range(QT):
                    pe.wait_ge(ptc_done, 4 * n + i + 1)
                    for kt in range(i + 1):
                        mm = pe.matmul(O_PS[:, i * P:(i + 1) * P], src[:, OFF[i] + kt * P:OFF[i] + (kt + 1) * P],
                                       vals[:, kt, bass.ts(head, P)], start=(kt == 0), stop=(kt == i))
                mm.then_inc(o_done, 1)

            def turn(src, n, x_before):
                pe.wait_ge(on_done, n + 1)
                if not (isinstance(n, int) and n < 1):
                    pe.wait_ge(xl_done, x_before)
                for i in range(QT):
                    mm = pe.transpose(OT[:, i * P:(i + 1) * P], src[:, i, :], ident[:, :])
                mm.then_inc(ot_done, 1)

            def diff_step(par, half, scores=True, turn_last=True):
                n = 2 * half + par
                if scores:
                    diff_scores(1 - par, half + par)
                transposes(probs[par][:, 0, :], lambda i: (a_done, 4 * n + i + 1), n)
                weighted(pT[par], v_tok, n, n, oc_done)
                if turn_last:
                    turn(o_raw[1 - par], n - 1, X["diff_o"] + n - 1)

            diff_scores(0, 0)
            diff_step(0, 0, turn_last=False)
            with pe.Fori(0, HEADS // 2 - 1) as i:
                diff_step(1, i)
                diff_step(0, i + 1)
            diff_step(1, HEADS // 2 - 1, scores=False)

            linear("wo_a", 2, xb_hi, xb_lo, lambda k: (xl_done, X["diff_o"] + k + 1),
                   hook=lambda k: turn(o_raw[1], HEADS - 1, X["diff_o"] + HEADS - 1) if k == 6 else None)
            mlp("mlp0", 1, xa_hi, xa_lo, xb_hi, xb_lo, X["mlp0"], 0)
            c, t = C["dkv"], T["dkv"]
            features(c % 2, c, t, xa_hi, xa_lo, ready=lambda k: (xl_done, X["dkv"] + k + 1))
            stat(2)
            features((c + 1) % 2, c + 1, t + 2, xa_hi, xa_lo, hook=lambda k: broadcast(2) if k == 4 else None)
            features(c % 2, c + 2, t + 4, xb_hi, xb_lo, ready=lambda k: (xl_done, X["dq"] + k + 1))
            features((c + 1) % 2, c + 3, t + 6, xb_hi, xb_lo, n=1)
            stat(3)
            c, t = C["ukv"], T["ukv"]
            features(c % 2, c, t, ckv_hi, ckv_lo, kt=2, cols=1024, n=8,
                     ready=lambda k: (xl_done, X["ckv"] + k + 1),
                     pair_hook=lambda a: broadcast(3) if a == 2 else None)
            pe.wait_ge(wlo_done, c + 2)
            stat(4)
            w_hi, w_lo = (w[(c + 1) % 2][:, :].rearrange("p (k m) -> p k m", k=2) for w in (whi, wlo))
            for q in range(QT):
                for half in range(2):
                    tt = t + 8 + 2 * q + half
                    bank_ready(tt)
                    for k in range(2):
                        rows, cols = slice(q * P, q * P + P), slice(512 * half, 512 * half + 512)
                        mm = products(ps[tt % 4][:, :], ckv_hi[:, k, rows], ckv_lo[:, k, rows],
                                      w_hi[:, k, cols], w_lo[:, k, cols], k == 0, k == 1)
                    mm.then_inc(tile_done, 1)
            broadcast(4)
            c, t = C["uq"], T["uq"]
            for u in range(3):
                features((c + u) % 2, c + u, t + 4 * u, cq_hi, cq_lo, kt=3, cols=512, n=4,
                         ready=(lambda k: (xl_done, X["cq"] + k + 1)) if u == 0 else None)

            def mla_scores(par, n):
                pe.wait_ge(stage_full[par], STAGE_DIFF + 48 * (n // 2 + 1) if isinstance(n, int) else
                           STAGE_DIFF + 48 + 24 * (n - par))
                for i in range(QT):
                    bank_ready(T["mla"] + i, 4, n)
                    b, w, q = ps[(T["mla"] + i) % 4], P * (i + 1), slice(P * i, P * i + P)
                    pe.matmul(b[:, 0:w], mla_qn[par][:, q], k_nope[:, n, 0:w], start=True, stop=False)
                    pe.matmul(b[:, 0:w], mla_qr[par][0:64, q], mla_kr[0:64, 0:w], start=False, stop=True)\
                        .then_inc(tile_done, 1)

            def mla_step(par, n, scores=True, turn_last=True):
                if scores:
                    mla_scores(1 - par, n + 1)
                transposes(mla_probs[par], lambda i: (bank_free[(T["mla"] + i) % 4], (T["mla"] + i) // 4 + 1 + n),
                           HEADS + n)
                weighted(mla_pT[par], v_tok2, n, HEADS + n, on_done)
                if turn_last:
                    turn(mla_o[1 - par], HEADS + n - 1, X["mla_o"] + n - 1)

            pe.wait_ge(kr_full, 32)
            mla_scores(0, 0)
            mla_step(0, 0, turn_last=False)
            with pe.Fori(0, HEADS // 2 - 1) as i:
                mla_step(1, 2 * i + 1)
                mla_step(0, 2 * i + 2)
            mla_step(1, HEADS - 1, scores=False)

            linear("wo_b", 2, xa_hi, xa_lo, lambda k: (xl_done, X["mla_o"] + k + 1),
                   hook=lambda k: turn(mla_o[1], 2 * HEADS - 1, X["mla_o"] + HEADS - 1) if k == 6 else None)
            mlp("mlp1", 5, xb_hi, xb_lo, xa_hi, xa_lo, X["mlp1"], 8 * ROUNDS)
            c, t = C["w_in"], T["w_in"]
            features(c % 2, c, t, xb_hi, xb_lo, ready=lambda k: (xl_done, X["w_in"] + k + 1))
            pe.wait_ge(sq_done, SQ[7])
            for q in range(QT):
                for k in range(KD):
                    mm = pe.matmul(STAT[:, 2 * q:2 * q + 2], squares[:, k, q * P:(q + 1) * P], gain_sq[:, k, :],
                                   start=(k == 0), stop=(k == KD - 1))
            mm.then_inc(stat_done, 1)

            def both_rstd(k):
                if k == 6:
                    pe.wait_ge(r12_done, 1)
                    broadcast(None, r12)

            features((c + 1) % 2, c + 1, t + 2, xb_hi, xb_lo, hook=both_rstd)
            pe.wait_ge(rstd_f_done, 7)
            broadcast(6)
            features(c % 2, c + 2, t + 4, xb_hi, xb_lo, n=1)
            bank_ready(t + 5)
            w_hi, w_lo = (w[c % 2][:, :].rearrange("p (k m) -> p k m", k=KD)[:, :, P:P + IDX_HEADS] for w in (whi, wlo))
            for q in range(QT):
                for k in range(KD):
                    rows = slice(q * P, q * P + P)
                    mm = products(ps[(t + 5) % 4][:, IDX_HEADS * q:IDX_HEADS * (q + 1)], xb_hi[:, k, rows],
                                  xb_lo[:, k, rows], w_hi[:, k, :], w_lo[:, k, :], k == 0, k == KD - 1)
            mm.then_inc(tile_done, 1)
            features((c + 1) % 2, c + 3, t + 6, xb_hi, xb_lo)
            t = T["idx"]
            for i in range(1, QT):
                for hd in range(IDX_HEADS):
                    tt = t + IDX_HEADS * (i - 1) + hd
                    bank_ready(tt)
                    if i == 1 and hd == 0:
                        for tile in range(T["w_in"], T["w_in"] + 5):
                            pe.wait_ge(bank_free[tile % 4], tile // 4 + 1)
                    rows = slice(64 * (hd % 2), 64 * (hd % 2) + 64)
                    pe.matmul(ps[tt % 4][:, 0:P * (i + 1)], iq[rows, hd // 2, P * i:P * i + P],
                              ik[rows, 0:P * (i + 1)], start=True, stop=True).then_inc(tile_done, 1)
            c, t = C["w_in2"], T["w_in2"]
            for u in range(9):
                if u in (1, 4):
                    tokens((c + u) % 2, c + u, t + 2 * u, xb_hi, xb_lo)
                else:
                    features((c + u) % 2, c + u, t + 2 * u, xb_hi, xb_lo)

            def scores2(jb):
                q, k, _, hd = JOBS[jb]
                rows = slice(64 * (hd % 2), 64 * (hd % 2) + 64)
                for i in range(QT):
                    tt = T_JOB[jb] + i
                    bank_ready(tt)
                    if jb in (0, 4) and i == 0:
                        for tile in Q_TILES[jb // 4]:
                            pe.wait_ge(bank_free[tile % 4], tile // 4 + 1)
                    pe.matmul(ps[tt % 4][:, 0:P * (i + 1)], q[rows, hd // 2, P * i:P * i + P],
                              k[rows, hd // 2, 0:P * (i + 1)], start=True, stop=True).then_inc(tile_done, 1)

            def step2(jb):
                _, _, v, hd = JOBS[jb]
                n = 2 * HEADS + jb
                if jb < 7:
                    scores2(jb + 1)
                transposes(probs2[jb % 2], lambda i: (bank_free[(T_JOB[jb] + i) % 4], (T_JOB[jb] + i) // 4 + 1), n)
                pe.wait_ge(on_done, n)
                for i in range(QT):
                    pe.wait_ge(ptc_done, 4 * n + i + 1)
                    for kt in range(i + 1):
                        mm = pe.matmul(O_PS[:, i * 64:(i + 1) * 64],
                                       pT2[jb % 2][:, OFF[i] + kt * P:OFF[i] + (kt + 1) * P],
                                       v[:, kt, 64 * hd:64 * hd + 64], start=(kt == 0), stop=(kt == i))
                mm.then_inc(o_done, 1)

            def turn2(pair):
                pe.wait_ge(on_done, 2 * HEADS + 2 * pair + 2)
                if pair:
                    pe.wait_ge(xl_done, X["mix"] + 4 + pair)
                for i in range(QT):
                    mm = pe.transpose(OT[:, i * P:(i + 1) * P], o2[pair % 2][:, i, :], ident[:, :])
                mm.then_inc(ot_done, 1)

            scores2(0)
            for jb in range(8):
                step2(jb)
                if jb == 1:
                    pe.wait_ge(pool_d_done, 4)
                    pe.wait_ge(poolw_full, 16)
                    for a in range(2):
                        tt = T["pool"] + a
                        bank_ready(tt)
                        pe.matmul(ps[tt % 4][:, :], pool_w[:, a, :], pool_d[:, a, :], start=True, stop=True)\
                            .then_inc(tile_done, 1)
                if jb >= 2 and jb % 2 == 0:
                    turn2((jb - 2) // 2)

            linear("w_out", 2, xa_hi, xa_lo, lambda k: (xl_done, X["mix"] + k + 1),
                   hook=lambda k: turn2(3) if k == 6 else None)

            def proj(u, ready):
                c, t = C[f"proj{u}"], T[f"proj{u}"]
                features(c % 2, c, t, p_hi, p_lo, kt=2, cols=512, n=4, ready=ready)

            proj(0, lambda k: (xl_done, X["p"] + k + 1))
            stat(8)
            broadcast(8)

            def gate_up(r, n, first):
                c, t = C[f"gu{r}"], T[f"gu{r}"]
                if first:
                    features(c % 2, c, t, xb_hi, xb_lo, ready=lambda k: (xl_done, X["ffn"] + k + 1))
                    stat(9)
                    features((c + 1) % 2, c + 1, t + 2, xb_hi, xb_lo,
                             hook=lambda k: broadcast(9) if k == 5 else None)
                with pe.Fori(1 if first else 0, n // 2) as i:
                    for s in range(2):
                        features((c + s) % 2, c + s + 2 * i, t + 2 * s, xb_hi, xb_lo, per=4, i=i)

            def down(r, n):
                c, t = C[f"dn{r}"], T[f"dn{r}"]
                for s in range(2):
                    features((c + s) % 2, c + s, t + 2 * s, xa_hi, xa_lo, kt=n,
                             ready=(lambda k: (hid_lo, HID2 + 8 * r + k + 1)) if s == 0 else None)
                for s in range(2):
                    features((c + s) % 2, c + 2 + s, t + 4 + 2 * s, xa_hi, xa_lo, kt=n)

            for r, n in enumerate(GU_TILES):
                gate_up(r, n, r == 0)
                down(r, n)
            proj(1, None)
            stat(10)
            broadcast(10)

            linear("ple", 2, xb_hi, xb_lo, lambda k: (xl_done, X["ple"] + k + 1), norm=11)

        @block.scalar
        def _(act):
            def hi(c0, j, t_before):
                slot = c0 % 2
                act.wait_ge(raw_full[slot], 16 * (c0 // 2 + 1) + 8 * j)
                if not isinstance(t_before, int) or t_before > 0:
                    act.wait_ge(tile_done, t_before)
                act.activation(whi[slot][:, :], raw[slot][:, :], ACT.Copy).then_inc(whi_done, 1)

            def bank_out(t, per=0, i=0):
                act.wait_ge(bank_free[t % 4], t // 4 + 1 + (per // 4) * i)

            def x_hi(dst, src, scale):
                act.activation(dst, src, ACT.Copy, scale=scale).then_inc(xh_done, 1)

            for i in range(4):
                act.dma_start(h[:, 2 * i:2 * i + 2, :], x_view[:, 2 * i:2 * i + 2, :]).then_inc(x_loaded[i], 16)
                for dst, src in consts[3 * i:3 * i + 3]:
                    act.dma_start(dst, src).then_inc(const_loaded, 16)
            act.wait_ge(const_loaded, 16 * len(consts))
            hi(0, 0, 0)
            for k in range(KD):
                act.wait_ge(x_loaded[k // 2], 16)
                x_hi(xa_hi[:, k, :], h[:, k, :], g("attn0", k))
            for hd in range(HEADS):
                act.wait_ge(rows_mm, hd + 1)
                act.activation(bias_rows[:, hd, :], ps[4 + hd % 4][:, 0:ROWS], ACT.Copy).then_inc(rows_done, 1)
            act.wait_ge(rows_done, HEADS)
            act.dma_start(rows_view, bias_rows[:, :, :]).then_inc(rows_stored, 16)
            act.wait_ge(lam_done, 2)
            act.activation(lam_ab[:, 2:4], lam_ab[:, 0:2], ACT.Exp).then_inc(lam_exp, 1)

            c, t = C["qk"], T["qk"]
            hi(c + 1, 0, 0)
            hi(c + 2, 0, t + 2)
            with act.Fori(1, 4) as i:
                for s in range(2):
                    hi(c + s + 1, 2 * i, t + 2 * s + 4 * i)

            c, t = C["v"], T["v"]
            act.wait_ge(rstd_t_done, 1)
            with act.Fori(0, 2) as i:
                for s in range(2):
                    hi(c + s + 1, 2 * i, t + 2 * s + 4 * i)
                    for u in range(2):
                        tt = t + 2 * s + u
                        act.wait_ge(tile_done, tt + 1 + 4 * i)
                        for half in range(2):
                            q = 2 * u + half
                            ins = act.activation(v_tok[:, q, bass.ds(256 * s + 512 * i, 256)],
                                                 ps[tt % 4][:, 256 * half:256 * half + 256],
                                                 ACT.Copy, scale=rstd_t[:, q:q + 1])
                        ins.then_inc(bank_free[tt % 4], 1)

            def diff_exp(par, half):
                n = 2 * half + par
                for i in range(QT):
                    for comp in range(2):
                        j = 2 * i + comp
                        b = (T["diff"] + 8 * par + j) % 4
                        act.wait_ge(nm_done, 8 * n + j + 1)
                        if j == 0 and not (isinstance(half, int) and half < 1):
                            act.wait_ge(tr_done, 4 * (n - 1))
                        act.activation(probs[par][:, comp, OFF[i]:OFF[i] + P * (i + 1)], ps[b][:, 0:P * (i + 1)],
                                       ACT.Exp, bias=negmin[:, par, j:j + 1], scale=-1.0,
                                       accum_out=rowsum[:, par, j:j + 1]).then_inc(bank_free[b], 1)

            def copy_pT(pT, par, n):
                for i in range(QT):
                    act.wait_ge(tr_done, 4 * n + i + 1)
                    if i == 0 and not (isinstance(n, int) and n < 2):
                        act.wait_ge(o_done, n - 1)
                    act.activation(pT[par][:, OFF[i]:OFF[i] + P * (i + 1)], ps[PT0 + i % 2][:, 0:P * (i + 1)],
                                   ACT.Copy).then_inc(ptc_done, 1)

            def diff_copy_o(par, n):
                act.wait_ge(o_done, n + 1)
                if not (isinstance(n, int) and n < 2):
                    act.wait_ge(ot_done, n - 1)
                act.activation(o_raw[par][:, :, :].rearrange("p a b -> p (a b)"), O_PS[:, :],
                               ACT.Copy).then_inc(oc_done, 1)

            def head_hi(dst, n, n0, scale):
                act.wait_ge(ot_done, n0 + n + 1)
                act.activation(dst[:, n, :], OT[:, :], ACT.Copy, scale=scale).then_inc(xh_done, 1)

            def diff_step(par, half, ahead=True, behind=True):
                n = 2 * half + par
                if ahead:
                    diff_exp(1 - par, half + par)
                copy_pT(pT, par, n)
                diff_copy_o(par, n)
                if behind:
                    head_hi(xb_hi, n - 1, 0, gsub[:, 0:1])

            act.wait_ge(dve_const, 4)
            diff_exp(0, 0)
            diff_step(0, 0, behind=False)
            diff_step(1, 0)
            with act.Fori(1, HEADS // 2 - 1) as half:
                diff_step(0, half)
                diff_step(1, half)
            diff_step(0, HEADS // 2 - 1)
            diff_step(1, HEADS // 2 - 1, ahead=False)
            head_hi(xb_hi, HEADS - 1, 0, gsub[:, 0:1])

            def residual(stage, dst, gname):
                c, t = C[stage], T[stage]
                for u in range(4):
                    hi(c + u + 1, 0, t + 2 * u)
                    for a in range(2):
                        bank_out(t + 2 * u + a)
                        x_hi(dst[:, 2 * u + a, :], h[:, 2 * u + a, :], gname(2 * u + a))

            def mlp(stage, hhi, dst, gname):
                c, t = C[stage], T[stage]

                def one_round(r, last):
                    for u in range(4):
                        hi(c + u + 1, 8 * r, t + 2 * u + 16 * r)
                        for a in range(2):
                            bank_out(t + 2 * u + a, 16, r)
                            act.activation(hhi[:, 2 * u + a, :], u_tmp[:, a, :], ACT.Square).then_inc(hid_hi, 1)
                    for d in range(4):
                        hi(c + d + 5, 8 * r, t + 8 + 2 * d + 16 * r)
                        if last:
                            for a in range(2):
                                bank_out(t + 8 + 2 * d + a, 16, r)
                                x_hi(dst[:, 2 * d + a, :], h[:, 2 * d + a, :], gname(2 * d + a))

                with act.Fori(0, ROUNDS - 1) as r:
                    one_round(r, False)
                one_round(ROUNDS - 1, True)

            residual("wo_a", xa_hi, gains_of("mlp0"))
            mlp("mlp0", xb_hi, xa_hi, gains_of("kv_in"))
            c, t = C["dkv"], T["dkv"]
            hi(c + 1, 0, t)
            for k in range(KD):
                x_hi(xb_hi[:, k, :], h[:, k, :], g("attn1", k))
            hi(c + 2, 0, t + 2)
            for a in range(2):
                bank_out(t + a)
                x_hi(ckv_hi[:, a, :], ckv[:, a, :], g("kv", a))
            hi(c + 3, 0, t + 4)
            hi(c + 4, 0, t + 6)
            for a in range(3):
                bank_out(t + 4 + a)
                x_hi(cq_hi[:, a, :], cq_raw[:, a, :], g("q", a))
            c, t = C["ukv"], T["ukv"]
            hi(c + 1, 0, t)
            hi(c + 2, 0, t + 8)
            act.wait_ge(rstd_t_done, 4)
            for q in range(QT):
                for half in range(2):
                    tt = t + 8 + 2 * q + half
                    act.wait_ge(tile_done, tt + 1)
                    act.activation(v_tok2[:, q, 512 * half:512 * half + 512], ps[tt % 4][:, :], ACT.Copy,
                                   scale=rstd_t[:, 12 + q:13 + q]).then_inc(bank_free[tt % 4], 1)
            c, t = C["uq"], T["uq"]
            for u in range(3):
                hi(c + u + 1, 0, t + 4 * u)

            def mla_exp(par, n):
                for i in range(QT):
                    b = (T["mla"] + i) % 4
                    act.wait_ge(nm_done, NM_DIFF + 4 * n + i + 1)
                    if i == 0 and not (isinstance(n, int) and n < 2):
                        act.wait_ge(tr_done, 4 * (HEADS + n - 1))
                    act.activation(mla_probs[par][:, OFF[i]:OFF[i] + P * (i + 1)], ps[b][:, 0:P * (i + 1)],
                                   ACT.Exp, bias=negmin[:, par, i:i + 1], scale=-1.0,
                                   accum_out=rowsum[:, par, i:i + 1]).then_inc(bank_free[b], 1)

            def mla_step(par, n, ahead=True, behind=True):
                if ahead:
                    mla_exp(1 - par, n + 1)
                copy_pT(mla_pT, par, HEADS + n)
                if behind:
                    head_hi(xa_hi, n - 1, HEADS, 1.0)

            mla_exp(0, 0)
            mla_step(0, 0, behind=False)
            with act.Fori(0, HEADS // 2 - 1) as i:
                mla_step(1, 2 * i + 1)
                mla_step(0, 2 * i + 2)
            mla_step(1, HEADS - 1, ahead=False)
            head_hi(xa_hi, HEADS - 1, HEADS, 1.0)

            residual("wo_b", xb_hi, gains_of("mlp1"))
            mlp("mlp1", xa_hi, xb_hi, lambda k: g_x2[:, k:k + 1])
            c, t = C["w_in"], T["w_in"]
            for u in range(4):
                hi(c + u + 1, 0, t + 2 * u)
            t = T["idx"]
            for j in range(IDX_HEADS * (QT - 1)):
                i, tt = 1 + j // IDX_HEADS, t + j
                act.wait_ge(tile_done, tt + 1)
                if j >= 2:
                    act.wait_ge(idx_acc, j - 1)
                act.activation(idx_relu[:, j % 2, 0:P * (i + 1)], ps[tt % 4][:, 0:P * (i + 1)], ACT.Relu)\
                    .then_inc(bank_free[tt % 4], 1)

            def take_tokens(dst, t):
                for u in range(2):
                    tt = t + u
                    act.wait_ge(tile_done, tt + 1)
                    for half in range(2):
                        q = 2 * u + half
                        ins = act.activation(dst[:, q, :], ps[tt % 4][:, 256 * half:256 * half + 256], ACT.Copy,
                                             scale=r12[:, q:q + 1])
                    ins.then_inc(bank_free[tt % 4], 1)

            act.wait_ge(r12_done, 1)
            c, t = C["w_in2"], T["w_in2"]
            for u in range(9):
                hi(c + u + 1, 0, t + 2 * u)
                if u in (1, 4):
                    take_tokens(cv if u == 1 else dv, t + 2 * u)
                if u == 8:
                    for a in range(2):
                        act.wait_ge(conv_out, a + 1)
                        x_hi(xa_hi[:, a, :], conv_y[:, a, :], 1.0)

            def exp2(jb):
                for i in range(QT):
                    b, j = (T_JOB[jb] + i) % 4, 4 * jb + i
                    act.wait_ge(nm_done, NM_MLA + j + 1)
                    if i == 0 and jb >= 2:
                        act.wait_ge(tr_done, 4 * (2 * HEADS + jb - 1))
                    act.activation(probs2[jb % 2][:, OFF[i]:OFF[i] + P * (i + 1)], ps[b][:, 0:P * (i + 1)],
                                   ACT.Exp, bias=negmin[:, jb % 2, i:i + 1], scale=-1.0,
                                   accum_out=rowsum[:, jb % 2, i:i + 1]).then_inc(bank_free[b], 1)

            def pair_hi(pair):
                act.wait_ge(ot_done, 2 * HEADS + pair + 1)
                x_hi(xa_hi[:, 4 + pair, :], OT[:, :], 1.0)

            exp2(0)
            for jb in range(8):
                if jb < 7:
                    exp2(jb + 1)
                copy_pT(pT2, jb % 2, 2 * HEADS + jb)
                if jb == 1:
                    for a in range(2):
                        act.wait_ge(tile_done, T["pool"] + a + 1)
                        x_hi(xa_hi[:, 2 + a, :], ps[(T["pool"] + a) % 4][:, :], g("pool_scale", a))
                if jb >= 2 and jb % 2 == 0:
                    pair_hi((jb - 2) // 2)
            pair_hi(3)

            def take_copy(dst, tt):
                act.wait_ge(tile_done, tt + 1)
                act.activation(dst, ps[tt % 4][:, :], ACT.Copy).then_inc(bank_free[tt % 4], 1)

            c, t = C["w_out"], T["w_out"]
            for u in range(4):
                hi(c + u + 1, 0, t + 2 * u)
                if u == 2:
                    act.wait_ge(p_full, 16)
                    for a in range(2):
                        x_hi(p_hi[:, a, :], p_raw[:, a, :], 1.0)
                for a in range(2):
                    take_copy(branch[:, 2 * u + a, :], t + 2 * u + a)

            def proj(u):
                hi(C[f"proj{u}"] + 1, 0, T[f"proj{u}"])
                for a in range(4):
                    take_copy(projected[:, 4 * u + a, :], T[f"proj{u}"] + a)

            def onto_residual(gname, n0):
                for k in range(KD):
                    act.wait_ge(res_done, n0 + k + 1)
                    x_hi(xb_hi[:, k, :], h[:, k, :], g(gname, k))

            proj(0)
            onto_residual("ffn_pre", 0)

            def gate_up(r, n):
                c, t = C[f"gu{r}"], T[f"gu{r}"]

                def pair(i):
                    for s in range(2):
                        hi(c + s + 1, 2 * i, t + 2 * s + 4 * i)
                        act.wait_ge(bank_free[(t + 2 * s) % 4], (t + 2 * s) // 4 + 1 + i)
                        act.activation(silu_t[:, s, :], gate_t[:, s, :], ACT.Silu).then_inc(silu_done, 1)
                        act.wait_ge(hid_sq, HID2 + 8 * r + 2 * i + s + 1)
                        act.activation(xa_hi[:, 2 * i + s, :], hid_t[:, s, :], ACT.Copy).then_inc(hid_hi, 1)

                pair(0)
                with act.Fori(1, n // 2) as i:
                    pair(i)

            def down(r):
                c, t = C[f"dn{r}"], T[f"dn{r}"]
                for u in range(4):
                    hi(c + u + 1, 0, t + 2 * u)
                    if r == 0:
                        for a in range(2):
                            take_copy(branch[:, 2 * u + a, :], t + 2 * u + a)

            for r, n in enumerate(GU_TILES):
                gate_up(r, n)
                down(r)
            proj(1)
            onto_residual("ple", KD)

            c, t = C["ple"], T["ple"]
            for u in range(4):
                if u < 3:
                    hi(c + u + 1, 0, t + 2 * u)
                for a in range(2):
                    bank_out(t + 2 * u + a)
                    act.activation(silu_t[:, a, :], gate_t[:, a, :], ACT.Sigmoid).then_inc(silu_done, 1)

        @block.vector
        def _(dve):
            def lo(c, slot):
                dve.wait_ge(whi_done, c + 1)
                dve.tensor_tensor(wlo[slot][:, :], raw[slot][:, :], whi[slot][:, :].bitcast(F32),
                                  ALU.subtract).then_inc(wlo_done, 1)

            def x_lo(dst, src, scale, dst_hi, n):
                dve.wait_ge(xh_done, n + 1)
                dve.scalar_tensor_tensor(out=dst, in0=src, scalar=scale, in1=dst_hi.bitcast(F32),
                                         op0=ALU.mult, op1=ALU.subtract).then_inc(xl_done, 1)

            def mean_square(n, dim):
                dve.wait_ge(stat_done, STATS[n] + 1)
                dve.tensor_scalar(ms_t[:, 4 * n:4 * n + 4], STAT[:, 0:QT], 1.0 / dim, EPS, ALU.mult, ALU.add).then_inc(ms_done, 1)

            def take_rstd(n, dst=None):
                dve.wait_ge(bc_done, n + 1)
                dve.tensor_copy((rstd_f if dst is None else dst)[:, :], BC[:, :]).then_inc(rstd_f_done, 1)
                dve.wait_ge(rstd_f_done, n + 1)

            def tile_ready(t, per=0, i=0):
                dve.wait_ge(tile_done, t + 1 + per * i)

            dve.memset(ones[:, :], 1.0)
            dve.memset(half_neg[:, :], -0.5).then_inc(dve_const, 1)
            dve.wait_ge(const_loaded, 16 * len(consts))
            for j in range(2):
                dve.tensor_tensor_reduce(out=sq_tmp[:, 64 * j:64 * j + 64], in0=lam_in[:, 2 * j, :],
                                         in1=lam_in[:, 2 * j + 1, :], scale=1.0, scalar=0.0, op0=ALU.mult,
                                         op1=ALU.add, accum_out=lam_ab[:, j:j + 1]).then_inc(lam_done, 1)
            lo(0, 0)
            for k in range(KD):
                x_lo(xa_lo[:, k, :], h[:, k, :], g("attn0", k), xa_hi[:, k, :], X["qkv"] + k)
            dve.wait_ge(lam_exp, 1)
            dve.scalar_tensor_tensor(out=neg_lam[:, :], in0=lam_ab[:, 3:4], scalar=-LAMBDA_INIT, in1=lam_ab[:, 2:3],
                                     op0=ALU.add, op1=ALU.subtract).then_inc(dve_const, 1)
            dve.tensor_tensor(g_x2[:, :], gains_all("final"), gains_all("mix_pre"), ALU.mult).then_inc(dve_const, 1)
            dve.memset(gain_sq[:, :, 0:1], 1.0)
            dve.tensor_tensor(gain_sq[:, :, 1:2], gains_all("final").unsqueeze(2), gains_all("final").unsqueeze(2), ALU.mult)
            dve.tensor_scalar(gsub[:, :], g("subln", 0), 1.0 - LAMBDA_INIT, None, ALU.mult).then_inc(dve_const, 1)

            def rope(t, dst1, dst2, cos_n, sin_n, rope_tmp, n_before, per=0, i=0):
                be, bo = ps[t % 4], ps[(t + 1) % 4]
                tile_ready(t + 1, per, i)
                if not (isinstance(n_before, int) and n_before < 1):
                    dve.wait_ge(rope_done, n_before)
                dve.tensor_tensor(dst1, be[:, :], cos_n[:, :], ALU.mult)
                dve.tensor_tensor(rope_tmp[:, 1, :], be[:, :], sin_n[:, :], ALU.mult).then_inc(bank_free[t % 4], 1)
                dve.tensor_tensor(rope_tmp[:, 0, :], bo[:, :], sin_n[:, :], ALU.mult)
                dve.tensor_tensor(dst2, bo[:, :], cos_n[:, :], ALU.mult).then_inc(bank_free[(t + 1) % 4], 1)

            c, t = C["qk"], T["qk"]
            lo(c + 1, (c + 1) % 2)
            dve.wait_ge(rows_stored, 16)
            mean_square(0, D)
            take_rstd(0)
            for dst, src, s in ((cq, cos_t, -DIFF_SCALE), (sq_, sin_t, -DIFF_SCALE), (ck, cos_t, 1.0), (sk, sin_t, 1.0)):
                dve.scalar_tensor_tensor(out=dst[:, :], in0=src[:, :], scalar=s, in1=rstd_f[:, :],
                                         op0=ALU.mult, op1=ALU.mult).then_inc(table_done, 1)
            dve.wait_ge(table_done, 4)
            rope(t, qk[:, 0, 0, 0, :], qk[:, 1, 0, 0, :], cq, sq_, rope_tmp, 0)
            lo(c + 2, c % 2)
            rope(t + 2, qk[:, 0, 1, 0, :], qk[:, 1, 1, 0, :], ck, sk, rope_tmp, 1)
            with dve.Fori(1, 4) as i:
                for s in range(2):
                    lo(c + s + 1 + 2 * i, (c + s + 1) % 2)
                    rope(t + 2 * s, qk[:, 0, s, i, :], qk[:, 1, s, i, :], (cq, ck)[s], (sq_, sk)[s],
                         rope_tmp, 2 * i + s, per=4, i=i)

            c = C["v"]
            with dve.Fori(0, 2) as i:
                for s in range(2):
                    lo(c + s + 1 + 2 * i, (c + s + 1) % 2)

            def diff_min(par, half):
                n = 2 * half + par
                for i in range(QT):
                    for comp in range(2):
                        j = 2 * i + comp
                        b = ps[(T["diff"] + 8 * par + j) % 4]
                        tile_ready(T["diff"] + 8 * par + j, 16, half)
                        dve.tensor_tensor(b[:, P * i:P * (i + 1)], b[:, P * i:P * (i + 1)], mask[:, :], ALU.add)\
                           .then_inc(mask_done, 1)
                        dve.wait_ge(mask_done, 8 * n + j + 1)
                        dve.tensor_reduce(negmin[:, par, j:j + 1], b[:, 0:P * (i + 1)], AX.X, ALU.min)\
                           .then_inc(nm_done, 1)

            def diff_coefs(par, half):
                n = 2 * half + par
                b = (T["diff"] + 8 * par + 7) % 4
                dve.wait_ge(bank_free[b], (T["diff"] + 8 * par + 7) // 4 + 1 + 4 * half)
                dve.reciprocal(rinv[:, par, :], rowsum[:, par, :]).then_inc(ri_done, 1)
                dve.wait_ge(ri_done, n + 1)
                dve.tensor_scalar(coef2[:, par, :], rinv[:, par, 1:8:2], neg_lam[:, 0:1], None, ALU.mult)\
                   .then_inc(rc_done, 1)

            def diff_combine(par, half):
                n = 2 * half + par
                for i in range(QT):
                    w = slice(OFF[i], OFF[i] + P * (i + 1))
                    dve.wait_ge(p2_done, 4 * n + i + 1)
                    dve.scalar_tensor_tensor(out=probs[par][:, 0, w], in0=probs[par][:, 0, w],
                                             scalar=rinv[:, par, 2 * i:2 * i + 1], in1=probs[par][:, 1, w],
                                             op0=ALU.mult, op1=ALU.add).then_inc(a_done, 1)

            def diff_mean_square(n):
                dve.wait_ge(sqo_done, n + 1)
                dve.tensor_reduce(o_ss[:, :], o_sq[:, :].rearrange("p (a b) -> p a b", a=QT), AX.X, ALU.add)\
                   .then_inc(oss_done, 1)
                dve.wait_ge(oss_done, n + 1)
                dve.tensor_scalar(o_ms[:, :], o_ss[:, :], 1.0 / P, SUBLN_EPS, ALU.mult, ALU.add).then_inc(oms_done, 1)

            def diff_normalise(par, n):
                dve.wait_ge(orstd_done, n + 1)
                dve.tensor_tensor(o_raw[par][:, :, :], o_raw[par][:, :, :],
                                  o_rstd[:, :].unsqueeze(2).to_broadcast([P, QT, P]), ALU.mult).then_inc(on_done, 1)

            def head_lo(dst, dst_hi, n, x0, scale):
                dve.wait_ge(xh_done, x0 + n + 1)
                dve.scalar_tensor_tensor(out=dst[:, n, :], in0=OT[:, :], scalar=scale,
                                         in1=dst_hi[:, n, :].bitcast(F32),
                                         op0=ALU.mult, op1=ALU.subtract).then_inc(xl_done, 1)

            def diff_step(par, half, ahead=True, behind=True, far=True):
                n = 2 * half + par
                if far:
                    head_lo(xb_lo, xb_hi, n - 2, X["diff_o"], gsub[:, 0:1])
                diff_coefs(par, half)
                if behind:
                    diff_mean_square(n - 1)
                diff_combine(par, half)
                if ahead:
                    diff_min(1 - par, half + par)
                if behind:
                    diff_normalise(1 - par, n - 1)

            dve.wait_ge(dve_const, 4)
            diff_min(0, 0)
            diff_step(0, 0, behind=False, far=False)
            diff_step(1, 0, far=False)
            with dve.Fori(1, HEADS // 2 - 1) as half:
                diff_step(0, half)
                diff_step(1, half)
            diff_step(0, HEADS // 2 - 1)
            diff_step(1, HEADS // 2 - 1, ahead=False)
            head_lo(xb_lo, xb_hi, HEADS - 2, X["diff_o"], gsub[:, 0:1])
            diff_mean_square(HEADS - 1)
            diff_normalise(1, HEADS - 1)
            head_lo(xb_lo, xb_hi, HEADS - 1, X["diff_o"], gsub[:, 0:1])

            def residual(stage, dst, dst_hi, gname, x0):
                c, t = C[stage], T[stage]
                for u in range(4):
                    lo(c + u + 1, (c + u + 1) % 2)
                    for a in range(2):
                        add_residual(2 * u + a, t + 2 * u + a)
                    for a in range(2):
                        k = 2 * u + a
                        x_lo(dst[:, k, :], h[:, k, :], gname(k), dst_hi[:, k, :], x0 + k)

            def add_residual(k, t, per=0, i=0):
                tile_ready(t, per, i)
                dve.tensor_tensor(h[:, k, :], ps[t % 4][:, :], h[:, k, :], ALU.add).then_inc(bank_free[t % 4], 1)

            def mlp(stage, norm, dst, dst_hi, gname, x0, hid0):
                c, t = C[stage], T[stage]

                def one_round(r, first, last):
                    for u in range(4):
                        lo(c + u + 1 + 8 * r, (c + u + 1) % 2)
                        if first and u == 0:
                            mean_square(norm, D)
                            take_rstd(norm)
                        for a in range(2):
                            tt = t + 2 * u + a
                            tile_ready(tt, 16, r)
                            if not (first and u == 0 and hid0 == 0):
                                dve.wait_ge(hid_lo, hid0 + 8 * r + 2 * u + a - 1)
                            dve.scalar_tensor_tensor(out=u_tmp[:, a, :], in0=ps[tt % 4][:, :], scalar=0.0,
                                                     in1=rstd_f[:, :], op0=ALU.max, op1=ALU.mult)\
                               .then_inc(bank_free[tt % 4], 1)
                    for d in range(4):
                        lo(c + d + 5 + 8 * r, (c + d + 5) % 2)
                        for a in range(2):
                            add_residual(2 * d + a, t + 8 + 2 * d + a, 16, r)
                        if last:
                            for a in range(2):
                                k = 2 * d + a
                                x_lo(dst[:, k, :], h[:, k, :], gname(k), dst_hi[:, k, :], x0 + k)

                one_round(0, True, False)
                with dve.Fori(1, ROUNDS - 1) as r:
                    one_round(r, False, False)
                one_round(ROUNDS - 1, False, True)

            residual("wo_a", xa_lo, xa_hi, gains_of("mlp0"), X["mlp0"])
            mlp("mlp0", 1, xa_lo, xa_hi, gains_of("kv_in"), X["dkv"], 0)
            c, t = C["dkv"], T["dkv"]

            def take_scaled(dst, tt, scale=None):
                tile_ready(tt)
                if scale is None:
                    ins = dve.tensor_tensor(dst, ps[tt % 4][:, :], rstd_f[:, :], ALU.mult)
                else:
                    ins = dve.scalar_tensor_tensor(out=dst, in0=ps[tt % 4][:, :], scalar=scale, in1=rstd_f[:, :],
                                                   op0=ALU.mult, op1=ALU.mult)
                ins.then_inc(bank_free[tt % 4], 1)

            def rope_tables(n_before, scale):
                for j, src in enumerate((cos_t, sin_t)):
                    dve.scalar_tensor_tensor(out=table2[:, j, :], in0=src[:, :], scalar=scale, in1=rstd_f[:, :],
                                             op0=ALU.mult, op1=ALU.mult).then_inc(table_done, 1)
                dve.wait_ge(table_done, n_before + 2)

            lo(c + 1, (c + 1) % 2)
            for k in range(KD):
                x_lo(xb_lo[:, k, :], h[:, k, :], g("attn1", k), xb_hi[:, k, :], X["dq"] + k)
            mean_square(2, D)
            take_rstd(2)
            for a in range(2):
                take_scaled(ckv[:, a, :], t + a)
            lo(c + 2, c % 2)
            for a in range(2):
                x_lo(ckv_lo[:, a, :], ckv[:, a, :], g("kv", a), ckv_hi[:, a, :], X["ckv"] + a)
            rope_tables(4, 1.0)
            rope(t + 2, k_eo[:, 0, :], k_eo[:, 1, :], table2[:, 0, :], table2[:, 1, :], rope_tmp2, 8)
            lo(c + 3, (c + 1) % 2)
            for a in range(2):
                take_scaled(cq_raw[:, a, :], t + 4 + a)
            lo(c + 4, c % 2)
            take_scaled(cq_raw[:, 2, :], t + 6)
            for a in range(3):
                x_lo(cq_lo[:, a, :], cq_raw[:, a, :], g("q", a), cq_hi[:, a, :], X["cq"] + a)
            c, t = C["ukv"], T["ukv"]
            mean_square(3, 256)
            lo(c + 1, (c + 1) % 2)
            take_rstd(3)
            for a in range(8):
                take_scaled(k_nope[:, a, :], t + a)
            mean_square(4, 384)
            lo(c + 2, c % 2)
            take_rstd(4)
            c, t = C["uq"], T["uq"]
            rope_tables(6, -MLA_SCALE)
            for u in range(2):
                lo(c + u + 1, (c + u + 1) % 2)
                for a in range(4):
                    take_scaled(q_nope[:, 4 * u + a, :], t + 4 * u + a, -MLA_SCALE)
            lo(c + 3, (c + 3) % 2)
            for j in range(2):
                rope(t + 8 + 2 * j, qr_eo[:, 2 * j, :], qr_eo[:, 2 * j + 1, :], table2[:, 0, :], table2[:, 1, :],
                     rope_tmp2, 9 + j)

            def mla_min(par, n):
                for i in range(QT):
                    b = ps[(T["mla"] + i) % 4]
                    tile_ready(T["mla"] + i, 4, n)
                    dve.tensor_tensor(b[:, P * i:P * (i + 1)], b[:, P * i:P * (i + 1)], mask[:, :], ALU.add)\
                       .then_inc(mask_done, 1)
                    dve.wait_ge(mask_done, NM_DIFF + 4 * n + i + 1)
                    dve.tensor_reduce(negmin[:, par, i:i + 1], b[:, 0:P * (i + 1)], AX.X, ALU.min)\
                       .then_inc(nm_done, 1)

            def mla_inverse(par, n):
                b = (T["mla"] + 3) % 4
                dve.wait_ge(bank_free[b], (T["mla"] + 3) // 4 + 1 + n)
                dve.reciprocal(rinv[:, par, 0:QT], rowsum[:, par, 0:QT]).then_inc(ri_done, 1)

            def mla_normalise(par, n):
                dve.wait_ge(o_done, HEADS + n + 1)
                dve.wait_ge(ri_done, HEADS + n + 1)
                dve.tensor_tensor(mla_o[par][:, :, :], O_PS[:, :].rearrange("p (a b) -> p a b", a=QT),
                                  rinv[:, par, 0:QT].unsqueeze(2).to_broadcast([P, QT, P]), ALU.mult)\
                   .then_inc(on_done, 1)

            def mla_step(par, n, ahead=True, behind=True, far=True):
                if far:
                    head_lo(xa_lo, xa_hi, n - 2, X["mla_o"], 1.0)
                if behind:
                    mla_normalise(1 - par, n - 1)
                if ahead:
                    mla_min(1 - par, n + 1)
                mla_inverse(par, n)

            mla_min(0, 0)
            mla_step(0, 0, behind=False, far=False)
            mla_step(1, 1, far=False)
            with dve.Fori(1, HEADS // 2 - 1) as i:
                mla_step(0, 2 * i)
                mla_step(1, 2 * i + 1)
            mla_step(0, HEADS - 2)
            mla_step(1, HEADS - 1, ahead=False)
            head_lo(xa_lo, xa_hi, HEADS - 2, X["mla_o"], 1.0)
            mla_normalise(1, HEADS - 1)
            head_lo(xa_lo, xa_hi, HEADS - 1, X["mla_o"], 1.0)

            residual("wo_b", xb_lo, xb_hi, gains_of("mlp1"), X["mlp1"])
            mlp("mlp1", 5, xb_lo, xb_hi, lambda k: g_x2[:, k:k + 1], X["w_in"], 8 * ROUNDS)
            c, t = C["w_in"], T["w_in"]
            lo(c + 1, (c + 1) % 2)
            pairs = STAT[:, 0:2 * QT].rearrange("p (q b) -> p q b", b=2)
            dve.wait_ge(stat_done, STATS[6] + 1)
            dve.tensor_scalar(ms_t[:, 24:28], pairs[:, :, 0], 1.0 / D, EPS, ALU.mult, ALU.add).then_inc(ms_done, 1)
            dve.wait_ge(rstd_t_done, 7)
            dve.tensor_tensor(r1_sq[:, :], rstd_t[:, 24:28], rstd_t[:, 24:28], ALU.mult).then_inc(small_done, 1)
            dve.wait_ge(small_done, 1)
            dve.scalar_tensor_tensor(out=r1_ms[:, :], in0=pairs[:, :, 1], scalar=1.0 / D, in1=r1_sq[:, :],
                                     op0=ALU.mult, op1=ALU.mult).then_inc(small_done, 1)
            dve.wait_ge(small_done, 2)
            dve.tensor_scalar(ms_t[:, 28:32], r1_ms[:, :], EPS, None, ALU.add).then_inc(ms_done, 1)
            dve.wait_ge(rstd_t_done, 8)
            dve.tensor_tensor(r12[:, :], rstd_t[:, 24:28], rstd_t[:, 28:32], ALU.mult).then_inc(r12_done, 1)
            take_rstd(6)
            for a in range(2):
                take_scaled(iq[:, a, :], t + a)
            lo(c + 2, c % 2)
            take_rstd(7, r1_f)
            for a in range(2):
                take_scaled(iq[:, 2 + a, :], t + 2 + a)
            lo(c + 3, (c + 1) % 2)
            take_scaled(ik[:, :], t + 4)
            tile_ready(t + 5)
            for q in range(QT):
                ins = dve.tensor_scalar(iw[:, q, :], ps[(t + 5) % 4][:, IDX_HEADS * q:IDX_HEADS * (q + 1)],
                                        r12[:, q:q + 1], IDX_SCALE, ALU.mult, ALU.mult)
            ins.then_inc(bank_free[(t + 5) % 4], 1)
            lo(c + 4, c % 2)
            for a in range(2):
                take_scaled(cq2[:, a, :], t + 6 + a, -HEAD_SCALE)
            dve.wait_ge(bank_free[(t + 5) % 4], (t + 5) // 4 + 1)
            t = T["idx"]
            for i in range(1, QT):
                row = idx_score[:, IDX_OFF[i]:IDX_OFF[i] + P * (i + 1)]
                for hd in range(IDX_HEADS):
                    j = IDX_HEADS * (i - 1) + hd
                    src = idx_relu[:, j % 2, 0:P * (i + 1)]
                    dve.wait_ge(bank_free[(t + j) % 4], (t + j) // 4 + 1)
                    if hd == 0:
                        dve.tensor_scalar(row, src, iw[:, i, 0:1], None, ALU.mult).then_inc(idx_acc, 1)
                    else:
                        dve.wait_ge(idx_acc, j)
                        dve.scalar_tensor_tensor(out=row, in0=src, scalar=iw[:, i, hd:hd + 1], in1=row,
                                                 op0=ALU.mult, op1=ALU.add).then_inc(idx_acc, 1)
                diag = idx_score[:, IDX_OFF[i] + P * i:IDX_OFF[i] + P * (i + 1)]
                dve.wait_ge(idx_acc, IDX_HEADS * i)
                dve.tensor_tensor(diag, diag, mask[:, :], ALU.subtract).then_inc(top_done, 1)

            def top_rounds(first, last):
                for n in range(first, last):
                    i, rnd = 1 + n // ROUNDS_TOP, n % ROUNDS_TOP
                    row = idx_score[:, IDX_OFF[i]:IDX_OFF[i] + P * (i + 1)]
                    dve.wait_ge(top_done, QT - 1 + 2 * n)
                    dve.max(top8[:, :], row).then_inc(top_done, 1)
                    dve.wait_ge(top_done, QT - 1 + 2 * n + 1)
                    dve.match_replace(row, top8[:, :], row, TAKEN).then_inc(top_done, 1)
                    if rnd == ROUNDS_TOP - 1:
                        dve.wait_ge(top_done, QT - 1 + 2 * n + 2)
                        dve.tensor_scalar(row, row, TAKEN / 2, BIG, ALU.is_gt, ALU.mult).then_inc(sel_done, 1)

            c, t = C["w_in2"], T["w_in2"]
            n_rounds = ROUNDS_TOP * (QT - 1)
            for u in range(9):
                lo(c + u + 1, (c + u + 1) % 2)
                top_rounds(n_rounds * u // 9, n_rounds * (u + 1) // 9)
                if u in (1, 4):
                    continue
                for a in range(2):
                    tt = t + 2 * u + a
                    if u == 0:
                        take_scaled(ck2[:, a, :], tt)
                    elif u == 2:
                        take_scaled(dq2[:, a, :], tt, -HEAD_SCALE)
                    elif u == 3:
                        take_scaled(dk2[:, a, :], tt)
                    elif u == 5:
                        take_scaled(conv_in[:, a, :], tt)
                    elif u == 6:
                        take_scaled(conv_gate[:, a, :], tt)
                    elif u == 7:
                        take_scaled(conv_gate2[:, a, :], tt)
                    else:
                        take_scaled(pool_v[:, a, PAD:PAD + S], tt)
                if u == 6:
                    dve.memset(pool_v[:, :, 0:PAD], 0.0).then_inc(pool_zero, 1)
                if u == 7:
                    for a in range(2):
                        x, y = conv_in[:, a, :], conv_y[:, a, :]
                        dve.wait_ge(conv_x, a + 1)
                        dve.tensor_scalar(y, x, g("conv", 4 + a), None, ALU.mult).then_inc(conv_step, 1)
                        for tap in (1, 2):
                            dve.wait_ge(conv_step, 3 * a + tap)
                            dve.scalar_tensor_tensor(out=y[:, tap:S], in0=x[:, 0:S - tap],
                                                     scalar=g("conv", 2 * (2 - tap) + a), in1=y[:, tap:S],
                                                     op0=ALU.mult, op1=ALU.add).then_inc(conv_step, 1)

            def mix_lo(n, src, scale):
                x_lo(xa_lo[:, n, :], src, scale, xa_hi[:, n, :], X["mix"] + n)

            for a in range(2):
                mix_lo(a, conv_y[:, a, :], 1.0)
            for j, (a, rows, src, w) in enumerate(POOL_GROUPS):
                s_ = pool_s[src]
                dve.wait_ge(pool_s_done, POOL_STEPS[j])
                dve.tensor_tensor(s_[rows, PAD:2 * PAD], s_[rows, PAD:2 * PAD], pool_fix[rows, a, :], ALU.mult)\
                    .then_inc(pool_fix_done, 1)
                dve.wait_ge(pool_fix_done, j + 1)
                dve.scalar_tensor_tensor(out=pool_d[rows, a, :], in0=s_[rows, PAD:PAD + S], scalar=1.0 / w,
                                         in1=pool_v[rows, a, PAD:PAD + S], op0=ALU.mult, op1=ALU.subtract)\
                    .then_inc(pool_d_done, 1)

            dve.wait_ge(nbias_full, 16)
            dve.tensor_tensor(nbias[:, :, P:2 * P], nbias[:, :, P:2 * P],
                              mask[:, :].unsqueeze(1).to_broadcast([P, HEADS, P]), ALU.add).then_inc(nb_masked, 1)
            dve.wait_ge(nb_masked, 1)

            def min2(jb):
                head = NB_HEAD[jb]
                for i in range(QT):
                    tt, j = T_JOB[jb] + i, 4 * jb + i
                    b, w0 = ps[tt % 4], P * max(i - 1, 0)
                    tile_ready(tt)
                    ins = dve.tensor_tensor(b[:, w0:P * (i + 1)], b[:, w0:P * (i + 1)],
                                            nbias[:, head, 2 * P - (P * (i + 1) - w0):2 * P], ALU.add)
                    ins.then_inc(mask_done, 1)
                    dve.wait_ge(mask_done, MASK2[jb] + (1 if jb < 4 or i == 0 else 2) * i + (1 if jb < 4 or i == 0 else 0))
                    if jb >= 4 and i >= 1:
                        dve.wait_ge(sel_done, i)
                        dve.tensor_tensor(b[:, 0:P * (i + 1)], b[:, 0:P * (i + 1)],
                                          idx_score[:, IDX_OFF[i]:IDX_OFF[i] + P * (i + 1)], ALU.add)\
                           .then_inc(mask_done, 1)
                        dve.wait_ge(mask_done, MASK2[jb] + 2 * i + 1)
                    dve.tensor_reduce(negmin[:, jb % 2, i:i + 1], b[:, 0:P * (i + 1)], AX.X, ALU.min)\
                       .then_inc(nm_done, 1)

            def inverse2(jb):
                tt = T_JOB[jb] + 3
                dve.wait_ge(bank_free[tt % 4], tt // 4 + 1)
                dve.reciprocal(rinv[:, jb % 2, 0:QT], rowsum[:, jb % 2, 0:QT]).then_inc(ri_done, 1)

            def normalise2(jb):
                dve.wait_ge(o_done, 2 * HEADS + jb + 1)
                dve.wait_ge(ri_done, 2 * HEADS + jb + 1)
                pair = jb // 2
                if jb % 2 == 0 and pair >= 2:
                    dve.wait_ge(ot_done, 2 * HEADS + pair - 1)
                dve.tensor_tensor(o2[pair % 2][:, :, 64 * (jb % 2):64 * (jb % 2) + 64],
                                  O_PS[:, 0:256].rearrange("p (a b) -> p a b", a=QT),
                                  rinv[:, jb % 2, 0:QT].unsqueeze(2).to_broadcast([P, QT, 64]), ALU.mult)\
                   .then_inc(on_done, 1)

            min2(0)
            for jb in range(8):
                if jb >= 3 and jb % 2 == 1:
                    mix_lo(4 + (jb - 3) // 2, OT[:, :], 1.0)
                if jb >= 1:
                    normalise2(jb - 1)
                if jb == 2:
                    for a in range(2):
                        tt = T["pool"] + a
                        dve.wait_ge(xh_done, X["mix"] + 2 + a + 1)
                        dve.scalar_tensor_tensor(out=xa_lo[:, 2 + a, :], in0=ps[tt % 4][:, :], scalar=g("pool_scale", a),
                                                 in1=xa_hi[:, 2 + a, :].bitcast(F32), op0=ALU.mult, op1=ALU.subtract)\
                            .then_inc(xl_done, 1)
                        dve.wait_ge(xl_done, X["mix"] + 2 + a + 1)
                        dve.sem_inc(bank_free[tt % 4], 1)
                if jb < 7:
                    min2(jb + 1)
                inverse2(jb)
            normalise2(7)
            mix_lo(7, OT[:, :], 1.0)
            for k in range(KD):
                ins = dve.scalar_tensor_tensor(out=h[:, k, :], in0=h[:, k, :], scalar=g("final", k), in1=r1_f[:, :],
                                               op0=ALU.mult, op1=ALU.mult)
            ins.then_inc(x2_done, 1)

            c, t = C["w_out"], T["w_out"]
            for u in range(4):
                lo(c + u + 1, (c + u + 1) % 2)
            for a in range(2):
                x_lo(p_lo[:, a, :], p_raw[:, a, :], 1.0, p_hi[:, a, :], X["p"] + a)

            def onto_residual(n, gname, gnext, x0, n0):
                mean_square(n, D)
                take_rstd(n)
                for k in range(KD):
                    if n0 + k >= 2:
                        dve.wait_ge(res_done, n0 + k - 1)
                    dve.scalar_tensor_tensor(out=branch_t[:, k % 2, :], in0=branch[:, k, :], scalar=g(gname, k),
                                             in1=rstd_f[:, :], op0=ALU.mult, op1=ALU.mult).then_inc(branch_done, 1)
                    if k >= 1:
                        x_lo(xb_lo[:, k - 1, :], h[:, k - 1, :], g(gnext, k - 1), xb_hi[:, k - 1, :], x0 + k - 1)
                x_lo(xb_lo[:, KD - 1, :], h[:, KD - 1, :], g(gnext, KD - 1), xb_hi[:, KD - 1, :], x0 + KD - 1)

            lo(C["proj0"] + 1, (C["proj0"] + 1) % 2)
            dve.wait_ge(x2_done, 1)
            onto_residual(8, "mix_post", "ffn_pre", X["ffn"], 0)

            def gate_up(r, n, first):
                c, t = C[f"gu{r}"], T[f"gu{r}"]

                def pair(i):
                    for s in range(2):
                        j = HID2 + 8 * r + 2 * i + s
                        lo(c + s + 1 + 2 * i, (c + s + 1) % 2)
                        if first and isinstance(i, int) and s == 0:
                            mean_square(9, D)
                            take_rstd(9)
                        tt = t + 2 * s
                        tile_ready(tt, 4, i)
                        if not (first and isinstance(i, int)):
                            dve.wait_ge(hid_sq, j - 1)
                        dve.tensor_tensor(gate_t[:, s, :], ps[tt % 4][:, :], rstd_f[:, :], ALU.mult)\
                            .then_inc(bank_free[tt % 4], 1)
                        tile_ready(tt + 1, 4, i)
                        dve.tensor_tensor(up_t[:, s, :], ps[(tt + 1) % 4][:, :], rstd_f[:, :], ALU.mult)\
                            .then_inc(bank_free[(tt + 1) % 4], 1)

                pair(0)
                with dve.Fori(1, n // 2) as i:
                    pair(i)

            def down(r):
                c, t = C[f"dn{r}"], T[f"dn{r}"]
                for u in range(4):
                    lo(c + u + 1, (c + u + 1) % 2)
                    for a in range(2):
                        k, tt = 2 * u + a, t + 2 * u + a
                        if r == 0:
                            continue
                        tile_ready(tt)
                        if r == 1:
                            b0 = T["dn0"] + k
                            dve.wait_ge(bank_free[b0 % 4], b0 // 4 + 1)
                        dve.tensor_tensor(branch[:, k, :], ps[tt % 4][:, :], branch[:, k, :], ALU.add)\
                            .then_inc(bank_free[tt % 4], 1)

            for r, n in enumerate(GU_TILES):
                gate_up(r, n, r == 0)
                down(r)
            lo(C["proj1"] + 1, (C["proj1"] + 1) % 2)
            onto_residual(10, "ffn_post", "ple", X["ple"], KD)

            c, t = C["ple"], T["ple"]
            for u in range(4):
                if u < 3:
                    lo(c + u + 1, (c + u + 1) % 2)
                if u == 0:
                    mean_square(11, D)
                    take_rstd(11)
                for a in range(2):
                    k, tt = 2 * u + a, t + 2 * u + a
                    tile_ready(tt)
                    if u:
                        dve.wait_ge(silu_done, N_SILU + k - 1)
                    dve.tensor_tensor(gate_t[:, a, :], ps[tt % 4][:, :], rstd_f[:, :], ALU.mult)\
                        .then_inc(bank_free[tt % 4], 1)
                for a in range(2):
                    k = 2 * u + a
                    dve.wait_ge(gated_done, k + 1)
                    dve.tensor_tensor(h[:, k, :], h[:, k, :], projected[:, k, :], ALU.add).then_inc(y_done, 1)

        @block.gpsimd
        def _(pool):
            def square_tile(src, k, n):
                if k == 0:
                    pool.tensor_tensor(ssq[:, :], src, src, ALU.mult).then_inc(sq_done, 1)
                else:
                    if k >= 2:
                        pool.wait_ge(ssq_done, SSQ[n] + k - 1)
                    pool.tensor_tensor(sq_tmp[:, :], src, src, ALU.mult).then_inc(sq_done, 1)
                    pool.wait_ge(sq_done, SQ[n] + k + 1)
                    pool.tensor_tensor(ssq[:, :], ssq[:, :], sq_tmp[:, :], ALU.add).then_inc(ssq_done, 1)

            def rstd(n):
                pool.wait_ge(ms_done, n + 1)
                pool.tensor_tensor(rstd_t[:, 4 * n:4 * n + 4], ms_t[:, 4 * n:4 * n + 4], half_neg[:, :], ALU.pow).then_inc(rstd_t_done, 1)

            pool.wait_ge(dve_const, 1)
            for k in range(KD):
                pool.wait_ge(x_loaded[k // 2], 16)
                if k == 1:
                    pool.wait_ge(lam_done, 2)
                square_tile(h[:, k, :], k, 0)
            rstd(0)

            def rope(t, dst1, dst2, rope_tmp, per=0, i=0):
                b = (t + 1) % 4
                pool.wait_ge(bank_free[b], (t + 1) // 4 + 1 + (per // 4) * i)
                pool.tensor_tensor(dst1, dst1, rope_tmp[:, 0, :], ALU.subtract)
                pool.tensor_tensor(dst2, dst2, rope_tmp[:, 1, :], ALU.add).then_inc(rope_done, 1)

            with pool.Fori(0, 4) as i:
                for s in range(2):
                    rope(T["qk"] + 2 * s, qk[:, 0, s, i, :], qk[:, 1, s, i, :], rope_tmp, 4, i)

            def diff_scale(par, half):
                for i in range(QT):
                    w = slice(OFF[i], OFF[i] + P * (i + 1))
                    pool.tensor_scalar(probs[par][:, 1, w], probs[par][:, 1, w], coef2[:, par, i:i + 1], 1.0,
                                       ALU.mult, ALU.mult).then_inc(p2_done, 1)

            def diff_square(par, n):
                pool.wait_ge(oc_done, n + 1)
                o = o_raw[par][:, :, :].rearrange("p a b -> p (a b)")
                pool.tensor_tensor(o_sq[:, :], o, o, ALU.mult).then_inc(sqo_done, 1)

            def diff_rstd(n):
                pool.wait_ge(oms_done, n + 1)
                pool.tensor_tensor(o_rstd[:, :], o_ms[:, :], half_neg[:, :], ALU.pow).then_inc(orstd_done, 1)

            def diff_step(par, half, behind=True):
                n = 2 * half + par
                pool.wait_ge(rc_done, n + 1)
                if behind:
                    diff_square(1 - par, n - 1)
                diff_scale(par, half)
                if behind:
                    diff_rstd(n - 1)

            diff_step(0, 0, behind=False)
            with pool.Fori(0, HEADS // 2 - 1) as i:
                diff_step(1, i)
                diff_step(0, i + 1)
            diff_step(1, HEADS // 2 - 1)
            diff_square(1, HEADS - 1)
            diff_rstd(HEADS - 1)

            def norm_tiles(t, n):
                for k in range(KD):
                    pool.wait_ge(bank_free[(t + k) % 4], (t + k) // 4 + 1)
                    square_tile(h[:, k, :], k, n)
                rstd(n)

            def hidden(t, hhi, hlo, hid0, r):
                for j in range(KD):
                    a = j % 2
                    tt = t + j
                    pool.wait_ge(bank_free[tt % 4], tt // 4 + 1 + 4 * r)
                    pool.tensor_tensor(u_sq[:, a, :], u_tmp[:, a, :], u_tmp[:, a, :], ALU.mult).then_inc(hid_sq, 1)
                    pool.wait_ge(hid_sq, hid0 + 8 * r + j + 1)
                    pool.wait_ge(hid_hi, hid0 + 8 * r + j + 1)
                    pool.tensor_tensor(hlo[:, j, :], u_sq[:, a, :], hhi[:, j, :].bitcast(F32), ALU.subtract)\
                        .then_inc(hid_lo, 1)

            norm_tiles(T["wo_a"], 1)
            with pool.Fori(0, ROUNDS) as r:
                hidden(T["mlp0"], xb_hi, xb_lo, 0, r)
            norm_tiles(T["mlp0"] + 56, 2)
            t = T["dkv"]
            for a in range(2):
                pool.wait_ge(bank_free[(t + a) % 4], (t + a) // 4 + 1)
                square_tile(ckv[:, a, :], a, 3)
            rope(t + 2, k_eo[:, 0, :], k_eo[:, 1, :], rope_tmp2)
            rstd(3)
            for a in range(3):
                pool.wait_ge(bank_free[(t + 4 + a) % 4], (t + 4 + a) // 4 + 1)
                square_tile(cq_raw[:, a, :], a, 4)
            rstd(4)
            for j in range(2):
                rope(T["uq"] + 8 + 2 * j, qr_eo[:, 2 * j, :], qr_eo[:, 2 * j + 1, :], rope_tmp2)
            norm_tiles(T["wo_b"], 5)
            with pool.Fori(0, ROUNDS) as r:
                hidden(T["mlp1"], xa_hi, xa_lo, 8 * ROUNDS, r)
            t = T["mlp1"] + 56
            for k in range(KD):
                pool.wait_ge(bank_free[(t + k) % 4], (t + k) // 4 + 1)
                pool.tensor_tensor(squares[:, k, :], h[:, k, :], h[:, k, :], ALU.mult).then_inc(sq_done, 1)
            rstd(6)
            rstd(7)

            t = T["w_in2"]
            for a in range(2):
                tt = t + 12 + a
                pool.wait_ge(bank_free[tt % 4], tt // 4 + 1)
                pool.tensor_tensor(conv_in[:, a, :], conv_in[:, a, :], conv_gate[:, a, :], ALU.mult).then_inc(conv_x, 1)
            for a in range(2):
                tt = t + 14 + a
                pool.wait_ge(bank_free[tt % 4], tt // 4 + 1)
                pool.wait_ge(conv_step, 3 * (a + 1))
                pool.tensor_tensor(conv_y[:, a, :], conv_y[:, a, :], conv_gate2[:, a, :], ALU.mult).then_inc(conv_out, 1)

            def window(dst, src, shift, low):
                pool.tensor_tensor(dst[:, low:PAD + S], src[:, low:PAD + S], src[:, low - shift:PAD + S - shift],
                                   ALU.add).then_inc(pool_s_done, 1)

            pool.wait_ge(pool_zero, 1)
            steps = 0
            for a, windows in ((0, ((0, 1, 1), (1, 2, 3))), (1, ((2, 1, 1), (3, 2, 3), (2, 4, 7), (3, 8, 15)))):
                tt = t + 16 + a
                pool.wait_ge(bank_free[tt % 4], tt // 4 + 1)
                src = pool_v[:, a, :]
                for dst, shift, low in windows:
                    if steps:
                        pool.wait_ge(pool_s_done, steps)
                    window(pool_s[dst], src, shift, low)
                    src = pool_s[dst]
                    steps += 1

            def branch_tiles(t, n):
                for k in range(KD):
                    tt = t + k
                    pool.wait_ge(bank_free[tt % 4], tt // 4 + 1)
                    square_tile(branch[:, k, :], k, n)
                rstd(n)

            def onto_residual(n0, n):
                for k in range(KD):
                    pool.wait_ge(branch_done, n0 + k + 1)
                    pool.tensor_tensor(h[:, k, :], h[:, k, :], branch_t[:, k % 2, :], ALU.add).then_inc(res_done, 1)
                    pool.wait_ge(res_done, n0 + k + 1)
                    square_tile(h[:, k, :], k, n)
                rstd(n)

            branch_tiles(T["w_out"], 8)
            onto_residual(0, 9)

            def gate_up(r, n):
                t = T[f"gu{r}"]

                def pair(i):
                    for s in range(2):
                        j = HID2 + 8 * r + 2 * i + s
                        tt = t + 2 * s + 1
                        pool.wait_ge(bank_free[tt % 4], tt // 4 + 1 + i)
                        pool.wait_ge(silu_done, j - HID2 + 1)
                        pool.wait_ge(hid_lo, j - 1)
                        pool.tensor_tensor(hid_t[:, s, :], silu_t[:, s, :], up_t[:, s, :], ALU.mult).then_inc(hid_sq, 1)
                        pool.wait_ge(hid_sq, j + 1)
                        pool.wait_ge(hid_hi, j + 1)
                        pool.tensor_tensor(xa_lo[:, 2 * i + s, :], hid_t[:, s, :],
                                           xa_hi[:, 2 * i + s, :].bitcast(F32), ALU.subtract).then_inc(hid_lo, 1)

                with pool.Fori(0, n // 2) as i:
                    pair(i)

            for r, n in enumerate(GU_TILES):
                gate_up(r, n)
            branch_tiles(T["dn2"], 10)
            onto_residual(KD, 11)

            t = T["ple"]
            for k in range(KD):
                pool.wait_ge(silu_done, N_SILU + k + 1)
                pool.tensor_tensor(projected[:, k, :], projected[:, k, :], silu_t[:, k % 2, :], ALU.mult)\
                    .then_inc(gated_done, 1)


def pack_weights(inp):
    chunks = []

    def put(w, cols, k_tiles=KD):
        a = w[:, cols].reshape(k_tiles, P, len(cols)).transpose(1, 0, 2).reshape(P, -1)
        full = np.zeros((P, CHUNK), a.dtype)
        full[:, :a.shape[1]] = a
        chunks.append(full)

    def put_all(w, width=256):
        for n in range(0, w.shape[1], width):
            put(w, np.arange(n, n + width), w.shape[0] // P)

    def put_mlp(up, down):
        for r in range(ROUNDS):
            put_all(up[:, r * D:(r + 1) * D])
            put_all(down[r * D:(r + 1) * D])

    w = inp["w_qkv_a"][0]
    for j in range(4):
        for part in range(2):
            cols = [part * D + 64 * (4 * j + comp) + 32 * half + r
                    for half in range(2) for comp in range(4) for r in range(32)]
            put(w, np.array(cols))
    put_all(w[:, 2 * D:])
    put_all(inp["w_o_a"][0])
    put_mlp(inp["w_up"][0], inp["w_down"][0])
    dkv, ukv, dq, uq = inp["w_dkv"], inp["w_ukv"], inp["w_dq"][0], inp["w_uq"][0]
    put(dkv, np.arange(256))
    put(dkv, np.concatenate([np.tile(np.arange(256 + 32 * half, 288 + 32 * half), 4) for half in range(2)]))
    put(dq, np.arange(256))
    put(dq, np.concatenate([np.arange(256, 384)] * 2))
    heads = np.arange(HEADS)[:, None]
    for part in range(2):
        put(ukv, (256 * heads + 128 * part + np.arange(128)).ravel(), 2)
    for part in range(2):
        put(uq, (192 * heads[4 * part:4 * part + 4] + np.arange(128)).ravel(), 3)
    put(uq, np.concatenate([(192 * heads[4 * j:4 * j + 4] + 128 + 32 * half + np.arange(32)).ravel()
                            for j in range(2) for half in range(2)]), 3)
    put_all(inp["w_o_b"][0])
    put_mlp(inp["w_up"][1], inp["w_down"][1])
    w = inp["w_in_2"][0]
    at = dict(a_in=0, a_c=256, a_b=512, pv=768, cq=1024, ck=1280, cv=1536, iq=1792, ik=2304, iw=2368, dq=2376, dk=2632, dv=2888)
    put_all(w[:, at["iq"]:at["iq"] + 512])
    put(np.concatenate([w, np.zeros((D, 1), w.dtype)], 1),
        np.concatenate([np.tile(at["ik"] + np.arange(64), 2), at["iw"] + np.arange(IDX_HEADS),
                        np.full(P - IDX_HEADS, w.shape[1])]))
    for name in ("cq", "ck", "cv", "dq", "dk", "dv", "a_in", "a_c", "a_b", "pv"):
        put(w, at[name] + np.arange(256))
    wo = inp["w_out_2"][0]
    put_all(np.concatenate([wo[0:512], wo[768:1024], wo[512:768]]))
    proj, gate_up, down = inp["w_ple_proj_2"][0], inp["w_gate_up_2"][0], inp["w_down_2"][0]
    put(proj, np.arange(512), 2)
    tile0 = 0
    for n in GU_TILES:
        for j in range(tile0, tile0 + n):
            put(gate_up, np.concatenate([j * P + np.arange(P), down.shape[0] + j * P + np.arange(P)]))
        put_all(down[tile0 * P:(tile0 + n) * P])
        tile0 += n
    put(proj, 512 + np.arange(512), 2)
    put_all(inp["w_ple_gate_2"][0])
    assert len(chunks) == N_CHUNKS
    return np.stack(chunks)


def pack_gains(inp):
    vectors = [inp["attn_norm_g"][0], inp["attn_norm_g"][1], inp["kv_in_norm_g"], inp["mlp_norm_g"][0],
               inp["mlp_norm_g"][1], inp["final_norm_g"], inp["g_mix_pre_2"][0], inp["g_mix_post_2"][0],
               inp["g_ffn_pre_2"][0], inp["g_ffn_post_2"][0], inp["g_ple_2"][0], inp["kv_norm_g"],
               inp["q_norm_g"][0], inp["subln_g"][0], inp["pool_scale_2"][0], inp["conv_w_2"][0].reshape(-1)]
    return np.ascontiguousarray(np.concatenate([v.reshape(-1, P) for v in vectors]).T)


def rope_tables():
    inv_freq = np.float32(10000.0) ** (-np.arange(0, 64, 2, dtype=np.float32) / np.float32(64))
    ang = inv_freq[:, None] * np.arange(S, dtype=np.float32)[None, :]
    return np.tile(np.cos(ang), (4, 1)).astype(np.float32), np.tile(np.sin(ang), (4, 1)).astype(np.float32)


def distance_buckets():
    dist = np.maximum(2 * P - 1 - np.arange(ROWS), 0)
    exact = BUCKETS // 2
    large = exact + (np.log(np.maximum(dist, 1).astype(np.float32) / np.float32(exact))
                     / np.float32(np.log(MAX_DIST / exact)) * np.float32(BUCKETS - exact)).astype(np.int32)
    bucket = np.where(dist < exact, dist, np.minimum(large, BUCKETS - 1))
    eye = np.eye(BUCKETS, dtype=np.float32)
    out = eye[:, BUCKETS - 1:] - eye[:, bucket]
    out[:, 2 * P:] = 0.0
    return np.ascontiguousarray(out)


def pool_counts():
    out = np.ones((P, 2, PAD), np.float32)
    for a, rows, _, w in POOL_GROUPS:
        out[rows, a, :] = w / np.minimum(np.arange(PAD) + 1, w)
    return out.reshape(P, -1)


def pool_blocks(w):
    out = np.zeros((P, 2, P), w.dtype)
    for j in range(4):
        rows = slice(64 * (j % 2), 64 * (j % 2) + 64)
        out[rows, j // 2, rows] = w[j]
    return out.reshape(P, -1)


def lay_out(inp):
    cos, sin = rope_tables()
    return {
        "pT_in": np.ascontiguousarray(inp["p_2"][0, 0].T), "tab_in": np.ascontiguousarray(inp["rel_bias_2"].T),
        "buckets_in": distance_buckets(), "pool_w_in": pool_blocks(inp["pool_w_2"][0]), "pool_fix_in": pool_counts(),
        "wst": pack_weights(inp), "xT": np.ascontiguousarray(inp["x"][0].T), "gains": pack_gains(inp),
        "cos": cos, "sin": sin, "ident_in": np.eye(P, dtype=np.float32),
        "mask_in": np.triu(np.full((P, P), BIG, np.float32), 1),
        "lam": np.concatenate([inp["lambda_q1"], inp["lambda_k1"], inp["lambda_q2"], inp["lambda_k2"]], 1),
    }


def kernel(**inputs):
    from concourse import bacc
    from concourse.bass_utils import run_bass_kernel_spmd

    nc = bacc.Bacc("TRN2", target_bir_lowering=False, num_devices=1)
    arrays = lay_out({name: np.asarray(a) for name, a in inputs.items()})
    args = {name: nc.dram_tensor(name, a.shape, mybir.dt.from_np(a.dtype), kind="ExternalInput").ap()
            for name, a in arrays.items()}
    out = nc.dram_tensor("outT", (D, S), F32, kind="ExternalOutput").ap()
    build(nc, outT=out, **args)
    result = run_bass_kernel_spmd(nc, [arrays], core_ids=[0])
    return np.ascontiguousarray(result.results[0]["outT"].T)[None]
```

```python
from contextlib import ExitStack

import numpy as np

import concourse.bass as bass
from concourse import mybir

F32 = mybir.dt.float32
F32R = mybir.dt.float32r
BF16 = mybir.dt.bfloat16
ALU = mybir.AluOpType
ACT = mybir.ActivationFunctionType
AX = mybir.AxisListType

P = 128
S = 512
QT = S // P
D = 1024
KD = D // P
CHUNK = 2048
HEADS = 8
FF = 4096
ROUNDS = FF // D
EPS = 1e-6
SUBLN_EPS = 1e-5
LAMBDA_INIT = 0.8 - 0.6
DIFF_SCALE = 64 ** -0.5
MLA_SCALE = (128 + 64) ** -0.5
BIG = 1e30

GAINS = {}


def _gain_columns():
    at = 0
    for name, n in (("attn0", 8), ("attn1", 8), ("kv_in", 8), ("mlp0", 8), ("mlp1", 8), ("final", 8),
                    ("mix_pre", 8), ("mix_post", 8), ("ffn_pre", 8), ("ffn_post", 8), ("ple", 8),
                    ("kv", 2), ("q", 3), ("subln", 1), ("pool_scale", 2), ("conv", 6)):
        GAINS[name] = (at, n)
        at += n
    return at


N_GAINS = _gain_columns()

STAGES = (
    ("qk", 8, 16), ("v", 4, 8), ("diff", 0, 64), ("wo_a", 4, 8), ("mlp0", 32, 64),
          ("dkv", 4, 7), ("ukv", 2, 16), ("uq", 3, 12), ("mla", 0, 32), ("wo_b", 4, 8), ("mlp1", 32, 64),
          ("w_in", 4, 7), ("w_in2", 5, 38), ("att2", 4, 38),
          ("w_out", 4, 8), ("proj0", 1, 4), ("gu0", 8, 16), ("dn0", 4, 8), ("gu1", 8, 16), ("dn1", 4, 8),
          ("gu2", 6, 12), ("dn2", 4, 8), ("proj1", 1, 4), ("ple", 4, 8), ("end2", 0, 0))
C, T = {}, {}


def _plan():
    c = t = 0
    for name, n_chunks, n_tiles in STAGES:
        C[name], T[name] = c, t
        c, t = c + n_chunks, t + n_tiles
    return c, t


N_CHUNKS, N_TILES = _plan()

SQUARED = (8, 8, 8, 2, 3, 8, 16, 0, 8, 8, 8, 8)
ADDED = (7, 7, 7, 1, 2, 7, 14, 0, 7, 7, 7, 7)
N_NORMS = len(SQUARED)
SQ = [sum(SQUARED[:n]) for n in range(N_NORMS + 1)]
SSQ = [sum(ADDED[:n]) for n in range(N_NORMS + 1)]
STATS = [n if n < 7 else n - 1 for n in range(N_NORMS)]

IDX_HEADS, TOPK = 8, 128
IDX_SCALE = IDX_HEADS ** -0.5 * 64 ** -0.5
HEAD_SCALE = 64 ** -0.5
ROUNDS_TOP = TOPK // 8
TAKEN = -3e38
IDX_OFF = [0, 0, 2 * P, 5 * P]
BUCKETS, MAX_DIST = 32, 128
ROWS = 3 * P
PAD = 16
GU_TILES = (8, 8, 6)
HID2 = 2 * 8 * ROUNDS
N_SILU = sum(GU_TILES)
RES_DVE, RES_POOL = (0, 2, 4, 7), (1, 3, 5, 6)
POOL_GROUPS = ((0, slice(0, 64), 0, 2), (0, slice(64, 128), 1, 4), (1, slice(0, 64), 2, 8), (1, slice(64, 128), 3, 16))
POOL_STEPS = (2, 2, 6, 6)
T_IDX = [None] + [T["w_in2"] + 10 * j for j in range(3)]
T_CK, T_CV, T_DQ, T_DK, T_DV = (T["w_in2"] + j for j in (8, 18, 28, 30, 36))
T_JOB = [T["w_in2"] + 32 if j == 0 else T["att2"] + 5 * (j - 1) for j in range(8)]
T_PROJ = [T["att2"] + 5 * j + 4 if j < 7 else T["att2"] + 37 for j in range(8)]
T_POOL = T["att2"] + 35
Q_TILES = ([T_DQ, T_DQ + 1, T_DK, T_DK + 1], [T["w_in"] + 5, T["w_in"] + 6, T_CK, T_CK + 1])
V_TILES = ([T_DV, T_DV + 1], [T_CV, T_CV + 1])
POOL_LO = (C["w_in2"], C["att2"] + 2)
MIX_PAIR, MIX_POOL, MIX_CONV = (0, 1, 2, 6), (3, 4), (5, 7)
NB_HEAD = (4, 5, 6, 7, 0, 1, 2, 3)

OFF = [P * i * (i + 1) // 2 for i in range(QT)]
ROWLEN = P * QT * (QT + 1) // 2


def build(nc, wst, xT, gains, cos, sin, ident_in, mask_in, lam, pT_in, tab_in, buckets_in, pool_w_in, pool_fix_in, outT):
    ctx = ExitStack()
    with ctx:
        def sem(name):
            return ctx.enter_context(nc.semaphore(name))

        base = [(nc.sbuf_base + 31) // 32 * 32]
        top = nc.sbuf_usable_end

        def at(name, shape, dt, offset):
            return nc.alloc_sbuf_tensor_at(name, shape, dt, offset=offset)

        def sb(name, shape, dt=F32):
            n = (2 if dt == BF16 else 4) * int(np.prod(shape[1:]))
            t = at(name, shape, dt, base[0])
            base[0] += (n + 31) // 32 * 32
            assert base[0] <= top, (name, base[0], top)
            return t

        h = sb("h", [P, KD, S])
        raw = [sb(f"raw{s}", [P, CHUNK]) for s in range(2)]
        whi = [sb(f"whi{s}", [P, CHUNK], F32R) for s in range(2)]
        wlo = [sb(f"wlo{s}", [P, CHUNK], F32R) for s in range(2)]
        xa_at = base[0]
        xa_hi, xa_lo = sb("xa_hi", [P, KD, S], F32R), sb("xa_lo", [P, KD, S], F32R)
        xb_at = base[0]
        xb_hi, xb_lo = sb("xb_hi", [P, KD, S], F32R), sb("xb_lo", [P, KD, S], F32R)
        cos_t, sin_t = sb("cos_t", [P, S]), sb("sin_t", [P, S])
        rstd_f = sb("rstd_f", [P, S])
        sq_at = base[0]
        sq_tmp, ssq = sb("sq_tmp", [P, S]), sb("ssq", [P, S])
        gain = sb("gain", [P, N_GAINS])
        ident = sb("ident", [P, P])
        mask = sb("mask", [P, P])
        ident_b, mask_b = sb("ident_b", [P, P], BF16), sb("mask_b", [P, P], BF16)
        ones = sb("ones", [P, 1])
        ms_t, rstd_t = sb("ms_t", [P, QT * N_NORMS]), sb("rstd_t", [P, QT * N_NORMS])
        r1_sq, r1_ms, r12 = (sb(n, [P, QT]) for n in ("r1_sq", "r1_ms", "r12"))
        tab = sb("tab", [P, HEADS])
        iw = sb("iw", [P, QT, IDX_HEADS])
        top8 = sb("top8", [P, 8])
        pool_fix = sb("pool_fix", [P, 2, PAD])
        g_x2 = sb("g_x2", [P, KD])
        half_neg = sb("half_neg", [P, QT])
        lam_ab = sb("lam_ab", [P, 4])
        neg_lam = sb("neg_lam", [P, 1])
        gsub = sb("gsub", [P, 1])
        negmin = sb("negmin", [P, 2, 8])
        rowsum, rinv = sb("rowsum", [P, 2, 8]), sb("rinv", [P, 2, QT])
        coef2, eps_o = sb("coef2", [P, 2, QT]), sb("eps_o", [P, HEADS, QT])
        o_ss, o_ms, o_rstd = (sb(n, [P, QT]) for n in ("o_ss", "o_ms", "o_rstd"))
        G = base[0]
        K = 1024

        qk = at("qk", [P, 2, 2, 4, S], F32, G)
        v_tok = at("v_tok", [P, QT, D], F32, G + 32 * K)
        stage = [at(f"stage{s}", [P, 2, S], F32, G + 48 * K + 4 * K * s) for s in range(2)]
        probs = [at(f"probs{s}", [P, 2, ROWLEN], F32, xa_at + 10 * K * s) for s in range(2)]
        pT = [at(f"pT{s}", [P, ROWLEN], F32, xa_at + 20 * K + 5 * K * s) for s in range(2)]
        cq, sq_, ck, sk = (at(n, [P, S], F32, xb_at + 2 * K * j) for j, n in enumerate(("cq", "sq_", "ck", "sk")))
        rope_tmp = at("rope_tmp", [P, 2, S], F32, xb_at + 8 * K)
        o_raw = [at(f"o_raw{s}", [P, QT, P], F32, G + 56 * K + 2 * K * s) for s in range(2)]
        o_sq = sq_tmp
        lam_in = at("lam_in", [P, 4, 64], F32, G)
        bias_rows = at("bias_rows", [P, ROWS], F32, G + 8 * K)
        buckets = at("buckets", [P, ROWS], F32, G + 20 * K)
        squares0 = at("squares0", [P, KD, S], F32, xb_at + 16 * K)
        iq = at("iq", [P, 4, S], F32, G)
        ik_iw = at("ik_iw", [P, S], F32, G + 8 * K)
        idx_score = at("idx_score", [P, 9 * P], F32, G + 10 * K)
        sel = at("sel", [P, 9 * P], BF16, sq_at)
        idx_relu = at("idx_relu", [P, 2, S], F32, G + 15 * K)
        cq2, ck2 = (at(n, [P, 2, S], F32, G + (20 + 4 * j) * K) for j, n in enumerate(("cq2", "ck2")))
        cv = at("cv", [P, QT, 256], F32, G + 28 * K)
        dq2, dk2 = (at(n, [P, 2, S], F32, G + (32 + 4 * j) * K) for j, n in enumerate(("dq2", "dk2")))
        dv = at("dv", [P, QT, 256], F32, G + 40 * K)
        nbias = at("nbias", [P, HEADS, 2 * P], F32, G + 44 * K)
        conv_in, conv_gate, conv_y = (at(n, [P, 2, S], F32, G + (52 + 4 * j) * K)
                                      for j, n in enumerate(("conv_in", "conv_gate", "conv_y")))
        ik_odd = at("ik_odd", [P, S], F32, G + 52 * K)
        r1_f = at("r1_f", [P, S], F32, G + 64 * K)
        squares = at("squares", [P, KD, S], F32, G + 48 * K)
        squares_g = at("squares_g", [P, KD, S], F32, G + 32 * K)
        pool_v = at("pool_v", [P, 2, PAD + S], F32, G + 32 * K)
        pool_s = [at(f"pool_s{j}", [P, PAD + S], F32, (G + 37 * K if j < 2 else xa_at + 26 * K) + 2112 * (j % 2))
                  for j in range(4)]
        pool_d = conv_in
        probs2 = [at(f"probs2{s}", [P, ROWLEN], F32, G + 5 * K * s) for s in range(2)]
        pT2 = at("pT2", [P, ROWLEN], F32, G + 15 * K)
        o2 = [t[:, :].rearrange("p (a b) -> p a b", a=QT) for t in (cos_t, sin_t)]
        pool_w = at("pool_w", [P, 2, P], F32, xa_at + 31 * K)
        gate_t, silu_t, up_t, hid_t = (at(n, [P, 2, S], F32, G + 4 * K * j)
                                       for j, n in enumerate(("gate_t", "silu_t", "up_t", "hid_t")))
        squares2 = at("squares2", [P, KD, S], F32, G)
        p_raw = at("p_raw", [P, 2, S], F32, G + 20 * K)
        p_hi, p_lo = (at(n, [P, 2, S], F32R, G + (24 + 4 * j) * K) for j, n in enumerate(("p_hi", "p_lo")))
        branch = at("branch", [P, KD, S], F32, G + 32 * K)
        projected = at("projected", [P, KD, S], F32, G + 48 * K)
        JOBS = [(dq2, dk2, dv, hd) for hd in range(4)] + [(cq2, ck2, cv, hd) for hd in range(4)]
        scratch = nc.dram_tensor("bias_scratch", (HEADS, P * ROWS), F32, kind="Internal").ap()
        rows_view = scratch.rearrange("h (p x) -> h p x", p=P)
        skewed = scratch[:, P - 1:P - 1 + P * (ROWS - 1)].rearrange("h (p x) -> p h x", p=P)[:, :, 0:2 * P]
        p_view = pT_in.rearrange("(k p) n -> p k n", p=P)
        out_view = outT.rearrange("(k p) n -> p k n", p=P)
        q_nope = at("q_nope", [P, HEADS, S], F32, xb_at)
        k_nope = at("k_nope", [P, HEADS, S], F32, xb_at + 16 * K)
        v_tok2 = at("v_tok2", [P, QT, D], F32, G)
        qr_eo = at("qr_eo", [P, 4, S], F32, G + 16 * K)
        k_eo = at("k_eo", [P, 2, S], F32, G + 24 * K)
        rope_tmp2 = at("rope_tmp2", [P, 2, S], F32, G + 28 * K)
        table2 = at("table2", [P, 2, S], F32, G + 32 * K)
        mla_qn = [at(f"mla_qn{s}", [P, S], F32, G + 28 * K + 2 * K * s) for s in range(2)]
        mla_qr = [at(f"mla_qr{s}", [P, S], F32, G + 32 * K + 2 * K * s) for s in range(2)]
        mla_kr = at("mla_kr", [P, S], F32, G + 36 * K)
        ckv = at("ckv", [P, 2, S], F32, G + 36 * K)
        ckv_hi, ckv_lo = (at(n, [P, 2, S], F32R, G + 40 * K + 4 * K * j) for j, n in enumerate(("ckv_hi", "ckv_lo")))
        cq_raw = at("cq_raw", [P, 3, S], F32, G + 48 * K)
        cq_hi, cq_lo = (at(n, [P, 3, S], F32R, G + 54 * K + 6 * K * j) for j, n in enumerate(("cq_hi", "cq_lo")))
        mla_probs = [at(f"mla_probs{s}", [P, ROWLEN], F32, G + 38 * K + 5 * K * s) for s in range(2)]
        mla_pT = [at(f"mla_pT{s}", [P, ROWLEN], F32, G + 48 * K + 5 * K * s) for s in range(2)]
        mla_o = [at(f"mla_o{s}", [P, QT, P], F32, G + 58 * K + 2 * K * s) for s in range(2)]
        u_tmp = at("u_tmp", [P, 2, S], F32, G)
        u_sq = at("u_sq", [P, 2, S], F32, G + 4 * K)
        assert G + 60 * K <= top, (G + 60 * K, top)

        ps = [ctx.enter_context(nc.psum_tensor(f"ps{b}", [P, S], F32)) for b in range(8)]
        STAT, BC, PT0, O_PS, OT = ps[6], ps[7], 4, ps[6], ps[7]

        raw_full = [sem(f"raw_full{s}") for s in range(2)]
        whi_done = sem("whi_done")
        wlo_done = sem("wlo_done")
        tile_done = sem("tile_done")
        bank_free = [sem(f"bank_free{b}") for b in range(4)]
        x_loaded = [sem(f"x_loaded{i}") for i in range(4)]
        const_loaded, gain_loaded, buckets_loaded = sem("const_loaded"), sem("gain_loaded"), sem("buckets_loaded")
        dve_const = sem("dve_const")
        xh_done = sem("xh_done")
        xl_done = sem("xl_done")
        hid_hi, hid_sq, hid_lo = sem("hid_hi"), sem("hid_sq"), sem("hid_lo")
        sq_done, ssq_done = sem("sq_done"), sem("ssq_done")
        stat_done, ms_done, rstd_t_done = sem("stat_done"), sem("ms_done"), sem("rstd_t_done")
        bc_done, rstd_f_done = sem("bc_done"), sem("rstd_f_done")
        table_done, rope_done = sem("table_done"), sem("rope_done")
        lam_done, lam_exp = sem("lam_done"), sem("lam_exp")
        kr_full = sem("kr_full")
        stage_full = [sem(f"stage_full{s}") for s in range(2)]
        mask_done, ri_done = sem("mask_done"), sem("ri_done")
        nm_done, rc_done, a_done = sem("nm_done"), sem("rc_done"), sem("a_done")
        tr_done, ptc_done = sem("tr_done"), sem("ptc_done")
        o_done, oc_done, sqo_done = sem("o_done"), sem("oc_done"), sem("sqo_done")
        oss_done, oms_done, orstd_done = sem("oss_done"), sem("oms_done"), sem("orstd_done")
        on_done, ot_done = sem("on_done"), sem("ot_done")
        rows_mm, rows_done, rows_stored, nbias_full = (sem(n) for n in ("rows_mm", "rows_done", "rows_stored", "nbias_full"))
        r12_done, small_done, idx_acc, top_done, sel_done = (sem(n) for n in ("r12_done", "small_done", "idx_acc", "top_done", "sel_done"))
        ik_full, iwt_done, diag_done = sem("ik_full"), sem("iwt_done"), sem("diag_done")
        conv_x, conv_step, conv_out = sem("conv_x"), sem("conv_step"), sem("conv_out")
        pool_zero, pool_s_done, pool_fix_done, pool_d_done = (sem(n) for n in ("pool_zero", "pool_s_done", "pool_fix_done", "pool_d_done"))
        nb_masked, x2_done, p_full, poolw_full = sem("nb_masked"), sem("x2_done"), sem("p_full"), sem("poolw_full")
        res_dve, res_pool, branch_done, silu_done, gated_done, y_done = (sem(n) for n in ("res_dve", "res_pool", "branch_done", "silu_done", "gated_done", "y_done"))
        out_done = sem("out_done")

        def gains_of(name):
            return lambda k: g(name, k)

        def gains_all(name):
            c0, n = GAINS[name]
            return gain[:, c0:c0 + n]

        def g(name, k):
            c0 = GAINS[name][0] + k
            return gain[:, c0:c0 + 1]

        X = dict(qkv=0, diff_o=8, mlp0=16, dkv=24, dq=32, ckv=40, cq=42, mla_o=45, mlp1=53, w_in=61, mix=69, p=77, ffn=79, ple=87)
        STAGE_DIFF = 64 * HEADS // 2
        NM_DIFF = 8 * HEADS
        NM_MLA = NM_DIFF + 4 * HEADS

        x_view = xT.rearrange("(k p) n -> p k n", p=P)
        consts = [(ident[:, :], ident_in), (cos_t[:, :], cos), (sin_t[:, :], sin),
                  (mask[:, :], mask_in), (lam_in[:, :, :].rearrange("p a b -> p (a b)"), lam.partition_broadcast(P)),
                  (tab[0:BUCKETS, :], tab_in),
                  (pool_fix[:, :, :].rearrange("p a b -> p (a b)"), pool_fix_in)]

        block = ctx.enter_context(nc.Block())

        @block.sync
        def _(sp):
            def load(c, slot):
                if not isinstance(c, int) or c >= 2:
                    sp.wait_ge(wlo_done, c - 1)
                sp.dma_start(raw[slot][:, :], wst[c]).then_inc(raw_full[slot], 16)

            def load_pairs(c0, c1):
                with sp.Fori(0, (c1 - c0) // 2) as i:
                    for s in range(2):
                        load(c0 + s + 2 * i, (c0 + s) % 2)
                if (c1 - c0) % 2:
                    load(c1 - 1, (c1 - 1) % 2)

            def stage_diff(par, half, first):
                if first:
                    sp.wait_ge(rope_done, 8)
                else:
                    sp.wait_ge(tile_done, T["diff"] + 8 * par + 16 * half - 8)
                for comp in range(2):
                    for hf in range(2):
                        src, dst = 32 * (2 * par + comp), 64 * comp + 32 * hf
                        sp.dma_start(stage[par][dst:dst + 32, :, :],
                                     qk[src:src + 32, hf, :, half, :]).then_inc(stage_full[par], 16)

            load(0, 0)
            sp.wait_ge(x_loaded[2], 16)
            load(1, 1)
            for dst, src in consts:
                sp.dma_start(dst, src).then_inc(const_loaded, 16)
            load_pairs(2, 14)
            stage_diff(0, 0, True)
            stage_diff(1, 0, True)
            with sp.Fori(1, HEADS // 2) as half:
                for par in range(2):
                    stage_diff(par, half, False)
            load_pairs(14, C["dkv"] + 2)
            load_pairs(C["dkv"] + 2, C["wo_b"] + 2)
            sp.wait_ge(rope_done, 9)
            for hf in range(2):
                sp.dma_start(mla_kr[32 * hf:32 * hf + 32, :], k_eo[0:32, hf, :]).then_inc(kr_full, 16)
            sp.wait_ge(rope_done, 11)
            for n in range(HEADS):
                tile = T["uq"] + 4 + n
                sp.wait_ge(bank_free[tile % 4], tile // 4 + 1)
                par, rows = n % 2, slice(32 * (n % 4), 32 * (n % 4) + 32)
                if n >= 2:
                    sp.wait_ge(tile_done, T["mla"] + 4 * (n - 1))
                sp.dma_start(mla_qn[par][:, :], q_nope[:, n, :]).then_inc(stage_full[par], 16)
                for hf in range(2):
                    sp.dma_start(mla_qr[par][32 * hf:32 * hf + 32, :],
                                 qr_eo[rows, 2 * (n // 4) + hf, :]).then_inc(stage_full[par], 16)
            load_pairs(C["wo_b"] + 2, C["mlp1"] + 1)
            sp.wait_ge(tile_done, T["wo_b"] + 1)
            sp.dma_start(buckets[0:BUCKETS, :], buckets_in).then_inc(buckets_loaded, 16)
            load_pairs(C["mlp1"] + 1, C["w_in"] + 4)
            sp.wait_ge(stat_done, STATS[6] + 1)
            sp.wait_ge(rows_stored, 16)
            sp.dma_start(nbias[:, :, :], skewed).then_inc(nbias_full, 16)
            sp.wait_ge(tile_done, T["w_in"])
            sp.dma_start(pool_w[:, :, :].rearrange("p a b -> p (a b)"), pool_w_in).then_inc(poolw_full, 16)
            load(C["w_in"] + 4, C["w_in"] % 2)
            t = T["w_in"] + 4
            sp.wait_ge(bank_free[t % 4], t // 4 + 1)
            sp.dma_start(ik_odd[64:128, :], ik_iw[0:64, :]).then_inc(ik_full, 16)
            load_pairs(C["w_in"] + 5, C["proj0"])
            sp.wait_ge(tile_done, T["w_out"] + 1)
            sp.dma_start(p_raw[:, :, :], p_view).then_inc(p_full, 16)
            load_pairs(C["proj0"], C["end2"])
            for k in range(KD):
                sp.wait_ge(y_done, k + 1)
                sp.dma_start(out_view[:, k, :], h[:, k, :]).then_inc(out_done, 16)

            sp.wait_ge(out_done, 16 * KD)

        @block.tensor
        def _(pe):
            def products(out, lhs_hi, lhs_lo, rhs_hi, rhs_lo, first, last):
                pe.matmul(out, lhs_hi, rhs_hi, start=first, stop=False)
                pe.matmul(out, lhs_hi, rhs_lo, start=False, stop=False)
                return pe.matmul(out, lhs_lo, rhs_hi, start=False, stop=last)

            def bank_ready(t, per=0, i=0):
                if not isinstance(i, int) or t // 4 + (per // 4) * i > 0:
                    pe.wait_ge(bank_free[t % 4], t // 4 + (per // 4) * i)

            def features(slot, c, t0, xhi, xlo, kt=KD, cols=256, n=2, a_from=0, per=0, i=0, fresh=None,
                         hook=None, hook_lo=None, pair_hook=None):
                pe.wait_ge(wlo_done, c + 1)
                w_hi, w_lo = (w[slot][:, 0:kt * cols].rearrange("p (k m) -> p k m", k=kt) for w in (whi, wlo))
                for a0 in range(0, n, 2):
                    pair = range(a0, min(a0 + 2, n))
                    late = fresh is not None and a0 == 0
                    if pair_hook is not None:
                        pair_hook(a0)
                    for a in pair:
                        bank_ready(t0 + a, per, i)
                    for k in range(kt):
                        if hook is not None:
                            hook(k)
                        if late:
                            pe.wait_ge(fresh[0], fresh[2] + k + 1)
                        for a in pair:
                            out, m = ps[(t0 + a) % 4][:, :], slice((a_from + a) * P, (a_from + a + 1) * P)
                            if late:
                                pe.matmul(out, w_hi[:, k, m], xhi[:, k, :], start=(k == 0), stop=False)
                                pe.matmul(out, w_lo[:, k, m], xhi[:, k, :], start=False, stop=False)
                                continue
                            mm = products(out, w_hi[:, k, m], w_lo[:, k, m], xhi[:, k, :], xlo[:, k, :],
                                          k == 0, k == kt - 1)
                            if k == kt - 1:
                                mm.then_inc(tile_done, 1)
                    for k in range(kt if late else 0):
                        if hook_lo is not None:
                            hook_lo(k)
                        pe.wait_ge(fresh[1], fresh[2] + k + 1)
                        for a in pair:
                            m = slice((a_from + a) * P, (a_from + a + 1) * P)
                            mm = pe.matmul(ps[(t0 + a) % 4][:, :], w_hi[:, k, m], xlo[:, k, :], start=False, stop=(k == kt - 1))
                            if k == kt - 1:
                                mm.then_inc(tile_done, 1)

            def tokens(slot, c, t0, xhi, xlo, per=0, i=0):
                pe.wait_ge(wlo_done, c + 1)
                w_hi = whi[slot][:, :].rearrange("p (k m) -> p k m", k=KD)
                w_lo = wlo[slot][:, :].rearrange("p (k m) -> p k m", k=KD)
                for u in range(2):
                    bank_ready(t0 + u, per, i)
                    for half in range(2):
                        q = slice((2 * u + half) * P, (2 * u + half + 1) * P)
                        out = ps[(t0 + u) % 4][:, half * 256:half * 256 + 256]
                        for k in range(KD):
                            mm = products(out, xhi[:, k, q], xlo[:, k, q], w_hi[:, k, :], w_lo[:, k, :],
                                          k == 0, k == KD - 1)
                    mm.then_inc(tile_done, 1)

            def stat(n):
                pe.wait_ge(ssq_done, SSQ[n + 1])
                if n >= 8:
                    pe.wait_ge(on_done, 3 * HEADS)
                for q in range(QT):
                    mm = pe.matmul(STAT[:, q:q + 1], ssq[:, q * P:(q + 1) * P], ones[:, :], start=True, stop=True)
                mm.then_inc(stat_done, 1)

            def broadcast(n, src=None):
                if src is None:
                    pe.wait_ge(rstd_t_done, n + 1)
                    src = rstd_t[:, 4 * n:4 * n + 4]
                for q in range(QT):
                    mm = pe.matmul(BC[:, q * P:(q + 1) * P], src[:, q:q + 1].to_broadcast([P, P]), ident[:, :],
                                   start=True, stop=True)
                mm.then_inc(bc_done, 1)

            def late_rstd(norm, k):
                if k == (0 if norm == 0 else 3):
                    stat(norm)
                elif k == (3 if norm == 0 else 6):
                    if norm == 0:
                        pe.wait_ge(const_loaded, 16 * len(consts))
                    broadcast(norm)

            def linear(stage, pairs, xhi, xlo, fresh, norm=None, hook=None):
                c, t = C[stage], T[stage]
                features(c % 2, c, t, xhi, xlo, fresh=fresh, hook=hook)
                features((c + 1) % 2, c + 1, t + 2, xhi, xlo,
                         hook=(lambda k: late_rstd(norm, k)) if norm is not None else None)
                with pe.Fori(1, pairs) as i:
                    for s in range(2):
                        features((c + s) % 2, c + s + 2 * i, t + 2 * s, xhi, xlo, per=4, i=i)

            def bias_by_distance():
                pe.wait_ge(buckets_loaded, 16)
                pe.matmul(ps[PT0][0:HEADS, 0:ROWS], tab[0:BUCKETS, :], buckets[0:BUCKETS, :], start=True, stop=True)\
                    .then_inc(rows_mm, 1)

            def mlp(stage, norm, xhi, xlo, hhi, hlo, x0, hid0, rows=False):
                c, t = C[stage], T[stage]

                def one_round(r, first):
                    for u in range(4):
                        hook = None
                        if first and u == 1:
                            hook = lambda k: broadcast(norm) if k == 4 else None
                        elif first and u == 2 and rows:
                            bias_by_distance()
                        features((c + u) % 2, c + u + 8 * r, t + 2 * u, xhi, xlo, per=16, i=r, hook=hook,
                                 fresh=(xh_done, xl_done, x0) if first and u == 0 else None)
                        if first and u == 0:
                            stat(norm)
                    for d in range(4):
                        features((c + d) % 2, c + 4 + d + 8 * r, t + 8 + 2 * d, hhi, hlo, per=16, i=r,
                                 fresh=(hid_hi, hid_lo, hid0 + 8 * r) if d == 0 else None)

                one_round(0, True)
                with pe.Fori(1, ROUNDS) as r:
                    one_round(r, False)

            linear("qk", 4, xa_hi, xa_lo, (xh_done, xl_done, X["qkv"]), norm=0)
            with pe.Fori(0, 2) as i:
                for s in range(2):
                    tokens((C["v"] + s) % 2, C["v"] + s + 2 * i, T["v"] + 2 * s, xa_hi, xa_lo, per=4, i=i)

            def mask_later(out):
                return pe.matmul(out, ident_b[:, :], mask_b[:, :], start=False, stop=True)

            def diff_scores(par, half, tiles):
                if tiles[0] == 0:
                    pe.wait_ge(stage_full[par], 64 * (half + 1))
                for i in tiles:
                    for comp in range(2):
                        n = 8 * par + 2 * i + comp
                        bank_ready(T["diff"] + n, 16, half)
                        rows, b = slice(64 * comp, 64 * comp + 64), ps[(T["diff"] + n) % 4]
                        pe.matmul(b[:, 0:P * (i + 1)], stage[par][rows, 0, P * i:P * (i + 1)],
                                  stage[par][rows, 1, 0:P * (i + 1)], start=True, stop=False)
                        mask_later(b[:, P * i:P * (i + 1)]).then_inc(tile_done, 1)

            def transposes(src, ready, n):
                for i in range(QT):
                    pe.wait_ge(*ready(i))
                    if not (isinstance(n, int) and 4 * n + i < 2):
                        pe.wait_ge(ptc_done, 4 * n + i - 1)
                    for kt in range(i + 1):
                        mm = pe.transpose(ps[PT0 + i % 2][:, kt * P:(kt + 1) * P],
                                          src[:, OFF[i] + kt * P:OFF[i] + (kt + 1) * P], ident[:, :])
                    mm.then_inc(tr_done, 1)

            def weighted(src, vals, head, n, taken):
                if not (isinstance(n, int) and n < 1):
                    pe.wait_ge(taken, n)
                for i in range(QT):
                    pe.wait_ge(ptc_done, 4 * n + i + 1)
                    for kt in range(i + 1):
                        mm = pe.matmul(O_PS[:, i * P:(i + 1) * P], src[:, OFF[i] + kt * P:OFF[i] + (kt + 1) * P],
                                       vals[:, kt, bass.ts(head, P)], start=(kt == 0), stop=(kt == i))
                mm.then_inc(o_done, 1)

            def turn(src, n, x_before):
                pe.wait_ge(on_done, n + 1)
                if not (isinstance(n, int) and n < 1):
                    pe.wait_ge(xl_done, x_before)
                for i in range(QT):
                    mm = pe.transpose(OT[:, i * P:(i + 1) * P], src[:, i, :], ident[:, :])
                mm.then_inc(ot_done, 1)

            def diff_step(par, half, first=0, scores=True):
                n = 2 * half + par
                if scores:
                    diff_scores(1 - par, half + par, (0, 1))
                if first >= 3:
                    turn(o_raw[1 - par], n - 3, X["diff_o"] + n - 3)
                if first >= 1:
                    weighted(pT[1 - par], v_tok, n - 1, n - 1, oc_done)
                transposes(probs[par][:, 0, :], lambda i: (a_done, 4 * n + i + 1), n)
                if scores:
                    diff_scores(1 - par, half + par, (2, 3))

            pe.wait_ge(dve_const, 5)
            diff_scores(0, 0, (0, 1))
            diff_scores(0, 0, (2, 3))
            for n in range(3):
                diff_step(n % 2, n // 2, first=n)
            with pe.Fori(1, HEADS // 2 - 1) as i:
                diff_step(1, i, first=3)
                diff_step(0, i + 1, first=3)
            diff_step(1, HEADS // 2 - 1, first=3, scores=False)
            turn(o_raw[1], HEADS - 3, X["diff_o"] + HEADS - 3)
            weighted(pT[1], v_tok, HEADS - 1, HEADS - 1, oc_done)
            turn(o_raw[0], HEADS - 2, X["diff_o"] + HEADS - 2)

            linear("wo_a", 2, xb_hi, xb_lo, (xh_done, xl_done, X["diff_o"]),
                   hook=lambda k: turn(o_raw[1], HEADS - 1, X["diff_o"] + HEADS - 1) if k == 5 else None)
            mlp("mlp0", 1, xa_hi, xa_lo, xb_hi, xb_lo, X["mlp0"], 0)
            c, t = C["dkv"], T["dkv"]
            features(c % 2, c, t, xa_hi, xa_lo, fresh=(xh_done, xl_done, X["dkv"]))
            stat(2)
            features((c + 1) % 2, c + 1, t + 2, xa_hi, xa_lo, hook=lambda k: broadcast(2) if k == 4 else None)
            features(c % 2, c + 2, t + 4, xb_hi, xb_lo, fresh=(xh_done, xl_done, X["dq"]))
            features((c + 1) % 2, c + 3, t + 6, xb_hi, xb_lo, n=1)
            stat(3)
            c, t = C["ukv"], T["ukv"]
            features(c % 2, c, t, ckv_hi, ckv_lo, kt=2, cols=1024, n=8,
                     fresh=(xh_done, xl_done, X["ckv"]),
                     pair_hook=lambda a: broadcast(3) if a == 2 else None)
            pe.wait_ge(wlo_done, c + 2)
            stat(4)
            w_hi, w_lo = (w[(c + 1) % 2][:, :].rearrange("p (k m) -> p k m", k=2) for w in (whi, wlo))
            for q in range(QT):
                for half in range(2):
                    tt = t + 8 + 2 * q + half
                    bank_ready(tt)
                    for k in range(2):
                        rows, cols = slice(q * P, q * P + P), slice(512 * half, 512 * half + 512)
                        mm = products(ps[tt % 4][:, :], ckv_hi[:, k, rows], ckv_lo[:, k, rows],
                                      w_hi[:, k, cols], w_lo[:, k, cols], k == 0, k == 1)
                    mm.then_inc(tile_done, 1)
            broadcast(4)
            c, t = C["uq"], T["uq"]
            for u in range(3):
                features((c + u) % 2, c + u, t + 4 * u, cq_hi, cq_lo, kt=3, cols=512, n=4,
                         fresh=(xh_done, xl_done, X["cq"]) if u == 0 else None)

            def mla_scores(par, n):
                pe.wait_ge(stage_full[par], STAGE_DIFF + 48 * (n // 2 + 1) if isinstance(n, int) else
                           STAGE_DIFF + 48 + 24 * (n - par))
                for i in range(QT):
                    bank_ready(T["mla"] + i, 4, n)
                    b, w, q = ps[(T["mla"] + i) % 4], P * (i + 1), slice(P * i, P * i + P)
                    pe.matmul(b[:, 0:w], mla_qn[par][:, q], k_nope[:, n, 0:w], start=True, stop=False)
                    pe.matmul(b[:, 0:w], mla_qr[par][0:64, q], mla_kr[0:64, 0:w], start=False, stop=False)
                    mask_later(b[:, q]).then_inc(tile_done, 1)

            def mla_step(par, n, scores=True, turn_last=True):
                if scores:
                    mla_scores(1 - par, n + 1)
                transposes(mla_probs[par], lambda i: (bank_free[(T["mla"] + i) % 4], (T["mla"] + i) // 4 + 1 + n),
                           HEADS + n)
                weighted(mla_pT[par], v_tok2, n, HEADS + n, on_done)
                if turn_last:
                    turn(mla_o[1 - par], HEADS + n - 1, X["mla_o"] + n - 1)

            pe.wait_ge(kr_full, 32)
            mla_scores(0, 0)
            mla_step(0, 0, turn_last=False)
            with pe.Fori(0, HEADS // 2 - 1) as i:
                mla_step(1, 2 * i + 1)
                mla_step(0, 2 * i + 2)
            mla_step(1, HEADS - 1, scores=False)

            linear("wo_b", 2, xa_hi, xa_lo, (xh_done, xl_done, X["mla_o"]),
                   hook=lambda k: turn(mla_o[1], 2 * HEADS - 1, X["mla_o"] + HEADS - 1) if k == 6 else None)
            mlp("mlp1", 5, xb_hi, xb_lo, xa_hi, xa_lo, X["mlp1"], 8 * ROUNDS, rows=True)
            c, t = C["w_in"], T["w_in"]
            features(c % 2, c, t, xb_hi, xb_lo, fresh=(xh_done, xl_done, X["w_in"]))
            pe.wait_ge(ssq_done, SSQ[7])
            for q in range(QT):
                for j, sums in enumerate((ssq, sq_tmp)):
                    mm = pe.matmul(STAT[:, 2 * q + j:2 * q + j + 1], sums[:, q * P:(q + 1) * P], ones[:, :],
                                   start=True, stop=True)
            mm.then_inc(stat_done, 1)

            def both_rstd(k):
                if k == 4:
                    pe.wait_ge(r12_done, 1)
                    broadcast(None, r12)

            features((c + 1) % 2, c + 1, t + 2, xb_hi, xb_lo, hook=both_rstd)
            def final_rstd(k):
                if k == 4:
                    pe.wait_ge(rstd_f_done, 7)
                    broadcast(6)

            features(c % 2, c + 2, t + 4, xb_hi, xb_lo, n=1, hook=final_rstd)
            features((c + 1) % 2, c + 3, t + 5, xb_hi, xb_lo)
            pe.wait_ge(bank_free[(t + 4) % 4], (t + 4) // 4 + 1)
            for q in range(QT):
                mm = pe.transpose(STAT[:, IDX_HEADS * q:IDX_HEADS * (q + 1)], ik_iw[64:64 + IDX_HEADS, q * P:(q + 1) * P],
                                  ident[64:64 + IDX_HEADS, 64:64 + IDX_HEADS])
            mm.then_inc(iwt_done, 1)
            def index_scores(i):
                for hd in range(IDX_HEADS):
                    tt = T_IDX[i] + hd
                    bank_ready(tt)
                    if i == 1 and hd == 0:
                        for tile in range(T["w_in"], T["w_in"] + 4):
                            pe.wait_ge(bank_free[tile % 4], tile // 4 + 1)
                        pe.wait_ge(ik_full, 16)
                    rows = slice(64 * (hd % 2), 64 * (hd % 2) + 64)
                    pe.matmul(ps[tt % 4][:, 0:P * (i + 1)], iq[rows, hd // 2, P * i:P * i + P],
                              (ik_iw, ik_odd)[hd % 2][rows, 0:P * (i + 1)], start=True, stop=True).then_inc(tile_done, 1)

            def scores2(jb):
                q, k, _, hd = JOBS[jb]
                rows = slice(64 * (hd % 2), 64 * (hd % 2) + 64)
                for i in range(QT):
                    tt = T_JOB[jb] + i
                    bank_ready(tt)
                    if jb in (0, 4) and i == 0:
                        for tile in Q_TILES[jb // 4]:
                            pe.wait_ge(bank_free[tile % 4], tile // 4 + 1)
                    out, chosen = ps[tt % 4][:, 0:P * (i + 1)], jb >= 4 and i >= 1
                    mm = pe.matmul(out, q[rows, hd // 2, P * i:P * i + P], k[rows, hd // 2, 0:P * (i + 1)],
                                   start=True, stop=not chosen)
                    if chosen:
                        pe.wait_ge(sel_done, i)
                        mm = pe.matmul(out, ident_b[:, :], sel[:, IDX_OFF[i]:IDX_OFF[i] + P * (i + 1)],
                                       start=False, stop=True)
                    mm.then_inc(tile_done, 1)

            def weighted2(jb):
                _, _, v, hd = JOBS[jb]
                n = 2 * HEADS + jb
                if jb in (0, 4):
                    for tile in V_TILES[jb // 4]:
                        pe.wait_ge(bank_free[tile % 4], tile // 4 + 1)
                pe.wait_ge(on_done, n)
                for i in range(QT):
                    pe.wait_ge(ptc_done, 4 * n + i + 1)
                    for kt in range(i + 1):
                        mm = pe.matmul(O_PS[:, i * 64:(i + 1) * 64],
                                       pT2[:, OFF[i] + kt * P:OFF[i] + (kt + 1) * P],
                                       v[:, kt, 64 * hd:64 * hd + 64], start=(kt == 0), stop=(kt == i))
                mm.then_inc(o_done, 1)

            def turn2(pair):
                pe.wait_ge(on_done, 2 * HEADS + 2 * pair + 2)
                if pair:
                    pe.wait_ge(xl_done, X["mix"] + MIX_PAIR[pair - 1] + 1)
                for i in range(QT):
                    mm = pe.transpose(OT[:, i * P:(i + 1) * P], o2[pair % 2][:, i, :], ident[:, :])
                mm.then_inc(ot_done, 1)

            c = C["w_in2"]
            index_scores(1)
            features(c % 2, c, T_CK, xb_hi, xb_lo)
            index_scores(2)
            tokens((c + 1) % 2, c + 1, T_CV, xb_hi, xb_lo)
            index_scores(3)
            features(c % 2, c + 2, T_DQ, xb_hi, xb_lo)
            features((c + 1) % 2, c + 3, T_DK, xb_hi, xb_lo)
            scores2(0)
            tokens(c % 2, c + 4, T_DV, xb_hi, xb_lo)
            for jb in range(8):
                if jb < 7:
                    scores2(jb + 1)
                transposes(probs2[jb % 2], lambda i: (bank_free[(T_JOB[jb] + i) % 4], (T_JOB[jb] + i) // 4 + 1),
                           2 * HEADS + jb)
                weighted2(jb)
                if jb >= 2 and jb % 2 == 0:
                    turn2((jb - 2) // 2)
                if jb == 7:
                    pe.wait_ge(pool_d_done, 4)
                    pe.wait_ge(poolw_full, 16)
                    for a in range(2):
                        bank_ready(T_POOL + a)
                        pe.matmul(ps[(T_POOL + a) % 4][:, :], pool_w[:, a, :], pool_d[:, a, :], start=True, stop=True)\
                            .then_inc(tile_done, 1)
                u = C["att2"] + jb // 2
                features(u % 2, u, T_PROJ[jb], xb_hi, xb_lo, n=1, a_from=jb % 2)
            turn2(3)

            linear("w_out", 2, xa_hi, xa_lo, (xh_done, xl_done, X["mix"]))

            def proj(u, fresh):
                c, t = C[f"proj{u}"], T[f"proj{u}"]
                features(c % 2, c, t, p_hi, p_lo, kt=2, cols=512, fresh=fresh)
                stat(8 + 2 * u)
                features(c % 2, c, t + 2, p_hi, p_lo, kt=2, cols=512, a_from=2,
                         hook=lambda k: broadcast(8 + 2 * u) if k == 1 else None)

            proj(0, (xh_done, xl_done, X["p"]))

            def gate_up(r, n, first):
                c, t = C[f"gu{r}"], T[f"gu{r}"]
                if first:
                    features(c % 2, c, t, xb_hi, xb_lo, fresh=(xh_done, xl_done, X["ffn"]))
                    features((c + 1) % 2, c + 1, t + 2, xb_hi, xb_lo, hook=lambda k: late_rstd(9, k))
                with pe.Fori(1 if first else 0, n // 2) as i:
                    for s in range(2):
                        features((c + s) % 2, c + s + 2 * i, t + 2 * s, xb_hi, xb_lo, per=4, i=i)

            def down(r, n):
                c, t = C[f"dn{r}"], T[f"dn{r}"]
                for s in range(2):
                    features((c + s) % 2, c + s, t + 2 * s, xa_hi, xa_lo, kt=n,
                             fresh=(hid_hi, hid_lo, HID2 + 8 * r) if s == 0 else None)
                for s in range(2):
                    features((c + s) % 2, c + 2 + s, t + 4 + 2 * s, xa_hi, xa_lo, kt=n)

            for r, n in enumerate(GU_TILES):
                gate_up(r, n, r == 0)
                down(r, n)
            proj(1, None)

            linear("ple", 2, xb_hi, xb_lo, (xh_done, xl_done, X["ple"]), norm=11)

        @block.scalar
        def _(act):
            def hi(c0, j, t_before):
                slot = c0 % 2
                act.wait_ge(raw_full[slot], 16 * (c0 // 2 + 1) + 8 * j)
                if not isinstance(t_before, int) or t_before > 0:
                    act.wait_ge(tile_done, t_before)
                act.activation(whi[slot][:, :], raw[slot][:, :], ACT.Copy).then_inc(whi_done, 1)

            def bank_out(t, per=0, i=0):
                act.wait_ge(bank_free[t % 4], t // 4 + 1 + (per // 4) * i)

            def x_hi(dst, src, scale):
                act.activation(dst, src, ACT.Copy, scale=scale).then_inc(xh_done, 1)

            act.dma_start(gain[:, :], gains).then_inc(gain_loaded, 16)
            for i in range(4):
                act.dma_start(h[:, 2 * i:2 * i + 2, :], x_view[:, 2 * i:2 * i + 2, :]).then_inc(x_loaded[i], 16)
            hi(0, 0, 0)
            act.wait_ge(gain_loaded, 16)
            for k in range(KD):
                act.wait_ge(x_loaded[k // 2], 16)
                x_hi(xa_hi[:, k, :], h[:, k, :], g("attn0", k))
            for k in range(KD):
                act.activation(squares0[:, k, :], h[:, k, :], ACT.Square).then_inc(sq_done, 1)

            c, t = C["qk"], T["qk"]
            hi(c + 1, 0, 0)
            act.wait_ge(lam_done, 2)
            act.activation(lam_ab[:, 2:4], lam_ab[:, 0:2], ACT.Exp).then_inc(lam_exp, 1)
            hi(c + 2, 0, t + 2)
            with act.Fori(1, 4) as i:
                for s in range(2):
                    hi(c + s + 1, 2 * i, t + 2 * s + 4 * i)

            c, t = C["v"], T["v"]
            act.wait_ge(rstd_t_done, 1)
            with act.Fori(0, 2) as i:
                for s in range(2):
                    hi(c + s + 1, 2 * i, t + 2 * s + 4 * i)
                    for u in range(2):
                        tt = t + 2 * s + u
                        act.wait_ge(tile_done, tt + 1 + 4 * i)
                        for half in range(2):
                            q = 2 * u + half
                            ins = act.activation(v_tok[:, q, bass.ds(256 * s + 512 * i, 256)],
                                                 ps[tt % 4][:, 256 * half:256 * half + 256],
                                                 ACT.Copy, scale=rstd_t[:, q:q + 1])
                        ins.then_inc(bank_free[tt % 4], 1)

            def diff_exp(par, half, tiles):
                n = 2 * half + par
                for i in tiles:
                    for comp in range(2):
                        j = 2 * i + comp
                        b = (T["diff"] + 8 * par + j) % 4
                        act.wait_ge(nm_done, 8 * n + j + 1)
                        if j == 0 and not (isinstance(half, int) and half < 1):
                            act.wait_ge(tr_done, 4 * (n - 1))
                        act.activation(probs[par][:, comp, OFF[i]:OFF[i] + P * (i + 1)], ps[b][:, 0:P * (i + 1)],
                                       ACT.Exp, bias=negmin[:, par, j:j + 1], scale=-1.0,
                                       accum_out=rowsum[:, par, j:j + 1]).then_inc(bank_free[b], 1)

            def copy_pT(pT, par, n, tiles=range(QT)):
                for i in tiles:
                    act.wait_ge(tr_done, 4 * n + i + 1)
                    if i == 0 and not (isinstance(n, int) and n < 2):
                        act.wait_ge(o_done, n - 1)
                    act.activation(pT[par][:, OFF[i]:OFF[i] + P * (i + 1)], ps[PT0 + i % 2][:, 0:P * (i + 1)],
                                   ACT.Copy).then_inc(ptc_done, 1)

            def diff_copy_o(par, n):
                act.wait_ge(o_done, n + 1)
                if not (isinstance(n, int) and n < 2):
                    act.wait_ge(ot_done, n - 1)
                act.activation(o_raw[par][:, :, :].rearrange("p a b -> p (a b)"), O_PS[:, :],
                               ACT.Copy).then_inc(oc_done, 1)

            def head_hi(dst, n, n0, scale):
                act.wait_ge(ot_done, n0 + n + 1)
                act.activation(dst[:, n, :], OT[:, :], ACT.Copy, scale=scale).then_inc(xh_done, 1)

            def diff_step(par, half, first=0, ahead=True):
                n = 2 * half + par
                if ahead:
                    diff_exp(1 - par, half + par, (0, 1))
                if first >= 3:
                    head_hi(xb_hi, n - 3, 0, gsub[:, 0:1])
                if not ahead:
                    diff_copy_o(1 - par, n - 1)
                copy_pT(pT, par, n)
                if first >= 1 and ahead:
                    diff_copy_o(1 - par, n - 1)
                if ahead:
                    diff_exp(1 - par, half + par, (2, 3))

            act.wait_ge(dve_const, 4)
            diff_exp(0, 0, range(QT))
            for n in range(3):
                diff_step(n % 2, n // 2, first=n)
            with act.Fori(1, HEADS // 2 - 1) as i:
                diff_step(1, i, first=3)
                diff_step(0, i + 1, first=3)
            diff_step(1, HEADS // 2 - 1, first=3, ahead=False)
            head_hi(xb_hi, HEADS - 3, 0, gsub[:, 0:1])
            diff_copy_o(1, HEADS - 1)
            for n in (HEADS - 2, HEADS - 1):
                head_hi(xb_hi, n, 0, gsub[:, 0:1])

            def residual(stage, dst, gname):
                c, t = C[stage], T[stage]
                for u in range(4):
                    hi(c + u + 1, 0, t + 2 * u)
                    for a in range(2):
                        bank_out(t + 2 * u + a)
                        x_hi(dst[:, 2 * u + a, :], h[:, 2 * u + a, :], gname(2 * u + a))

            def mlp(stage, hhi, dst, gname, rows=False):
                c, t = C[stage], T[stage]

                def one_round(r, first, last):
                    for u in range(4):
                        if not (first and u == 1):
                            hi(c + u + 1, 8 * r, t + 2 * u + 16 * r)
                        if first and u == 0:
                            hi(c + 2, 0, t + 2)
                        if first and u == 2 and rows:
                            act.wait_ge(rows_mm, 1)
                            act.activation(bias_rows[0:HEADS, :], ps[PT0][0:HEADS, 0:ROWS], ACT.Copy).then_inc(rows_done, 1)
                            act.wait_ge(rows_done, 1)
                            act.dma_start(rows_view, bias_rows[0:HEADS, :].unsqueeze(1).to_broadcast([HEADS, P, ROWS]))\
                                .then_inc(rows_stored, 16)
                        for a in range(2):
                            bank_out(t + 2 * u + a, 16, r)
                            act.activation(hhi[:, 2 * u + a, :], u_tmp[:, a, :], ACT.Square).then_inc(hid_hi, 1)
                    for d in range(4):
                        hi(c + d + 5, 8 * r, t + 8 + 2 * d + 16 * r)
                        if last:
                            for a in range(2):
                                k = 2 * d + a
                                bank_out(t + 8 + k, 16, r)
                                x_hi(dst[:, k, :], h[:, k, :], gname(k))
                                if rows:
                                    act.activation(squares[:, k, :], h[:, k, :], ACT.Square).then_inc(sq_done, 1)
                                    act.activation(squares_g[:, k, :], h[:, k, :], ACT.Square, scale=g("final", k))\
                                        .then_inc(sq_done, 1)

                one_round(0, True, False)
                with act.Fori(1, ROUNDS - 1) as r:
                    one_round(r, False, False)
                one_round(ROUNDS - 1, False, True)

            residual("wo_a", xa_hi, gains_of("mlp0"))
            mlp("mlp0", xb_hi, xa_hi, gains_of("kv_in"))
            c, t = C["dkv"], T["dkv"]
            hi(c + 1, 0, t)
            for k in range(KD):
                x_hi(xb_hi[:, k, :], h[:, k, :], g("attn1", k))
            hi(c + 2, 0, t + 2)
            for a in range(2):
                bank_out(t + a)
                x_hi(ckv_hi[:, a, :], ckv[:, a, :], g("kv", a))
            hi(c + 3, 0, t + 4)
            hi(c + 4, 0, t + 6)
            for a in range(3):
                bank_out(t + 4 + a)
                x_hi(cq_hi[:, a, :], cq_raw[:, a, :], g("q", a))
            c, t = C["ukv"], T["ukv"]
            hi(c + 1, 0, t)
            hi(c + 2, 0, t + 8)
            act.wait_ge(rstd_t_done, 4)
            for q in range(QT):
                for half in range(2):
                    tt = t + 8 + 2 * q + half
                    act.wait_ge(tile_done, tt + 1)
                    act.activation(v_tok2[:, q, 512 * half:512 * half + 512], ps[tt % 4][:, :], ACT.Copy,
                                   scale=rstd_t[:, 12 + q:13 + q]).then_inc(bank_free[tt % 4], 1)
            c, t = C["uq"], T["uq"]
            for u in range(3):
                hi(c + u + 1, 0, t + 4 * u)

            def mla_exp(par, n, tiles=range(QT)):
                for i in tiles:
                    b = (T["mla"] + i) % 4
                    act.wait_ge(nm_done, NM_DIFF + 4 * n + i + 1)
                    if i == 0 and not (isinstance(n, int) and n < 2):
                        act.wait_ge(tr_done, 4 * (HEADS + n - 1))
                    act.activation(mla_probs[par][:, OFF[i]:OFF[i] + P * (i + 1)], ps[b][:, 0:P * (i + 1)],
                                   ACT.Exp, bias=negmin[:, par, i:i + 1], scale=-1.0,
                                   accum_out=rowsum[:, par, i:i + 1]).then_inc(bank_free[b], 1)

            def mla_step(par, n, ahead=True, behind=True):
                if ahead:
                    mla_exp(1 - par, n + 1, (0, 1, 2))
                copy_pT(mla_pT, par, HEADS + n, (0, 1))
                if ahead:
                    mla_exp(1 - par, n + 1, (3,))
                copy_pT(mla_pT, par, HEADS + n, (2, 3))
                if behind:
                    head_hi(xa_hi, n - 1, HEADS, 1.0)

            mla_exp(0, 0)
            mla_step(0, 0, behind=False)
            with act.Fori(0, HEADS // 2 - 1) as i:
                mla_step(1, 2 * i + 1)
                mla_step(0, 2 * i + 2)
            mla_step(1, HEADS - 1, ahead=False)
            head_hi(xa_hi, HEADS - 1, HEADS, 1.0)

            residual("wo_b", xb_hi, gains_of("mlp1"))
            mlp("mlp1", xa_hi, xb_hi, lambda k: g_x2[:, k:k + 1], rows=True)
            c, t = C["w_in"], T["w_in"]
            for u in range(4):
                hi(c + u + 1, 0, t + (0, 2, 4, 5)[u])
            def index_relu(i):
                for hd in range(IDX_HEADS):
                    j, tt = IDX_HEADS * (i - 1) + hd, T_IDX[i] + hd
                    act.wait_ge(tile_done, tt + 1)
                    if j >= 2:
                        act.wait_ge(idx_acc, j - 1)
                    act.activation(idx_relu[:, j % 2, 0:P * (i + 1)], ps[tt % 4][:, 0:P * (i + 1)], ACT.Relu)\
                        .then_inc(bank_free[tt % 4], 1)

            def take_tokens(dst, t):
                for u in range(2):
                    tt = t + u
                    act.wait_ge(tile_done, tt + 1)
                    for half in range(2):
                        q = 2 * u + half
                        ins = act.activation(dst[:, q, :], ps[tt % 4][:, 256 * half:256 * half + 256], ACT.Copy,
                                             scale=r12[:, q:q + 1])
                    ins.then_inc(bank_free[tt % 4], 1)

            def exp2(jb):
                for i in range(QT):
                    b, j = (T_JOB[jb] + i) % 4, 4 * jb + i
                    act.wait_ge(nm_done, NM_MLA + j + 1)
                    if i == 0 and jb >= 2:
                        act.wait_ge(tr_done, 4 * (2 * HEADS + jb - 1))
                    act.activation(probs2[jb % 2][:, OFF[i]:OFF[i] + P * (i + 1)], ps[b][:, 0:P * (i + 1)],
                                   ACT.Exp, bias=negmin[:, jb % 2, i:i + 1], scale=-1.0,
                                   accum_out=rowsum[:, jb % 2, i:i + 1]).then_inc(bank_free[b], 1)

            def copy_pT2(jb, tiles):
                n = 2 * HEADS + jb
                for i in tiles:
                    act.wait_ge(tr_done, 4 * n + i + 1)
                    if i == 0 and jb:
                        act.wait_ge(o_done, n)
                    act.activation(pT2[:, OFF[i]:OFF[i] + P * (i + 1)], ps[PT0 + i % 2][:, 0:P * (i + 1)],
                                   ACT.Copy).then_inc(ptc_done, 1)

            def pair_hi(pair):
                act.wait_ge(ot_done, 2 * HEADS + pair + 1)
                x_hi(xa_hi[:, MIX_PAIR[pair], :], OT[:, :], 1.0)

            def conv_hi(a):
                act.wait_ge(conv_out, a + 1)
                x_hi(xa_hi[:, MIX_CONV[a], :], conv_y[:, a, :], 1.0)

            act.wait_ge(r12_done, 1)
            c = C["w_in2"]
            index_relu(1)
            hi(c + 1, 0, T["w_in2"])
            index_relu(2)
            hi(c + 2, 0, T_CK + 2)
            take_tokens(cv, T_CV)
            index_relu(3)
            hi(c + 3, 0, T_CV + 2)
            hi(c + 4, 0, T_DQ + 2)
            exp2(0)
            hi(c + 5, 0, T_DK + 2)
            take_tokens(dv, T_DV)
            c = C["att2"]
            for jb in range(8):
                copy_pT2(jb, range(QT))
                if jb < 7:
                    exp2(jb + 1)
                if jb >= 2 and jb % 2 == 0:
                    pair_hi((jb - 2) // 2)
                if jb % 2 == 0:
                    hi(c + jb // 2 + 1, 0, T_PROJ[jb - 1] + 1 if jb else T_DV + 2)
            for a in range(2):
                act.wait_ge(tile_done, T_POOL + a + 1)
                x_hi(xa_hi[:, MIX_POOL[a], :], ps[(T_POOL + a) % 4][:, :], g("pool_scale", a))
            conv_hi(0)
            pair_hi(3)
            conv_hi(1)

            def take_copy(dst, tt, square=None):
                act.wait_ge(tile_done, tt + 1)
                if square is not None:
                    act.activation(square, ps[tt % 4][:, :], ACT.Square).then_inc(sq_done, 1)
                act.activation(dst, ps[tt % 4][:, :], ACT.Copy).then_inc(bank_free[tt % 4], 1)

            c, t = C["w_out"], T["w_out"]
            for u in range(4):
                hi(c + u + 1, 0, t + 2 * u)
                if u == 2:
                    act.wait_ge(p_full, 16)
                    for a in range(2):
                        x_hi(p_hi[:, a, :], p_raw[:, a, :], 1.0)
                for a in range(2):
                    take_copy(branch[:, 2 * u + a, :], t + 2 * u + a, square=squares2[:, 2 * u + a, :])

            def proj(u):
                hi(C[f"proj{u}"] + 1, 0, T[f"proj{u}"])
                for a in range(4):
                    take_copy(projected[:, 4 * u + a, :], T[f"proj{u}"] + a)

            def onto_residual(gname, n0, stage):
                def part(k):
                    done, order = (res_dve, RES_DVE) if k in RES_DVE else (res_pool, RES_POOL)
                    act.wait_ge(done, len(order) * n0 + order.index(k) + 1)
                    x_hi(xb_hi[:, k, :], h[:, k, :], g(gname, k))

                def square(k):
                    act.activation(squares2[:, k, :], h[:, k, :], ACT.Square).then_inc(sq_done, 1)

                squared = 0
                for k in range(KD):
                    part(k)
                    if k in (0, 2, 5):
                        square(squared)
                        squared += 1
                hi(C[stage] + 1, 0, T[stage])
                for k in range(squared, KD):
                    square(k)

            proj(0)
            onto_residual("ffn_pre", 0, "gu0")

            def gate_up(r, n):
                c, t = C[f"gu{r}"], T[f"gu{r}"]

                def pair(i, first=False):
                    for s in range(2):
                        if not first:
                            hi(c + s + 1, 2 * i, t + 2 * s + 4 * i)
                        if first and s == 0:
                            hi(c + 2, 0, t + 2)
                        act.wait_ge(bank_free[(t + 2 * s) % 4], (t + 2 * s) // 4 + 1 + i)
                        act.activation(silu_t[:, s, :], gate_t[:, s, :], ACT.Silu).then_inc(silu_done, 1)
                        act.wait_ge(hid_sq, HID2 + 8 * r + 2 * i + s + 1)
                        act.activation(xa_hi[:, 2 * i + s, :], hid_t[:, s, :], ACT.Copy).then_inc(hid_hi, 1)

                pair(0, first=(r == 0))
                with act.Fori(1, n // 2) as i:
                    pair(i)

            def down(r):
                c, t = C[f"dn{r}"], T[f"dn{r}"]
                for u in range(4):
                    hi(c + u + 1, 0, t + 2 * u)
                    for a in range(2):
                        if r == 0:
                            take_copy(branch[:, 2 * u + a, :], t + 2 * u + a)
                        elif r == len(GU_TILES) - 1:
                            bank_out(t + 2 * u + a)
                            act.activation(squares2[:, 2 * u + a, :], branch[:, 2 * u + a, :], ACT.Square).then_inc(sq_done, 1)

            for r, n in enumerate(GU_TILES):
                gate_up(r, n)
                down(r)
            proj(1)
            onto_residual("ple", 1, "ple")

            c, t = C["ple"], T["ple"]
            hi(c + 2, 0, t + 2)
            for u in range(4):
                if u == 1:
                    hi(c + 3, 0, t + 4)
                for a in range(2):
                    k = 2 * u + a
                    bank_out(t + k)
                    if u:
                        act.wait_ge(gated_done, k - 1)
                    act.activation(silu_t[:, a, :], gate_t[:, a, :], ACT.Sigmoid).then_inc(silu_done, 1)

        @block.vector
        def _(dve):
            def lo(c, slot):
                dve.wait_ge(whi_done, c + 1)
                dve.tensor_tensor(wlo[slot][:, :], raw[slot][:, :], whi[slot][:, :].bitcast(F32),
                                  ALU.subtract).then_inc(wlo_done, 1)

            def x_lo(dst, src, scale, dst_hi, n):
                dve.wait_ge(xh_done, n + 1)
                dve.scalar_tensor_tensor(out=dst, in0=src, scalar=scale, in1=dst_hi.bitcast(F32),
                                         op0=ALU.mult, op1=ALU.subtract).then_inc(xl_done, 1)

            def mean_square(n, dim):
                dve.wait_ge(stat_done, STATS[n] + 1)
                dve.tensor_scalar(ms_t[:, 4 * n:4 * n + 4], STAT[:, 0:QT], 1.0 / dim, EPS, ALU.mult, ALU.add).then_inc(ms_done, 1)

            def take_rstd(n, dst=None):
                dve.wait_ge(bc_done, n + 1)
                dve.tensor_copy((rstd_f if dst is None else dst)[:, :], BC[:, :]).then_inc(rstd_f_done, 1)
                dve.wait_ge(rstd_f_done, n + 1 - (n > 8) - (n > 10))

            def tile_ready(t, per=0, i=0):
                dve.wait_ge(tile_done, t + 1 + per * i)

            dve.memset(ones[:, :], 1.0)
            dve.memset(half_neg[:, :], -0.5).then_inc(dve_const, 1)
            lo(0, 0)
            dve.wait_ge(gain_loaded, 16)
            for k in range(KD):
                x_lo(xa_lo[:, k, :], h[:, k, :], g("attn0", k), xa_hi[:, k, :], X["qkv"] + k)
            lo(1, 1)
            dve.wait_ge(const_loaded, 16 * len(consts))
            for j in range(2):
                dve.tensor_tensor_reduce(out=lam_in[:, 2 * j, :], in0=lam_in[:, 2 * j, :],
                                         in1=lam_in[:, 2 * j + 1, :], scale=1.0, scalar=0.0, op0=ALU.mult,
                                         op1=ALU.add, accum_out=lam_ab[:, j:j + 1]).then_inc(lam_done, 1)
            dve.wait_ge(lam_exp, 1)
            dve.scalar_tensor_tensor(out=neg_lam[:, :], in0=lam_ab[:, 3:4], scalar=-LAMBDA_INIT, in1=lam_ab[:, 2:3],
                                     op0=ALU.add, op1=ALU.subtract).then_inc(dve_const, 1)
            dve.tensor_tensor(g_x2[:, :], gains_all("final"), gains_all("mix_pre"), ALU.mult).then_inc(dve_const, 1)
            dve.tensor_scalar(gsub[:, :], g("subln", 0), 1.0 - LAMBDA_INIT, None, ALU.mult).then_inc(dve_const, 1)
            dve.tensor_copy(ident_b[:, :], ident[:, :])
            dve.tensor_copy(mask_b[:, :], mask[:, :]).then_inc(dve_const, 1)

            def rope(t, dst1, dst2, cos_n, sin_n, rope_tmp, n_before, per=0, i=0):
                be, bo = ps[t % 4], ps[(t + 1) % 4]
                tile_ready(t + 1, per, i)
                if not (isinstance(n_before, int) and n_before < 1):
                    dve.wait_ge(rope_done, n_before)
                dve.tensor_tensor(dst1, be[:, :], cos_n[:, :], ALU.mult)
                dve.tensor_tensor(rope_tmp[:, 1, :], be[:, :], sin_n[:, :], ALU.mult).then_inc(bank_free[t % 4], 1)
                dve.tensor_tensor(rope_tmp[:, 0, :], bo[:, :], sin_n[:, :], ALU.mult)
                dve.tensor_tensor(dst2, bo[:, :], cos_n[:, :], ALU.mult).then_inc(bank_free[(t + 1) % 4], 1)

            c, t = C["qk"], T["qk"]
            mean_square(0, D)
            lo(c + 2, c % 2)
            take_rstd(0)
            for dst, src, s in ((cq, cos_t, -DIFF_SCALE), (sq_, sin_t, -DIFF_SCALE), (ck, cos_t, 1.0), (sk, sin_t, 1.0)):
                dve.scalar_tensor_tensor(out=dst[:, :], in0=src[:, :], scalar=s, in1=rstd_f[:, :],
                                         op0=ALU.mult, op1=ALU.mult).then_inc(table_done, 1)
            dve.wait_ge(table_done, 4)
            rope(t, qk[:, 0, 0, 0, :], qk[:, 1, 0, 0, :], cq, sq_, rope_tmp, 0)
            rope(t + 2, qk[:, 0, 1, 0, :], qk[:, 1, 1, 0, :], ck, sk, rope_tmp, 1)
            with dve.Fori(1, 4) as i:
                for s in range(2):
                    lo(c + s + 1 + 2 * i, (c + s + 1) % 2)
                    rope(t + 2 * s, qk[:, 0, s, i, :], qk[:, 1, s, i, :], (cq, ck)[s], (sq_, sk)[s],
                         rope_tmp, 2 * i + s, per=4, i=i)

            c = C["v"]
            with dve.Fori(0, 2) as i:
                for s in range(2):
                    lo(c + s + 1 + 2 * i, (c + s + 1) % 2)

            def diff_min(par, half, tiles):
                for i in tiles:
                    for comp in range(2):
                        j = 2 * i + comp
                        b = ps[(T["diff"] + 8 * par + j) % 4]
                        tile_ready(T["diff"] + 8 * par + j, 16, half)
                        dve.tensor_reduce(negmin[:, par, j:j + 1], b[:, 0:P * (i + 1)], AX.X, ALU.min)\
                           .then_inc(nm_done, 1)

            def diff_coefs(par, half):
                n = 2 * half + par
                s1, s2 = rowsum[:, par, 0:8:2], rowsum[:, par, 1:8:2]
                b = (T["diff"] + 8 * par + 7) % 4
                dve.wait_ge(bank_free[b], (T["diff"] + 8 * par + 7) // 4 + 1 + 4 * half)
                dve.reciprocal(rinv[:, par, :], s2).then_inc(ri_done, 1)
                dve.wait_ge(ri_done, n + 1)
                dve.scalar_tensor_tensor(out=coef2[:, par, :], in0=rinv[:, par, :], scalar=neg_lam[:, 0:1], in1=s1,
                                         op0=ALU.mult, op1=ALU.mult).then_inc(rc_done, 1)
                dve.scalar_tensor_tensor(out=eps_o[:, n, :], in0=s1, scalar=SUBLN_EPS, in1=s1,
                                         op0=ALU.mult, op1=ALU.mult)
                dve.wait_ge(rc_done, n + 1)

            def diff_combine(par, half):
                for i in range(QT):
                    w = slice(OFF[i], OFF[i] + P * (i + 1))
                    dve.scalar_tensor_tensor(out=probs[par][:, 0, w], in0=probs[par][:, 1, w],
                                             scalar=coef2[:, par, i:i + 1], in1=probs[par][:, 0, w],
                                             op0=ALU.mult, op1=ALU.add).then_inc(a_done, 1)

            def diff_mean_square(n):
                dve.wait_ge(sqo_done, n + 1)
                dve.tensor_reduce(o_ss[:, :], o_sq[:, :].rearrange("p (a b) -> p a b", a=QT), AX.X, ALU.add)\
                   .then_inc(oss_done, 1)
                dve.wait_ge(oss_done, n + 1)
                dve.scalar_tensor_tensor(out=o_ms[:, :], in0=o_ss[:, :], scalar=1.0 / P, in1=eps_o[:, n, :],
                                         op0=ALU.mult, op1=ALU.add).then_inc(oms_done, 1)

            def head_lo(dst, dst_hi, n, x0, scale):
                dve.wait_ge(xh_done, x0 + n + 1)
                dve.scalar_tensor_tensor(out=dst[:, n, :], in0=OT[:, :], scalar=scale,
                                         in1=dst_hi[:, n, :].bitcast(F32),
                                         op0=ALU.mult, op1=ALU.subtract).then_inc(xl_done, 1)

            def diff_step(par, half, first=0, ahead=True):
                n = 2 * half + par
                if not ahead:
                    diff_mean_square(n - 2)
                diff_coefs(par, half)
                if ahead:
                    diff_min(1 - par, half + par, (0, 1))
                diff_combine(par, half)
                if first >= 3:
                    head_lo(xb_lo, xb_hi, n - 3, X["diff_o"], gsub[:, 0:1])
                if first >= 2 and ahead:
                    diff_mean_square(n - 2)
                if ahead:
                    diff_min(1 - par, half + par, (2, 3))

            dve.wait_ge(dve_const, 4)
            diff_min(0, 0, range(QT))
            for n in range(3):
                diff_step(n % 2, n // 2, first=n)
            with dve.Fori(1, HEADS // 2 - 1) as i:
                diff_step(1, i, first=3)
                diff_step(0, i + 1, first=3)
            diff_step(1, HEADS // 2 - 1, first=3, ahead=False)
            diff_mean_square(HEADS - 2)
            head_lo(xb_lo, xb_hi, HEADS - 3, X["diff_o"], gsub[:, 0:1])
            diff_mean_square(HEADS - 1)
            for n in (HEADS - 2, HEADS - 1):
                head_lo(xb_lo, xb_hi, n, X["diff_o"], gsub[:, 0:1])

            def residual(stage, dst, dst_hi, gname, x0):
                c, t = C[stage], T[stage]
                for u in range(4):
                    lo(c + u + 1, (c + u + 1) % 2)
                    for a in range(2):
                        add_residual(2 * u + a, t + 2 * u + a)
                    for a in range(2):
                        k = 2 * u + a
                        x_lo(dst[:, k, :], h[:, k, :], gname(k), dst_hi[:, k, :], x0 + k)

            def add_residual(k, t, per=0, i=0):
                tile_ready(t, per, i)
                dve.tensor_tensor(h[:, k, :], ps[t % 4][:, :], h[:, k, :], ALU.add).then_inc(bank_free[t % 4], 1)

            def mlp(stage, norm, dst, dst_hi, gname, x0, hid0):
                c, t = C[stage], T[stage]

                def one_round(r, first, last):
                    for u in range(4):
                        if not (first and u == 1):
                            lo(c + u + 1 + 8 * r, (c + u + 1) % 2)
                        if first and u == 0:
                            lo(c + 2, c % 2)
                            mean_square(norm, D)
                            take_rstd(norm)
                        for a in range(2):
                            tt = t + 2 * u + a
                            tile_ready(tt, 16, r)
                            if not (first and u == 0 and hid0 == 0):
                                dve.wait_ge(hid_lo, hid0 + 8 * r + 2 * u + a - 1)
                            dve.scalar_tensor_tensor(out=u_tmp[:, a, :], in0=ps[tt % 4][:, :], scalar=0.0,
                                                     in1=rstd_f[:, :], op0=ALU.max, op1=ALU.mult)\
                               .then_inc(bank_free[tt % 4], 1)
                    for d in range(4):
                        lo(c + d + 5 + 8 * r, (c + d + 5) % 2)
                        for a in range(2):
                            add_residual(2 * d + a, t + 8 + 2 * d + a, 16, r)
                        if last:
                            for a in range(2):
                                k = 2 * d + a
                                x_lo(dst[:, k, :], h[:, k, :], gname(k), dst_hi[:, k, :], x0 + k)

                one_round(0, True, False)
                with dve.Fori(1, ROUNDS - 1) as r:
                    one_round(r, False, False)
                one_round(ROUNDS - 1, False, True)

            residual("wo_a", xa_lo, xa_hi, gains_of("mlp0"), X["mlp0"])
            mlp("mlp0", 1, xa_lo, xa_hi, gains_of("kv_in"), X["dkv"], 0)
            c, t = C["dkv"], T["dkv"]

            def take_scaled(dst, tt, scale=None):
                tile_ready(tt)
                if scale is None:
                    ins = dve.tensor_tensor(dst, ps[tt % 4][:, :], rstd_f[:, :], ALU.mult)
                else:
                    ins = dve.scalar_tensor_tensor(out=dst, in0=ps[tt % 4][:, :], scalar=scale, in1=rstd_f[:, :],
                                                   op0=ALU.mult, op1=ALU.mult)
                ins.then_inc(bank_free[tt % 4], 1)

            def rope_tables(n_before, scale):
                for j, src in enumerate((cos_t, sin_t)):
                    dve.scalar_tensor_tensor(out=table2[:, j, :], in0=src[:, :], scalar=scale, in1=rstd_f[:, :],
                                             op0=ALU.mult, op1=ALU.mult).then_inc(table_done, 1)
                dve.wait_ge(table_done, n_before + 2)

            lo(c + 1, (c + 1) % 2)
            for k in range(KD):
                x_lo(xb_lo[:, k, :], h[:, k, :], g("attn1", k), xb_hi[:, k, :], X["dq"] + k)
            mean_square(2, D)
            take_rstd(2)
            for a in range(2):
                take_scaled(ckv[:, a, :], t + a)
            lo(c + 2, c % 2)
            for a in range(2):
                x_lo(ckv_lo[:, a, :], ckv[:, a, :], g("kv", a), ckv_hi[:, a, :], X["ckv"] + a)
            rope_tables(4, 1.0)
            rope(t + 2, k_eo[:, 0, :], k_eo[:, 1, :], table2[:, 0, :], table2[:, 1, :], rope_tmp2, 8)
            lo(c + 3, (c + 1) % 2)
            for a in range(2):
                take_scaled(cq_raw[:, a, :], t + 4 + a)
            lo(c + 4, c % 2)
            take_scaled(cq_raw[:, 2, :], t + 6)
            for a in range(3):
                x_lo(cq_lo[:, a, :], cq_raw[:, a, :], g("q", a), cq_hi[:, a, :], X["cq"] + a)
            c, t = C["ukv"], T["ukv"]
            mean_square(3, 256)
            lo(c + 1, (c + 1) % 2)
            take_rstd(3)
            for a in range(8):
                take_scaled(k_nope[:, a, :], t + a)
            mean_square(4, 384)
            lo(c + 2, c % 2)
            take_rstd(4)
            c, t = C["uq"], T["uq"]
            rope_tables(6, -MLA_SCALE)
            lo(c + 1, (c + 1) % 2)
            for j in range(2):
                rope(t + 2 * j, qr_eo[:, 2 * j, :], qr_eo[:, 2 * j + 1, :], table2[:, 0, :], table2[:, 1, :],
                     rope_tmp2, 9 + j)
            for u in range(2):
                lo(c + u + 2, (c + u + 2) % 2)
                for a in range(4):
                    take_scaled(q_nope[:, 4 * u + a, :], t + 4 + 4 * u + a, -MLA_SCALE)

            def mla_min(par, n):
                for i in range(QT):
                    b = ps[(T["mla"] + i) % 4]
                    tile_ready(T["mla"] + i, 4, n)
                    dve.tensor_reduce(negmin[:, par, i:i + 1], b[:, 0:P * (i + 1)], AX.X, ALU.min)\
                       .then_inc(nm_done, 1)

            def mla_inverse(par, n):
                b = (T["mla"] + 3) % 4
                dve.wait_ge(bank_free[b], (T["mla"] + 3) // 4 + 1 + n)
                dve.reciprocal(rinv[:, par, 0:QT], rowsum[:, par, 0:QT]).then_inc(ri_done, 1)

            def mla_normalise(par, n):
                dve.wait_ge(o_done, HEADS + n + 1)
                dve.wait_ge(ri_done, HEADS + n + 1)
                dve.tensor_tensor(mla_o[par][:, :, :], O_PS[:, :].rearrange("p (a b) -> p a b", a=QT),
                                  rinv[:, par, 0:QT].unsqueeze(2).to_broadcast([P, QT, P]), ALU.mult)\
                   .then_inc(on_done, 1)

            def mla_step(par, n, ahead=True, behind=True, far=True):
                if far:
                    head_lo(xa_lo, xa_hi, n - 2, X["mla_o"], 1.0)
                if behind:
                    mla_normalise(1 - par, n - 1)
                if ahead:
                    mla_min(1 - par, n + 1)
                mla_inverse(par, n)

            mla_min(0, 0)
            mla_step(0, 0, behind=False, far=False)
            mla_step(1, 1, far=False)
            with dve.Fori(1, HEADS // 2 - 1) as i:
                mla_step(0, 2 * i)
                mla_step(1, 2 * i + 1)
            mla_step(0, HEADS - 2)
            mla_step(1, HEADS - 1, ahead=False)
            head_lo(xa_lo, xa_hi, HEADS - 2, X["mla_o"], 1.0)
            mla_normalise(1, HEADS - 1)
            head_lo(xa_lo, xa_hi, HEADS - 1, X["mla_o"], 1.0)

            residual("wo_b", xb_lo, xb_hi, gains_of("mlp1"), X["mlp1"])
            mlp("mlp1", 5, xb_lo, xb_hi, lambda k: g_x2[:, k:k + 1], X["w_in"], 8 * ROUNDS)
            c, t = C["w_in"], T["w_in"]
            for j in (1, 2):
                lo(c + j, (c + j) % 2)
            pairs = STAT[:, 0:2 * QT].rearrange("p (q b) -> p q b", b=2)
            dve.wait_ge(stat_done, STATS[6] + 1)
            dve.tensor_scalar(ms_t[:, 24:28], pairs[:, :, 0], 1.0 / D, EPS, ALU.mult, ALU.add).then_inc(ms_done, 1)
            dve.wait_ge(rstd_t_done, 7)
            dve.tensor_tensor(r1_sq[:, :], rstd_t[:, 24:28], rstd_t[:, 24:28], ALU.mult).then_inc(small_done, 1)
            dve.wait_ge(small_done, 1)
            dve.scalar_tensor_tensor(out=r1_ms[:, :], in0=pairs[:, :, 1], scalar=1.0 / D, in1=r1_sq[:, :],
                                     op0=ALU.mult, op1=ALU.mult).then_inc(small_done, 1)
            dve.wait_ge(small_done, 2)
            dve.tensor_scalar(ms_t[:, 28:32], r1_ms[:, :], EPS, None, ALU.add).then_inc(ms_done, 1)
            dve.wait_ge(rstd_t_done, 8)
            dve.tensor_tensor(r12[:, :], rstd_t[:, 24:28], rstd_t[:, 28:32], ALU.mult).then_inc(r12_done, 1)
            take_rstd(6)
            for a in range(2):
                take_scaled(iq[:, a, :], t + a)
            take_rstd(7, r1_f)
            for a in range(2):
                take_scaled(iq[:, 2 + a, :], t + 2 + a)
            lo(c + 3, (c + 1) % 2)
            dve.wait_ge(rows_stored, 16)
            take_scaled(ik_iw[:, :], t + 4)
            dve.wait_ge(nbias_full, 16)
            dve.tensor_tensor(nbias[:, :, P:2 * P], nbias[:, :, P:2 * P],
                              mask[:, :].unsqueeze(1).to_broadcast([P, HEADS, P]), ALU.add).then_inc(nb_masked, 1)
            for a in range(2):
                take_scaled(cq2[:, a, :], t + 5 + a, -HEAD_SCALE)
            dve.wait_ge(iwt_done, 1)
            dve.tensor_scalar(iw[:, :, :].rearrange("p a b -> p (a b)"), STAT[:, 0:IDX_HEADS * QT], IDX_SCALE, None,
                              ALU.mult).then_inc(small_done, 1)
            dve.wait_ge(small_done, 3)
            def index_sum(i):
                row = idx_score[:, IDX_OFF[i]:IDX_OFF[i] + P * (i + 1)]
                for hd in range(IDX_HEADS):
                    j, tt = IDX_HEADS * (i - 1) + hd, T_IDX[i] + hd
                    src = idx_relu[:, j % 2, 0:P * (i + 1)]
                    dve.wait_ge(bank_free[tt % 4], tt // 4 + 1)
                    if hd == 0:
                        dve.tensor_scalar(row, src, iw[:, i, 0:1], None, ALU.mult).then_inc(idx_acc, 1)
                    else:
                        dve.wait_ge(idx_acc, j)
                        dve.scalar_tensor_tensor(out=row, in0=src, scalar=iw[:, i, hd:hd + 1], in1=row,
                                                 op0=ALU.mult, op1=ALU.add).then_inc(idx_acc, 1)
                diag = idx_score[:, IDX_OFF[i] + P * i:IDX_OFF[i] + P * (i + 1)]
                dve.wait_ge(idx_acc, IDX_HEADS * i)
                dve.tensor_tensor(diag, diag, mask[:, :], ALU.subtract).then_inc(diag_done, 1)
                dve.wait_ge(diag_done, i)

            def top_rounds(first, last):
                for n in range(first, last):
                    i, rnd = 1 + n // ROUNDS_TOP, n % ROUNDS_TOP
                    row = idx_score[:, IDX_OFF[i]:IDX_OFF[i] + P * (i + 1)]
                    if n:
                        dve.wait_ge(top_done, 2 * n)
                    dve.max(top8[:, :], row).then_inc(top_done, 1)
                    dve.wait_ge(top_done, 2 * n + 1)
                    dve.match_replace(row, top8[:, :], row, TAKEN).then_inc(top_done, 1)
                    if rnd == ROUNDS_TOP - 1:
                        dve.wait_ge(top_done, 2 * n + 2)
                        dve.tensor_scalar(sel[:, IDX_OFF[i]:IDX_OFF[i] + P * (i + 1)], row, TAKEN / 2, BIG,
                                          ALU.is_gt, ALU.mult).then_inc(sel_done, 1)

            def min2(jb):
                head = NB_HEAD[jb]
                for i in range(QT):
                    tt, j = T_JOB[jb] + i, 4 * jb + i
                    b, w0 = ps[tt % 4], P * max(i - 1, 0)
                    tile_ready(tt)
                    dve.tensor_tensor(b[:, w0:P * (i + 1)], b[:, w0:P * (i + 1)],
                                      nbias[:, head, 2 * P - (P * (i + 1) - w0):2 * P], ALU.add).then_inc(mask_done, 1)
                    dve.wait_ge(mask_done, j + 1)
                    dve.tensor_reduce(negmin[:, jb % 2, i:i + 1], b[:, 0:P * (i + 1)], AX.X, ALU.min)\
                       .then_inc(nm_done, 1)

            def inverse2(jb):
                tt = T_JOB[jb] + 3
                dve.wait_ge(bank_free[tt % 4], tt // 4 + 1)
                dve.reciprocal(rinv[:, jb % 2, 0:QT], rowsum[:, jb % 2, 0:QT]).then_inc(ri_done, 1)

            def normalise2(jb):
                dve.wait_ge(o_done, 2 * HEADS + jb + 1)
                dve.wait_ge(ri_done, 2 * HEADS + jb + 1)
                pair = jb // 2
                if jb % 2 == 0 and pair >= 2:
                    dve.wait_ge(ot_done, 2 * HEADS + pair - 1)
                dve.tensor_tensor(o2[pair % 2][:, :, 64 * (jb % 2):64 * (jb % 2) + 64],
                                  O_PS[:, 0:256].rearrange("p (a b) -> p a b", a=QT),
                                  rinv[:, jb % 2, 0:QT].unsqueeze(2).to_broadcast([P, QT, 64]), ALU.mult)\
                   .then_inc(on_done, 1)

            def mix_lo(n, src, scale):
                x_lo(xa_lo[:, n, :], src, scale, xa_hi[:, n, :], X["mix"] + n)

            def convolve(a):
                x, y = conv_in[:, a, :], conv_y[:, a, :]
                dve.wait_ge(conv_x, a + 1)
                dve.tensor_scalar(y, x, g("conv", 4 + a), None, ALU.mult).then_inc(conv_step, 1)
                for tap in (1, 2):
                    dve.wait_ge(conv_step, 3 * a + tap)
                    dve.scalar_tensor_tensor(out=y[:, tap:S], in0=x[:, 0:S - tap],
                                             scalar=g("conv", 2 * (2 - tap) + a), in1=y[:, tap:S],
                                             op0=ALU.mult, op1=ALU.add).then_inc(conv_step, 1)

            def pool_mean(j):
                a, rows, src, w = POOL_GROUPS[j]
                s_ = pool_s[src]
                dve.wait_ge(pool_s_done, POOL_STEPS[j])
                dve.tensor_tensor(s_[rows, PAD:2 * PAD], s_[rows, PAD:2 * PAD], pool_fix[rows, a, :], ALU.mult)\
                    .then_inc(pool_fix_done, 1)
                dve.wait_ge(pool_fix_done, j + 1)
                dve.scalar_tensor_tensor(out=pool_d[rows, a, :], in0=s_[rows, PAD:PAD + S], scalar=1.0 / w,
                                         in1=pool_v[rows, a, PAD:PAD + S], op0=ALU.mult, op1=ALU.subtract)\
                    .then_inc(pool_d_done, 1)

            n_rounds = ROUNDS_TOP * (QT - 1)
            top_at = [0, 10, 20, 28, 34, 40, 43, 46, n_rounds]
            index_sum(1)
            top_rounds(top_at[0], top_at[1])
            for a in range(2):
                take_scaled(ck2[:, a, :], T_CK + a)
            index_sum(2)
            top_rounds(top_at[1], top_at[2])
            index_sum(3)
            top_rounds(top_at[2], top_at[3])
            for a in range(2):
                take_scaled(dq2[:, a, :], T_DQ + a, -HEAD_SCALE)
            dve.wait_ge(nb_masked, 1)
            top_rounds(top_at[3], top_at[4])
            for a in range(2):
                take_scaled(dk2[:, a, :], T_DK + a)
            min2(0)
            top_rounds(top_at[4], top_at[5])
            c = C["att2"]
            for jb in range(8):
                a = jb % 2
                inverse2(jb)
                if jb < 7:
                    min2(jb + 1)
                normalise2(jb)
                if jb < 3:
                    top_rounds(top_at[5 + jb], top_at[6 + jb])
                elif jb in (4, 5):
                    convolve(a)
                elif jb == 6:
                    for j in range(4):
                        pool_mean(j)
                if jb % 2 == 0 and jb:
                    if jb == 2:
                        dve.wait_ge(wlo_done, POOL_LO[1])
                    lo(c + jb // 2 + 1, (c + jb // 2 + 1) % 2)
                if jb >= 2 and jb % 2 == 0:
                    mix_lo(MIX_PAIR[(jb - 2) // 2], OT[:, :], 1.0)
                if jb < 2:
                    take_scaled(conv_in[:, a, :], T_PROJ[jb])
                elif jb < 4:
                    take_scaled(conv_gate[:, a, :], T_PROJ[jb])
                elif jb < 6:
                    take_scaled(pool_v[:, a, PAD:PAD + S], T_PROJ[jb])
                    if jb == 4:
                        dve.memset(pool_v[:, :, 0:PAD], 0.0).then_inc(pool_zero, 1)
                elif jb == 6:
                    take_scaled(conv_gate[:, 0, :], T_PROJ[jb])
            for a in range(2):
                mix_lo(MIX_POOL[a], ps[(T_POOL + a) % 4][:, :], g("pool_scale", a))
                dve.wait_ge(xl_done, X["mix"] + MIX_POOL[a] + 1)
                dve.sem_inc(bank_free[(T_POOL + a) % 4], 1)
            take_scaled(conv_gate[:, 1, :], T_PROJ[7])
            mix_lo(MIX_CONV[0], conv_y[:, 0, :], 1.0)
            mix_lo(MIX_PAIR[3], OT[:, :], 1.0)
            mix_lo(MIX_CONV[1], conv_y[:, 1, :], 1.0)
            for k in range(KD):
                ins = dve.scalar_tensor_tensor(out=h[:, k, :], in0=h[:, k, :], scalar=g("final", k), in1=r1_f[:, :],
                                               op0=ALU.mult, op1=ALU.mult)
            ins.then_inc(x2_done, 1)

            c, t = C["w_out"], T["w_out"]
            for u in range(4):
                lo(c + u + 1, (c + u + 1) % 2)
            for a in range(2):
                x_lo(p_lo[:, a, :], p_raw[:, a, :], 1.0, p_hi[:, a, :], X["p"] + a)

            def onto_residual(n, gname, gnext, x0, n0, c_next):
                mean_square(n, D)
                lo(c_next, c_next % 2)
                dve.wait_ge(bc_done, n + 1)

                def add(k):
                    dve.wait_ge(branch_done, KD * n0 + k + 1)
                    dve.tensor_tensor(h[:, k, :], h[:, k, :], branch[:, k, :], ALU.add).then_inc(res_dve, 1)

                for k in range(KD):
                    dve.scalar_tensor_tensor(out=branch[:, k, :], in0=branch[:, k, :], scalar=g(gname, k),
                                             in1=BC[:, :], op0=ALU.mult, op1=ALU.mult).then_inc(branch_done, 1)
                    if k in (0, 2, 7):
                        add(k)
                    elif k == 5:
                        add(4)
                for k in range(KD):
                    x_lo(xb_lo[:, k, :], h[:, k, :], g(gnext, k), xb_hi[:, k, :], x0 + k)

            dve.wait_ge(x2_done, 1)
            onto_residual(8, "mix_post", "ffn_pre", X["ffn"], 0, C["proj0"] + 1)

            def gate_up(r, n, first):
                c, t = C[f"gu{r}"], T[f"gu{r}"]

                def pair(i):
                    for s in range(2):
                        j = HID2 + 8 * r + 2 * i + s
                        if not (first and isinstance(i, int) and s == 1):
                            lo(c + s + 1 + 2 * i, (c + s + 1) % 2)
                        if first and isinstance(i, int) and s == 0:
                            lo(c + 2, c % 2)
                            mean_square(9, D)
                            take_rstd(9)
                        tt = t + 2 * s
                        tile_ready(tt, 4, i)
                        if not (first and isinstance(i, int)):
                            dve.wait_ge(hid_sq, j - 1)
                        dve.tensor_tensor(gate_t[:, s, :], ps[tt % 4][:, :], rstd_f[:, :], ALU.mult)\
                            .then_inc(bank_free[tt % 4], 1)
                        tile_ready(tt + 1, 4, i)
                        dve.tensor_tensor(up_t[:, s, :], ps[(tt + 1) % 4][:, :], rstd_f[:, :], ALU.mult)\
                            .then_inc(bank_free[(tt + 1) % 4], 1)

                pair(0)
                with dve.Fori(1, n // 2) as i:
                    pair(i)

            def down(r):
                c, t = C[f"dn{r}"], T[f"dn{r}"]
                for u in range(4):
                    lo(c + u + 1, (c + u + 1) % 2)
                    for a in range(2):
                        k, tt = 2 * u + a, t + 2 * u + a
                        if r == 0:
                            continue
                        tile_ready(tt)
                        if r == 1:
                            b0 = T["dn0"] + k
                            dve.wait_ge(bank_free[b0 % 4], b0 // 4 + 1)
                        dve.tensor_tensor(branch[:, k, :], ps[tt % 4][:, :], branch[:, k, :], ALU.add)\
                            .then_inc(bank_free[tt % 4], 1)

            for r, n in enumerate(GU_TILES):
                gate_up(r, n, r == 0)
                down(r)
            onto_residual(10, "ffn_post", "ple", X["ple"], 1, C["proj1"] + 1)

            c, t = C["ple"], T["ple"]

            def add_gated(k):
                dve.wait_ge(gated_done, k + 1)
                dve.tensor_tensor(h[:, k, :], h[:, k, :], projected[:, k, :], ALU.add).then_inc(y_done, 1)

            for j in (1, 2):
                lo(c + j, (c + j) % 2)
            mean_square(11, D)
            take_rstd(11)
            for u in range(4):
                for a in range(2):
                    k, tt = 2 * u + a, t + 2 * u + a
                    tile_ready(tt)
                    if u:
                        dve.wait_ge(silu_done, N_SILU + k - 1)
                    dve.tensor_tensor(gate_t[:, a, :], ps[tt % 4][:, :], rstd_f[:, :], ALU.mult)\
                        .then_inc(bank_free[tt % 4], 1)
                if u == 1:
                    lo(c + 3, (c + 3) % 2)
                if u:
                    for a in range(2):
                        add_gated(2 * u - 2 + a)
            for k in (KD - 2, KD - 1):
                dve.wait_ge(silu_done, N_SILU + k + 1)
                dve.tensor_tensor(projected[:, k, :], projected[:, k, :], silu_t[:, k % 2, :], ALU.mult)\
                    .then_inc(gated_done, 1)
                add_gated(k)

        @block.gpsimd
        def _(pool):
            def square_tile(src, k, n):
                if k == 0:
                    pool.tensor_tensor(ssq[:, :], src, src, ALU.mult).then_inc(sq_done, 1)
                else:
                    if k >= 2:
                        pool.wait_ge(ssq_done, SSQ[n] + k - 1)
                    pool.tensor_tensor(sq_tmp[:, :], src, src, ALU.mult).then_inc(sq_done, 1)
                    pool.wait_ge(sq_done, SQ[n] + k + 1)
                    pool.tensor_tensor(ssq[:, :], ssq[:, :], sq_tmp[:, :], ALU.add).then_inc(ssq_done, 1)

            def rstd(n):
                pool.wait_ge(ms_done, n + 1)
                pool.tensor_tensor(rstd_t[:, 4 * n:4 * n + 4], ms_t[:, 4 * n:4 * n + 4], half_neg[:, :], ALU.pow).then_inc(rstd_t_done, 1)

            def add_squares(squares, n):
                for k in range(1, KD):
                    pool.wait_ge(sq_done, SQ[n] + k + 1)
                    if k >= 2:
                        pool.wait_ge(ssq_done, SSQ[n] + k - 1)
                    pool.tensor_tensor(ssq[:, :], squares[:, 0, :] if k == 1 else ssq[:, :], squares[:, k, :],
                                       ALU.add).then_inc(ssq_done, 1)
                rstd(n)

            pool.wait_ge(dve_const, 1)
            add_squares(squares0, 0)

            def rope(t, dst1, dst2, rope_tmp, per=0, i=0):
                b = (t + 1) % 4
                pool.wait_ge(bank_free[b], (t + 1) // 4 + 1 + (per // 4) * i)
                pool.tensor_tensor(dst1, dst1, rope_tmp[:, 0, :], ALU.subtract)
                pool.tensor_tensor(dst2, dst2, rope_tmp[:, 1, :], ALU.add).then_inc(rope_done, 1)

            with pool.Fori(0, 4) as i:
                for s in range(2):
                    rope(T["qk"] + 2 * s, qk[:, 0, s, i, :], qk[:, 1, s, i, :], rope_tmp, 4, i)

            def diff_norm(par, n):
                pool.wait_ge(oc_done, n + 1)
                o = o_raw[par][:, :, :].rearrange("p a b -> p (a b)")
                pool.tensor_tensor(o_sq[:, :], o, o, ALU.mult).then_inc(sqo_done, 1)
                pool.wait_ge(oms_done, n + 1)
                pool.tensor_tensor(o_rstd[:, :], o_ms[:, :], half_neg[:, :], ALU.pow).then_inc(orstd_done, 1)
                pool.wait_ge(orstd_done, n + 1)
                pool.tensor_tensor(o_raw[par][:, :, :], o_raw[par][:, :, :],
                                   o_rstd[:, :].unsqueeze(2).to_broadcast([P, QT, P]), ALU.mult).then_inc(on_done, 1)

            with pool.Fori(0, HEADS // 2) as half:
                for par in range(2):
                    diff_norm(par, 2 * half + par)

            def norm_tiles(t, n):
                for k in range(KD):
                    pool.wait_ge(bank_free[(t + k) % 4], (t + k) // 4 + 1)
                    square_tile(h[:, k, :], k, n)
                rstd(n)

            def hidden(t, hhi, hlo, hid0, r):
                for j in range(KD):
                    a = j % 2
                    tt = t + j
                    pool.wait_ge(bank_free[tt % 4], tt // 4 + 1 + 4 * r)
                    pool.tensor_tensor(u_sq[:, a, :], u_tmp[:, a, :], u_tmp[:, a, :], ALU.mult).then_inc(hid_sq, 1)
                    pool.wait_ge(hid_sq, hid0 + 8 * r + j + 1)
                    pool.wait_ge(hid_hi, hid0 + 8 * r + j + 1)
                    pool.tensor_tensor(hlo[:, j, :], u_sq[:, a, :], hhi[:, j, :].bitcast(F32), ALU.subtract)\
                        .then_inc(hid_lo, 1)

            norm_tiles(T["wo_a"], 1)
            with pool.Fori(0, ROUNDS) as r:
                hidden(T["mlp0"], xb_hi, xb_lo, 0, r)
            norm_tiles(T["mlp0"] + 56, 2)
            t = T["dkv"]
            for a in range(2):
                pool.wait_ge(bank_free[(t + a) % 4], (t + a) // 4 + 1)
                square_tile(ckv[:, a, :], a, 3)
            rope(t + 2, k_eo[:, 0, :], k_eo[:, 1, :], rope_tmp2)
            rstd(3)
            for a in range(3):
                pool.wait_ge(bank_free[(t + 4 + a) % 4], (t + 4 + a) // 4 + 1)
                square_tile(cq_raw[:, a, :], a, 4)
            rstd(4)
            for j in range(2):
                rope(T["uq"] + 2 * j, qr_eo[:, 2 * j, :], qr_eo[:, 2 * j + 1, :], rope_tmp2)
            norm_tiles(T["wo_b"], 5)
            with pool.Fori(0, ROUNDS) as r:
                hidden(T["mlp1"], xa_hi, xa_lo, 8 * ROUNDS, r)
            for k in range(1, KD):
                pool.wait_ge(sq_done, SQ[6] + 2 * k + 2)
                if k >= 2:
                    pool.wait_ge(ssq_done, SSQ[6] + 2 * k - 2)
                for sums, src in ((ssq, squares), (sq_tmp, squares_g)):
                    pool.tensor_tensor(sums[:, :], src[:, 0, :] if k == 1 else sums[:, :], src[:, k, :],
                                       ALU.add).then_inc(ssq_done, 1)
            rstd(6)
            rstd(7)

            for c in range(*POOL_LO):
                if c == POOL_LO[0]:
                    pool.wait_ge(wlo_done, c)
                pool.wait_ge(whi_done, c + 1)
                pool.tensor_tensor(wlo[c % 2][:, :], raw[c % 2][:, :], whi[c % 2][:, :].bitcast(F32),
                                   ALU.subtract).then_inc(wlo_done, 1)

            def window(dst, src, shift, low):
                pool.tensor_tensor(dst[:, low:PAD + S], src[:, low:PAD + S], src[:, low - shift:PAD + S - shift],
                                   ALU.add).then_inc(pool_s_done, 1)

            for a in range(2):
                tt = T_PROJ[2 + a]
                pool.wait_ge(bank_free[tt % 4], tt // 4 + 1)
                pool.tensor_tensor(conv_in[:, a, :], conv_in[:, a, :], conv_gate[:, a, :], ALU.mult).then_inc(conv_x, 1)
            pool.wait_ge(pool_zero, 1)
            steps = 0
            for a, windows in ((0, ((0, 1, 1), (1, 2, 3))), (1, ((2, 1, 1), (3, 2, 3), (2, 4, 7), (3, 8, 15)))):
                tt = T_PROJ[4 + a]
                pool.wait_ge(bank_free[tt % 4], tt // 4 + 1)
                src = pool_v[:, a, :]
                for dst, shift, low in windows:
                    if steps:
                        pool.wait_ge(pool_s_done, steps)
                    window(pool_s[dst], src, shift, low)
                    src = pool_s[dst]
                    steps += 1
            for a in range(2):
                tt = T_PROJ[6 + a]
                pool.wait_ge(bank_free[tt % 4], tt // 4 + 1)
                pool.wait_ge(conv_step, 3 * (a + 1))
                pool.tensor_tensor(conv_y[:, a, :], conv_y[:, a, :], conv_gate[:, a, :], ALU.mult).then_inc(conv_out, 1)

            def onto_residual(n0, n):
                for k in RES_POOL:
                    pool.wait_ge(branch_done, KD * n0 + k + 1)
                    pool.tensor_tensor(h[:, k, :], h[:, k, :], branch[:, k, :], ALU.add).then_inc(res_pool, 1)
                add_squares(squares2, n)

            add_squares(squares2, 8)
            onto_residual(0, 9)

            def gate_up(r, n):
                t = T[f"gu{r}"]

                def pair(i):
                    for s in range(2):
                        j = HID2 + 8 * r + 2 * i + s
                        tt = t + 2 * s + 1
                        pool.wait_ge(bank_free[tt % 4], tt // 4 + 1 + i)
                        pool.wait_ge(silu_done, j - HID2 + 1)
                        pool.wait_ge(hid_lo, j - 1)
                        pool.tensor_tensor(hid_t[:, s, :], silu_t[:, s, :], up_t[:, s, :], ALU.mult).then_inc(hid_sq, 1)
                        pool.wait_ge(hid_sq, j + 1)
                        pool.wait_ge(hid_hi, j + 1)
                        pool.tensor_tensor(xa_lo[:, 2 * i + s, :], hid_t[:, s, :],
                                           xa_hi[:, 2 * i + s, :].bitcast(F32), ALU.subtract).then_inc(hid_lo, 1)

                with pool.Fori(0, n // 2) as i:
                    pair(i)

            for r, n in enumerate(GU_TILES):
                gate_up(r, n)
            add_squares(squares2, 10)
            onto_residual(1, 11)

            for k in range(KD - 2):
                pool.wait_ge(silu_done, N_SILU + k + 1)
                pool.tensor_tensor(projected[:, k, :], projected[:, k, :], silu_t[:, k % 2, :], ALU.mult)\
                    .then_inc(gated_done, 1)


def pack_weights(inp):
    chunks = []

    def put(w, cols, k_tiles=KD):
        a = w[:, cols].reshape(k_tiles, P, len(cols)).transpose(1, 0, 2).reshape(P, -1)
        full = np.zeros((P, CHUNK), a.dtype)
        full[:, :a.shape[1]] = a
        chunks.append(full)

    def put_all(w, width=256):
        for n in range(0, w.shape[1], width):
            put(w, np.arange(n, n + width), w.shape[0] // P)

    def put_mlp(up, down):
        for r in range(ROUNDS):
            put_all(up[:, r * D:(r + 1) * D])
            put_all(down[r * D:(r + 1) * D])

    w = inp["w_qkv_a"][0]
    for j in range(4):
        for part in range(2):
            cols = [part * D + 64 * (4 * j + comp) + 32 * half + r
                    for half in range(2) for comp in range(4) for r in range(32)]
            put(w, np.array(cols))
    put_all(w[:, 2 * D:])
    put_all(inp["w_o_a"][0])
    put_mlp(inp["w_up"][0], inp["w_down"][0])
    dkv, ukv, dq, uq = inp["w_dkv"], inp["w_ukv"], inp["w_dq"][0], inp["w_uq"][0]
    put(dkv, np.arange(256))
    put(dkv, np.concatenate([np.tile(np.arange(256 + 32 * half, 288 + 32 * half), 4) for half in range(2)]))
    put(dq, np.arange(256))
    put(dq, np.concatenate([np.arange(256, 384)] * 2))
    heads = np.arange(HEADS)[:, None]
    for part in range(2):
        put(ukv, (256 * heads + 128 * part + np.arange(128)).ravel(), 2)
    put(uq, np.concatenate([(192 * heads[4 * j:4 * j + 4] + 128 + 32 * half + np.arange(32)).ravel()
                            for j in range(2) for half in range(2)]), 3)
    for part in range(2):
        put(uq, (192 * heads[4 * part:4 * part + 4] + np.arange(128)).ravel(), 3)
    put_all(inp["w_o_b"][0])
    put_mlp(inp["w_up"][1], inp["w_down"][1])
    w = inp["w_in_2"][0]
    at = dict(a_in=0, a_c=256, a_b=512, pv=768, cq=1024, ck=1280, cv=1536, iq=1792, ik=2304, iw=2368, dq=2376, dk=2632, dv=2888)
    put_all(w[:, at["iq"]:at["iq"] + 512])
    put(w, np.concatenate([at["ik"] + np.arange(64), at["iw"] + np.arange(IDX_HEADS), np.full(256 - 64 - IDX_HEADS, at["ik"])]))
    for name in ("cq", "ck", "cv", "dq", "dk", "dv", "a_in", "a_c", "pv", "a_b"):
        put(w, at[name] + np.arange(256))
    wo = inp["w_out_2"][0].reshape(KD, P, D)
    order = np.zeros(KD, int)
    for tiles, first in ((MIX_CONV, 0), (MIX_POOL, 2), (MIX_PAIR[2:], 4), (MIX_PAIR[:2], 6)):
        order[list(tiles)] = first, first + 1
    put_all(wo[order].reshape(D, D))
    proj, gate_up, down = inp["w_ple_proj_2"][0], inp["w_gate_up_2"][0], inp["w_down_2"][0]
    put(proj, np.arange(512), 2)
    tile0 = 0
    for n in GU_TILES:
        for j in range(tile0, tile0 + n):
            put(gate_up, np.concatenate([j * P + np.arange(P), down.shape[0] + j * P + np.arange(P)]))
        put_all(down[tile0 * P:(tile0 + n) * P])
        tile0 += n
    put(proj, 512 + np.arange(512), 2)
    put_all(inp["w_ple_gate_2"][0])
    assert len(chunks) == N_CHUNKS
    return np.stack(chunks)


def pack_gains(inp):
    vectors = [inp["attn_norm_g"][0], inp["attn_norm_g"][1], inp["kv_in_norm_g"], inp["mlp_norm_g"][0],
               inp["mlp_norm_g"][1], inp["final_norm_g"], inp["g_mix_pre_2"][0], inp["g_mix_post_2"][0],
               inp["g_ffn_pre_2"][0], inp["g_ffn_post_2"][0], inp["g_ple_2"][0], inp["kv_norm_g"],
               inp["q_norm_g"][0], inp["subln_g"][0], inp["pool_scale_2"][0], inp["conv_w_2"][0].reshape(-1)]
    return np.ascontiguousarray(np.concatenate([v.reshape(-1, P) for v in vectors]).T)


def rope_tables():
    inv_freq = np.float32(10000.0) ** (-np.arange(0, 64, 2, dtype=np.float32) / np.float32(64))
    ang = inv_freq[:, None] * np.arange(S, dtype=np.float32)[None, :]
    return np.tile(np.cos(ang), (4, 1)).astype(np.float32), np.tile(np.sin(ang), (4, 1)).astype(np.float32)


def distance_buckets():
    dist = np.maximum(2 * P - 1 - np.arange(ROWS), 0)
    exact = BUCKETS // 2
    large = exact + (np.log(np.maximum(dist, 1).astype(np.float32) / np.float32(exact))
                     / np.float32(np.log(MAX_DIST / exact)) * np.float32(BUCKETS - exact)).astype(np.int32)
    bucket = np.where(dist < exact, dist, np.minimum(large, BUCKETS - 1))
    eye = np.eye(BUCKETS, dtype=np.float32)
    out = eye[:, BUCKETS - 1:] - eye[:, bucket]
    out[:, 2 * P:] = 0.0
    return np.ascontiguousarray(out)


def pool_counts():
    out = np.ones((P, 2, PAD), np.float32)
    for a, rows, _, w in POOL_GROUPS:
        out[rows, a, :] = w / np.minimum(np.arange(PAD) + 1, w)
    return out.reshape(P, -1)


def pool_blocks(w):
    out = np.zeros((P, 2, P), w.dtype)
    for j in range(4):
        rows = slice(64 * (j % 2), 64 * (j % 2) + 64)
        out[rows, j // 2, rows] = w[j]
    return out.reshape(P, -1)


def lay_out(inp):
    cos, sin = rope_tables()
    return {
        "pT_in": np.ascontiguousarray(inp["p_2"][0, 0].T), "tab_in": np.ascontiguousarray(inp["rel_bias_2"].T),
        "buckets_in": distance_buckets(), "pool_w_in": pool_blocks(inp["pool_w_2"][0]), "pool_fix_in": pool_counts(),
        "wst": pack_weights(inp), "xT": np.ascontiguousarray(inp["x"][0].T), "gains": pack_gains(inp),
        "cos": cos, "sin": sin, "ident_in": np.eye(P, dtype=np.float32),
        "mask_in": np.triu(np.full((P, P), BIG, np.float32), 1),
        "lam": np.concatenate([inp["lambda_q1"], inp["lambda_k1"], inp["lambda_q2"], inp["lambda_k2"]], 1),
    }


def kernel(**inputs):
    from concourse import bacc
    from concourse.bass_utils import run_bass_kernel_spmd

    nc = bacc.Bacc("TRN2", target_bir_lowering=False, num_devices=1)
    arrays = lay_out({name: np.asarray(a) for name, a in inputs.items()})
    args = {name: nc.dram_tensor(name, a.shape, mybir.dt.from_np(a.dtype), kind="ExternalInput").ap()
            for name, a in arrays.items()}
    out = nc.dram_tensor("outT", (D, S), F32, kind="ExternalOutput").ap()
    build(nc, outT=out, **args)
    result = run_bass_kernel_spmd(nc, [arrays], core_ids=[0])
    return np.ascontiguousarray(result.results[0]["outT"].T)[None]
```

```python
from contextlib import ExitStack

import numpy as np

import concourse.bass as bass
from concourse import mybir

F32 = mybir.dt.float32
F32R = mybir.dt.float32r
BF16 = mybir.dt.bfloat16
ALU = mybir.AluOpType
ACT = mybir.ActivationFunctionType
AX = mybir.AxisListType

P = 128
S = 512
QT = S // P
D = 1024
KD = D // P
CHUNK = 2048
HEADS = 8
FF = 4096
ROUNDS = FF // D
EPS = 1e-6
SUBLN_EPS = 1e-5
LAMBDA_INIT = 0.8 - 0.6
DIFF_SCALE = 64 ** -0.5
MLA_SCALE = (128 + 64) ** -0.5
BIG = 1e30

GAINS = {}


def _gain_columns():
    at = 0
    for name, n in (("attn0", 8), ("attn1", 8), ("kv_in", 8), ("mlp0", 8), ("mlp1", 8), ("final", 8),
                    ("mix_pre", 8), ("mix_post", 8), ("ffn_pre", 8), ("ffn_post", 8), ("ple", 8),
                    ("kv", 2), ("q", 3), ("subln", 1), ("pool_scale", 2), ("conv", 6)):
        GAINS[name] = (at, n)
        at += n
    return at


N_GAINS = _gain_columns()

STAGES = (
    ("qk", 8, 16), ("v", 4, 8), ("diff", 0, 64), ("wo_a", 4, 8), ("mlp0", 32, 64),
          ("dkv", 4, 7), ("ukv", 2, 16), ("uq", 3, 12), ("mla", 0, 32), ("wo_b", 4, 8), ("mlp1", 32, 64),
          ("w_in", 4, 7), ("w_in2", 5, 38), ("att2", 4, 38),
          ("w_out", 4, 8), ("proj0", 1, 4), ("gu0", 8, 16), ("dn0", 4, 8), ("gu1", 8, 16), ("dn1", 4, 8),
          ("gu2", 6, 12), ("dn2", 4, 8), ("proj1", 1, 4), ("ple", 4, 8), ("end2", 0, 0))
C, T = {}, {}


def _plan():
    c = t = 0
    for name, n_chunks, n_tiles in STAGES:
        C[name], T[name] = c, t
        c, t = c + n_chunks, t + n_tiles
    return c, t


N_CHUNKS, N_TILES = _plan()

SQUARED = (8, 8, 8, 2, 3, 8, 16, 0, 8, 8, 8, 8)
ADDED = (7, 7, 7, 1, 2, 7, 14, 0, 7, 7, 7, 7)
N_NORMS = len(SQUARED)
SQ = [sum(SQUARED[:n]) for n in range(N_NORMS + 1)]
SSQ = [sum(ADDED[:n]) for n in range(N_NORMS + 1)]
STATS = [n if n < 7 else n - 1 for n in range(N_NORMS)]

IDX_HEADS, TOPK = 8, 128
IDX_SCALE = IDX_HEADS ** -0.5 * 64 ** -0.5
HEAD_SCALE = 64 ** -0.5
ROUNDS_TOP = TOPK // 8
TAKEN = -3e38
IDX_OFF = [0, 0, 2 * P, 5 * P]
BUCKETS, MAX_DIST = 32, 128
ROWS = 3 * P
PAD = 16
GU_TILES = (8, 8, 6)
HID2 = 2 * 8 * ROUNDS
N_SILU = sum(GU_TILES)
Q_LO, Q_HI, K_HI, K_LO = range(4)
WARM = 18
FIRST, SECOND = slice(0, KD // 2 * 256), slice(KD // 2 * 256, KD * 256)
RES_DVE, RES_POOL = (0, 2, 4, 7), (1, 3, 5, 6)
POOL_GROUPS = ((0, slice(0, 64), 0, 2), (0, slice(64, 128), 1, 4), (1, slice(0, 64), 2, 8), (1, slice(64, 128), 3, 16))
POOL_STEPS = (2, 2, 6, 6)
T_IDX = [None] + [T["w_in2"] + 10 * j for j in range(3)]
T_CK, T_CV, T_DQ, T_DK, T_DV = (T["w_in2"] + j for j in (8, 18, 28, 30, 36))
T_JOB = [T["w_in2"] + 32 if j == 0 else T["att2"] + 5 * (j - 1) for j in range(8)]
T_PROJ = [T["att2"] + 5 * j + 4 if j < 7 else T["att2"] + 37 for j in range(8)]
T_POOL = T["att2"] + 35
Q_TILES = [(T_DQ + a, T_DK + a) for a in range(2)] + [(T["w_in"] + 5 + a, T_CK + a) for a in range(2)]
V_TILES = ([T_DV, T_DV + 1], [T_CV, T_CV + 1])
POOL_LO = (C["w_in2"], C["att2"] + 2)
MIX_PAIR, MIX_POOL, MIX_CONV = (0, 1, 2, 6), (3, 4), (5, 7)
NB_HEAD = (4, 5, 6, 7, 0, 1, 2, 3)

OFF = [P * i * (i + 1) // 2 for i in range(QT)]
ROWLEN = P * QT * (QT + 1) // 2
TR_ORDER = (1, 0, 2, 3)
TR_BANK = (1, 3, 3, 4)


def build(nc, wst, xT, gains, cos, sin, ident_in, mask_in, lam, pT_in, tab_in, buckets_in, pool_w_in, pool_fix_in, outT):
    ctx = ExitStack()
    with ctx:
        def sem(name):
            return ctx.enter_context(nc.semaphore(name))

        base = [(nc.sbuf_base + 31) // 32 * 32]
        top = nc.sbuf_usable_end

        def at(name, shape, dt, offset):
            return nc.alloc_sbuf_tensor_at(name, shape, dt, offset=offset)

        def sb(name, shape, dt=F32):
            n = (2 if dt == BF16 else 4) * int(np.prod(shape[1:]))
            t = at(name, shape, dt, base[0])
            base[0] += (n + 31) // 32 * 32
            assert base[0] <= top, (name, base[0], top)
            return t

        h = sb("h", [P, KD, S])
        raw = [sb(f"raw{s}", [P, CHUNK]) for s in range(2)]
        whi = [sb(f"whi{s}", [P, CHUNK], F32R) for s in range(2)]
        wlo = [sb(f"wlo{s}", [P, CHUNK], F32R) for s in range(2)]
        xa_at = base[0]
        xa_hi, xa_lo = sb("xa_hi", [P, KD, S], F32R), sb("xa_lo", [P, KD, S], F32R)
        xb_at = base[0]
        xb = sb("xb", [P, KD, 2, S], F32R)
        xb_hi, xb_lo = xb[:, :, 0, :], xb[:, :, 1, :]
        cos_t, sin_t = sb("cos_t", [P, S]), sb("sin_t", [P, S])
        rstd_f = sb("rstd_f", [P, S])
        sq_at = base[0]
        sq_tmp, ssq = sb("sq_tmp", [P, S]), sb("ssq", [P, S])
        gain = sb("gain", [P, N_GAINS])
        ident = sb("ident", [P, P])
        mask = sb("mask", [P, P])
        ident_b, mask_b = sb("ident_b", [P, P], BF16), sb("mask_b", [P, P], BF16)
        ones = sb("ones", [P, 1])
        ms_t, rstd_t = sb("ms_t", [P, QT * N_NORMS]), sb("rstd_t", [P, QT * N_NORMS])
        r1_sq, r1_ms, r12 = (sb(n, [P, QT]) for n in ("r1_sq", "r1_ms", "r12"))
        tab = sb("tab", [P, HEADS])
        iw = sb("iw", [P, QT, IDX_HEADS])
        top8 = sb("top8", [P, 8])
        pool_fix = sb("pool_fix", [P, 2, PAD])
        g_x2 = sb("g_x2", [P, KD])
        half_neg = sb("half_neg", [P, QT])
        lam_ab = sb("lam_ab", [P, 4])
        neg_lam = sb("neg_lam", [P, 1])
        gsub = sb("gsub", [P, 1])
        negmin = sb("negmin", [P, 2, 8])
        rowsum, rinv = sb("rowsum", [P, 2, 8]), sb("rinv", [P, 2, QT])
        coef2, eps_o = sb("coef2", [P, 2, QT]), sb("eps_o", [P, HEADS, QT])
        o_ss, o_ms, o_rstd = (sb(n, [P, QT]) for n in ("o_ss", "o_ms", "o_rstd"))
        G = base[0]
        K = 1024

        qk_split = [at(f"qk_split{hf}", [P, 4, 4, S], F32R, (xb_at, G)[hf]) for hf in range(2)]
        qk_raw = [at(f"qk_raw{hf}", [P, 4, 4, S], F32, (xb_at, G)[hf]) for hf in range(2)]
        v_tok = at("v_tok", [P, QT, D], F32, G + 32 * K)
        stage = [at(f"stage{s}", [P, 2, 2, S], F32R, G + 48 * K + 8 * K * s) for s in range(2)]
        stage_k_lo = [at(f"stage_k_lo{s}", [P, S], F32R, (G + 64 * K, sq_at + 2 * K)[s]) for s in range(2)]
        probs = [at(f"probs{s}", [P, 2, ROWLEN], F32, xa_at + 10 * K * s) for s in range(2)]
        pT = [at(f"pT{s}", [P, ROWLEN], F32, xa_at + 20 * K + 5 * K * s) for s in range(2)]
        cq, sq_, ck, sk = (at(n, [P, S], F32, G + 32 * K + 2 * K * j) for j, n in enumerate(("cq", "sq_", "ck", "sk")))
        rope_tmp = at("rope_tmp", [P, 2, S], F32, G + 40 * K)
        o_raw = [at(f"o_raw{s}", [P, QT, P], F32, G + 2 * K * s) for s in range(2)]
        o_sq = sq_tmp
        zeros = at("zeros", [P, P], F32, G + 48 * K)
        lam_in = at("lam_in", [P, 4, 64], F32, G)
        bias_rows = at("bias_rows", [P, ROWS], F32, G + 8 * K)
        buckets = at("buckets", [P, ROWS], F32, G + 20 * K)
        squares0 = at("squares0", [P, KD, S], F32, xb_at + 16 * K)
        iq = at("iq", [P, 4, S], F32, G)
        ik_iw = at("ik_iw", [P, S], F32, G + 8 * K)
        idx_score = at("idx_score", [P, 9 * P], F32, G + 10 * K)
        sel = at("sel", [P, 9 * P], BF16, sq_at)
        idx_relu = at("idx_relu", [P, 2, S], F32, G + 15 * K)
        cq2, ck2 = (at(n, [P, 2, S], F32, G + (20 + 4 * j) * K) for j, n in enumerate(("cq2", "ck2")))
        cv = at("cv", [P, QT, 256], F32, G + 28 * K)
        dq2, dk2 = (at(n, [P, 2, S], F32, G + (32 + 4 * j) * K) for j, n in enumerate(("dq2", "dk2")))
        dv = at("dv", [P, QT, 256], F32, G + 40 * K)
        nbias = at("nbias", [P, HEADS, 2 * P], F32, G + 44 * K)
        conv_in, conv_gate, conv_y = (at(n, [P, 2, S], F32, G + (52 + 4 * j) * K)
                                      for j, n in enumerate(("conv_in", "conv_gate", "conv_y")))
        ik_odd = at("ik_odd", [P, S], F32, G + 52 * K)
        r1_f = at("r1_f", [P, S], F32, G + 64 * K)
        squares = at("squares", [P, KD, S], F32, G + 48 * K)
        squares_g = at("squares_g", [P, KD, S], F32, G + 32 * K)
        pool_v = at("pool_v", [P, 2, PAD + S], F32, G + 32 * K)
        pool_s = [at(f"pool_s{j}", [P, PAD + S], F32, (G + 37 * K if j < 2 else xa_at + 26 * K) + 2112 * (j % 2))
                  for j in range(4)]
        pool_d = conv_in
        probs2 = [at(f"probs2{s}", [P, ROWLEN], F32, G + 5 * K * s) for s in range(2)]
        pT2 = at("pT2", [P, ROWLEN], F32, G + 15 * K)
        o2 = [t[:, :].rearrange("p (a b) -> p a b", a=QT) for t in (cos_t, sin_t)]
        pool_w = at("pool_w", [P, 2, P], F32, xa_at + 31 * K)
        gate_t, silu_t, up_t, hid_t = (at(n, [P, 2, S], F32, G + 4 * K * j)
                                       for j, n in enumerate(("gate_t", "silu_t", "up_t", "hid_t")))
        squares2 = at("squares2", [P, KD, S], F32, G)
        p_raw = at("p_raw", [P, 2, S], F32, G + 20 * K)
        p_hi, p_lo = (at(n, [P, 2, S], F32R, G + (24 + 4 * j) * K) for j, n in enumerate(("p_hi", "p_lo")))
        branch = at("branch", [P, KD, S], F32, G + 32 * K)
        projected = at("projected", [P, KD, S], F32, G + 48 * K)
        JOBS = [(dq2, dk2, dv, hd) for hd in range(4)] + [(cq2, ck2, cv, hd) for hd in range(4)]
        scratch = nc.dram_tensor("bias_scratch", (HEADS, P * ROWS), F32, kind="Internal").ap()
        rows_view = scratch.rearrange("h (p x) -> h p x", p=P)
        skewed = scratch[:, P - 1:P - 1 + P * (ROWS - 1)].rearrange("h (p x) -> p h x", p=P)[:, :, 0:2 * P]
        p_view = pT_in.rearrange("(k p) n -> p k n", p=P)
        out_view = outT.rearrange("(k p) n -> p k n", p=P)
        q_nope = at("q_nope", [P, HEADS, S], F32, xb_at)
        k_nope = at("k_nope", [P, HEADS, S], F32, xb_at + 16 * K)
        v_tok2 = at("v_tok2", [P, QT, D], F32, G)
        qr_eo = at("qr_eo", [P, 4, S], F32, G + 16 * K)
        k_eo = at("k_eo", [P, 2, S], F32, G + 24 * K)
        rope_tmp2 = at("rope_tmp2", [P, 2, S], F32, G + 28 * K)
        table2 = at("table2", [P, 2, S], F32, G + 32 * K)
        mla_qn = [at(f"mla_qn{s}", [P, S], F32, G + 28 * K + 2 * K * s) for s in range(2)]
        mla_qr = [at(f"mla_qr{s}", [P, S], F32R, G + 32 * K + 2 * K * s) for s in range(2)]
        mla_kr = at("mla_kr", [P, S], F32R, G + 36 * K)
        mla_kr_lo = at("mla_kr_lo", [P, S], F32R, xa_at + 30 * K)
        k_eo_hi = at("k_eo_hi", [P, 2, S], F32R, xa_at + 4 * K)
        k_eo_lo = at("k_eo_lo", [P, 2, S], F32R, xa_at + 8 * K)
        mla_v = [at(f"mla_v{s}", [P, QT, P], F32, G + 24 * K + 2 * K * s) for s in range(2)]
        qr_hi = [at(f"qr_hi{j}", [P, S], F32R, xa_at + o * K) for j, o in enumerate((24, 26, 12, 28))]
        qr_lo = at("qr_lo", [P, 4, S], F32R, G + 16 * K)
        ckv = at("ckv", [P, 2, S], F32, G + 36 * K)
        ckv_hi, ckv_lo = (at(n, [P, 2, S], F32R, G + 40 * K + 4 * K * j) for j, n in enumerate(("ckv_hi", "ckv_lo")))
        cq_raw = at("cq_raw", [P, 3, S], F32, G + 48 * K)
        cq_hi, cq_lo = (at(n, [P, 3, S], F32R, G + 54 * K + 6 * K * j) for j, n in enumerate(("cq_hi", "cq_lo")))
        mla_probs = [at(f"mla_probs{s}", [P, ROWLEN], F32, G + 38 * K + 5 * K * s) for s in range(2)]
        mla_pT = [at(f"mla_pT{s}", [P, QT, S], F32, G + 48 * K + 8 * K * s) for s in range(2)]
        u_tmp = at("u_tmp", [P, 2, S], F32, G)
        u_sq = at("u_sq", [P, 2, S], F32, G + 4 * K)
        assert G + 66 * K <= top, (G, top)

        ps = [ctx.enter_context(nc.psum_tensor(f"ps{b}", [P, S], F32)) for b in range(8)]
        STAT, BC, PT0, O_PS, OT = ps[6], ps[7], 4, ps[6], ps[7]
        MLA_O = (ps[6], ps[7])
        PT = [ps[PT0 + b][:, col:col + P * (i + 1)] for i, (b, col) in enumerate(((0, 0), (1, 0), (0, P), (1, 0)))]

        raw_full = [sem(f"raw_full{s}") for s in range(2)]
        whi_done = sem("whi_done")
        wlo_done = sem("wlo_done")
        tile_done = sem("tile_done")
        bank_free = [sem(f"bank_free{b}") for b in range(4)]
        first_full = sem("first_full")
        first_hi = sem("first_hi")
        first_lo = sem("first_lo")
        zeros_done = sem("zeros_done")
        x_loaded = [sem(f"x_loaded{i}") for i in range(4)]
        const_loaded = sem("const_loaded")
        gain_loaded = sem("gain_loaded")
        buckets_loaded = sem("buckets_loaded")
        dve_const = sem("dve_const")
        xh_done = sem("xh_done")
        xl_done = sem("xl_done")
        hid_hi = sem("hid_hi")
        hid_sq = sem("hid_sq")
        hid_lo = sem("hid_lo")
        sq_done = sem("sq_done")
        ssq_done = sem("ssq_done")
        stat_done = sem("stat_done")
        ms_done = sem("ms_done")
        rstd_t_done = sem("rstd_t_done")
        bc_done = sem("bc_done")
        rstd_f_done = sem("rstd_f_done")
        table_done = sem("table_done")
        rope_done = sem("rope_done")
        lam_done = sem("lam_done")
        lam_exp = sem("lam_exp")
        split_hi = sem("split_hi")
        split_lo = sem("split_lo")
        rope_hi = sem("rope_hi")
        stage_full = [[sem(f"stage_full{s}{c}") for c in range(2)] for s in range(2)]
        mla_full = [sem(f"mla_full{s}") for s in range(2)]
        v_full = [sem(f"v_full{s}") for s in range(2)]
        rope_lo = sem("rope_lo")
        kr_full = sem("kr_full")
        mask_done = sem("mask_done")
        nm_done = sem("nm_done")
        ri_done = sem("ri_done")
        rc_done = sem("rc_done")
        a_done = sem("a_done")
        pn_done = sem("pn_done")
        tr_done = sem("tr_done")
        ptc_done = sem("ptc_done")
        o_done = sem("o_done")
        oc_done = sem("oc_done")
        sqo_done = sem("sqo_done")
        oss_done = sem("oss_done")
        oms_done = sem("oms_done")
        orstd_done = sem("orstd_done")
        on_done = sem("on_done")
        ot_done = sem("ot_done")
        rows_mm = sem("rows_mm")
        rows_done = sem("rows_done")
        rows_stored = sem("rows_stored")
        nbias_full = sem("nbias_full")
        nb_masked = sem("nb_masked")
        r12_done = sem("r12_done")
        small_done = sem("small_done")
        ik_full = sem("ik_full")
        iwt_done = sem("iwt_done")
        idx_acc = sem("idx_acc")
        diag_done = sem("diag_done")
        top_done = sem("top_done")
        sel_done = sem("sel_done")
        conv_x = sem("conv_x")
        conv_step = sem("conv_step")
        conv_out = sem("conv_out")
        pool_zero = sem("pool_zero")
        pool_s_done = sem("pool_s_done")
        pool_fix_done = sem("pool_fix_done")
        pool_d_done = sem("pool_d_done")
        poolw_full = sem("poolw_full")
        x2_done = sem("x2_done")
        p_full = sem("p_full")
        res_dve = sem("res_dve")
        res_pool = sem("res_pool")
        branch_done = sem("branch_done")
        silu_done = sem("silu_done")
        gated_done = sem("gated_done")
        y_done = sem("y_done")
        out_done = sem("out_done")

        def gains_of(name):
            return lambda k: g(name, k)

        def gains_all(name):
            c0, n = GAINS[name]
            return gain[:, c0:c0 + n]

        def g(name, k):
            c0 = GAINS[name][0] + k
            return gain[:, c0:c0 + 1]

        X = dict(qkv=0, diff_o=8, mlp0=16, dkv=24, dq=32, ckv=40, cq=42, mla_o=45, mlp1=53, w_in=61, mix=69, p=77, ffn=79, ple=87)
        NM_DIFF = 8 * HEADS
        NM_MLA = NM_DIFF + 4 * HEADS

        x_view = xT.rearrange("(k p) n -> p k n", p=P)
        consts = [(ident[:, :], ident_in), (cos_t[:, :], cos), (sin_t[:, :], sin),
                  (mask[:, :], mask_in), (lam_in[:, :, :].rearrange("p a b -> p (a b)"), lam.partition_broadcast(P)),
                  (tab[0:BUCKETS, :], tab_in),
                  (pool_fix[:, :, :].rearrange("p a b -> p (a b)"), pool_fix_in)]

        block = ctx.enter_context(nc.Block())

        @block.sync
        def _(sp):
            def load(c, slot):
                if not isinstance(c, int) or c >= 2:
                    sp.wait_ge(wlo_done, c - 1)
                sp.dma_start(raw[slot][:, :], wst[c]).then_inc(raw_full[slot], 16)

            def load_pairs(c0, c1):
                with sp.Fori(0, (c1 - c0) // 2) as i:
                    for s in range(2):
                        load(c0 + s + 2 * i, (c0 + s) % 2)
                if (c1 - c0) % 2:
                    load(c1 - 1, (c1 - 1) % 2)

            def stage_diff(par, half, first):
                if first:
                    sp.wait_ge(split_lo, 4)
                for comp in range(2):
                    if not first:
                        sp.wait_ge(tile_done, T["diff"] + 8 * par + 16 * half - 16 + 4 * (comp + 1))
                    for hf in range(2):
                        rows = slice(32 * (2 * par + comp), 32 * (2 * par + comp) + 32)
                        own, other = (slice(64 * c + 32 * hf, 64 * c + 32 * hf + 32) for c in (comp, 1 - comp))
                        for dst, src in ((stage[par][own, comp, :, :], qk_split[hf][rows, half, Q_HI:K_HI + 1, :]),
                                         (stage[par][other, comp, :, :], qk_split[hf][rows, half, Q_LO:K_HI + 1:2, :]),
                                         (stage_k_lo[par][own, :], qk_split[hf][rows, half, K_LO, :])):
                            sp.dma_start(dst.bitcast(F32), src.bitcast(F32)).then_inc(stage_full[par][comp], 16)

            for part, full in ((FIRST, first_full), (SECOND, raw_full[0])):
                sp.dma_start(raw[0][:, part], wst[0][:, part]).then_inc(full, 16)
            sp.wait_ge(x_loaded[2], 16)
            load(1, 1)
            for dst, src in consts:
                sp.dma_start(dst, src).then_inc(const_loaded, 16)
            load_pairs(2, 6)
            stage_diff(0, 0, True)
            load_pairs(6, 8)
            stage_diff(1, 0, True)
            load_pairs(8, 14)
            sp.wait_ge(split_lo, 16)
            with sp.Fori(1, HEADS // 2) as half:
                for par in range(2):
                    stage_diff(par, half, False)
            load_pairs(14, C["dkv"] + 2)
            load_pairs(C["dkv"] + 2, C["wo_b"] + 2)
            sp.wait_ge(rope_lo, 1)
            for hf in range(2):
                for row in (0, 64):
                    sp.dma_start(mla_kr[row + 32 * hf:row + 32 * hf + 32, :].bitcast(F32), k_eo_hi[0:32, hf, :].bitcast(F32))\
                        .then_inc(kr_full, 16)
                sp.dma_start(mla_kr_lo[32 * hf:32 * hf + 32, :].bitcast(F32), k_eo_lo[0:32, hf, :].bitcast(F32)).then_inc(kr_full, 16)
            sp.wait_ge(rope_lo, 5)
            for n in range(HEADS):
                tile = T["uq"] + 4 + n
                sp.wait_ge(bank_free[tile % 4], tile // 4 + 1)
                par, rows = n % 2, slice(32 * (n % 4), 32 * (n % 4) + 32)
                if n >= 2:
                    sp.wait_ge(tile_done, T["mla"] + 4 * (n - 1))
                sp.dma_start(mla_qn[par][:, :], q_nope[:, n, :]).then_inc(mla_full[par], 16)
                for hf in range(2):
                    sp.dma_start(mla_qr[par][32 * hf:32 * hf + 32, :].bitcast(F32),
                                 qr_hi[2 * (n // 4) + hf][rows, :].bitcast(F32)).then_inc(mla_full[par], 16)
                    sp.dma_start(mla_qr[par][64 + 32 * hf:96 + 32 * hf, :].bitcast(F32),
                                 qr_lo[rows, 2 * (n // 4) + hf, :].bitcast(F32)).then_inc(mla_full[par], 16)
                if n >= 2:
                    sp.wait_ge(o_done, HEADS + n - 1)
                sp.dma_start(mla_v[par][:, :, :], v_tok2[:, :, P * n:P * n + P]).then_inc(v_full[par], 16)
            load_pairs(C["wo_b"] + 2, C["mlp1"] + 1)
            sp.wait_ge(tile_done, T["wo_b"] + 1)
            sp.dma_start(buckets[0:BUCKETS, :], buckets_in).then_inc(buckets_loaded, 16)
            load_pairs(C["mlp1"] + 1, C["w_in"] + 4)
            sp.wait_ge(stat_done, STATS[6] + 1)
            sp.wait_ge(rows_stored, 16)
            sp.dma_start(nbias[:, :, :], skewed).then_inc(nbias_full, 16)
            sp.wait_ge(tile_done, T["w_in"])
            sp.dma_start(pool_w[:, :, :].rearrange("p a b -> p (a b)"), pool_w_in).then_inc(poolw_full, 16)
            load(C["w_in"] + 4, C["w_in"] % 2)
            t = T["w_in"] + 4
            sp.wait_ge(bank_free[t % 4], t // 4 + 1)
            sp.dma_start(ik_odd[64:128, :], ik_iw[0:64, :]).then_inc(ik_full, 16)
            load_pairs(C["w_in"] + 5, C["proj0"])
            sp.wait_ge(tile_done, T["w_out"] + 1)
            sp.dma_start(p_raw[:, :, :], p_view).then_inc(p_full, 16)
            load_pairs(C["proj0"], C["end2"])
            for k in range(KD):
                sp.wait_ge(y_done, k + 1)
                sp.dma_start(out_view[:, k, :], h[:, k, :]).then_inc(out_done, 16)

            sp.wait_ge(out_done, 16 * KD)

        @block.tensor
        def _(pe):
            def products(out, lhs_hi, lhs_lo, rhs_hi, rhs_lo, first, last):
                pe.matmul(out, lhs_hi, rhs_hi, start=first, stop=False)
                pe.matmul(out, lhs_hi, rhs_lo, start=False, stop=False)
                return pe.matmul(out, lhs_lo, rhs_hi, start=False, stop=last)

            def bank_ready(t, per=0, i=0):
                if not isinstance(i, int) or t // 4 + (per // 4) * i > 0:
                    pe.wait_ge(bank_free[t % 4], t // 4 + (per // 4) * i)

            def features(slot, c, t0, xhi, xlo, kt=KD, cols=256, n=2, a_from=0, per=0, i=0, fresh=None,
                         hook=None, pair_hook=None):
                if isinstance(c, int) and c == 0:
                    pe.wait_ge(first_lo, 1)
                else:
                    pe.wait_ge(wlo_done, c + 1)
                w_hi, w_lo = (w[slot][:, 0:kt * cols].rearrange("p (k m) -> p k m", k=kt) for w in (whi, wlo))
                for a0 in range(0, n, 2):
                    pair = range(a0, min(a0 + 2, n))
                    late = fresh is not None and a0 == 0
                    if pair_hook is not None:
                        pair_hook(a0)
                    for a in pair:
                        bank_ready(t0 + a, per, i)
                    for k in range(kt):
                        if isinstance(c, int) and c == 0 and k == KD // 2:
                            pe.wait_ge(wlo_done, 1)
                        if hook is not None:
                            hook(k)
                        if late:
                            pe.wait_ge(fresh[0], fresh[2] + k + 1)
                        for a in pair:
                            out, m = ps[(t0 + a) % 4][:, :], slice((a_from + a) * P, (a_from + a + 1) * P)
                            if late:
                                pe.matmul(out, w_hi[:, k, m], xhi[:, k, :], start=(k == 0), stop=False)
                                pe.matmul(out, w_lo[:, k, m], xhi[:, k, :], start=False, stop=False)
                                continue
                            mm = products(out, w_hi[:, k, m], w_lo[:, k, m], xhi[:, k, :], xlo[:, k, :],
                                          k == 0, k == kt - 1)
                            if k == kt - 1:
                                mm.then_inc(tile_done, 1)
                    for k in range(kt if late else 0):
                        pe.wait_ge(fresh[1], fresh[2] + k + 1)
                        for a in pair:
                            m = slice((a_from + a) * P, (a_from + a + 1) * P)
                            mm = pe.matmul(ps[(t0 + a) % 4][:, :], w_hi[:, k, m], xlo[:, k, :], start=False, stop=(k == kt - 1))
                            if k == kt - 1:
                                mm.then_inc(tile_done, 1)

            def tokens(slot, c, t0, xhi, xlo, per=0, i=0):
                pe.wait_ge(wlo_done, c + 1)
                w_hi = whi[slot][:, :].rearrange("p (k m) -> p k m", k=KD)
                w_lo = wlo[slot][:, :].rearrange("p (k m) -> p k m", k=KD)
                for u in range(2):
                    bank_ready(t0 + u, per, i)
                    for half in range(2):
                        q = slice((2 * u + half) * P, (2 * u + half + 1) * P)
                        out = ps[(t0 + u) % 4][:, half * 256:half * 256 + 256]
                        for k in range(KD):
                            mm = products(out, xhi[:, k, q], xlo[:, k, q], w_hi[:, k, :], w_lo[:, k, :],
                                          k == 0, k == KD - 1)
                    mm.then_inc(tile_done, 1)

            def stat(n):
                pe.wait_ge(ssq_done, SSQ[n + 1])
                if n >= 8:
                    pe.wait_ge(on_done, 2 * HEADS)
                for q in range(QT):
                    mm = pe.matmul(STAT[:, q:q + 1], ssq[:, q * P:(q + 1) * P], ones[:, :], start=True, stop=True)
                mm.then_inc(stat_done, 1)

            def broadcast(n, src=None):
                if src is None:
                    pe.wait_ge(rstd_t_done, n + 1)
                    src = rstd_t[:, 4 * n:4 * n + 4]
                for q in range(QT):
                    mm = pe.matmul(BC[:, q * P:(q + 1) * P], src[:, q:q + 1].to_broadcast([P, P]), ident[:, :],
                                   start=True, stop=True)
                mm.then_inc(bc_done, 1)

            def late_rstd(norm, k):
                if k == 3:
                    stat(norm)
                elif k == (4 if norm == 0 else 6):
                    if norm == 0:
                        pe.wait_ge(const_loaded, 16 * len(consts))
                    broadcast(norm)

            def linear(stage, pairs, xhi, xlo, fresh, norm=None, hook=None):
                c, t = C[stage], T[stage]
                features(c % 2, c, t, xhi, xlo, fresh=fresh, hook=hook)
                features((c + 1) % 2, c + 1, t + 2, xhi, xlo,
                         hook=(lambda k: late_rstd(norm, k)) if norm is not None else None)
                with pe.Fori(1, pairs) as i:
                    for s in range(2):
                        features((c + s) % 2, c + s + 2 * i, t + 2 * s, xhi, xlo, per=4, i=i)

            def bias_by_distance():
                pe.wait_ge(buckets_loaded, 16)
                pe.matmul(ps[PT0][0:HEADS, 0:ROWS], tab[0:BUCKETS, :], buckets[0:BUCKETS, :], start=True, stop=True)\
                    .then_inc(rows_mm, 1)

            def mlp(stage, norm, xhi, xlo, hhi, hlo, x0, hid0, rows=False):
                c, t = C[stage], T[stage]

                def one_round(r, first):
                    for u in range(4):
                        hook = None
                        if first and u == 1:
                            hook = lambda k: broadcast(norm) if k == 4 else None
                        elif first and u == 2 and rows:
                            bias_by_distance()
                        features((c + u) % 2, c + u + 8 * r, t + 2 * u, xhi, xlo, per=16, i=r, hook=hook,
                                 fresh=(xh_done, xl_done, x0) if first and u == 0 else None)
                        if first and u == 0:
                            stat(norm)
                    for d in range(4):
                        features((c + d) % 2, c + 4 + d + 8 * r, t + 8 + 2 * d, hhi, hlo, per=16, i=r,
                                 fresh=(hid_hi, hid_lo, hid0 + 8 * r) if d == 0 else None)

                one_round(0, True)
                with pe.Fori(1, ROUNDS) as r:
                    one_round(r, False)

            pe.wait_ge(zeros_done, 1)
            for _ in range(WARM):
                pe.matmul(BC[:, 0:P], zeros[:, :], zeros[:, :], start=True, stop=True)

            linear("qk", 4, xa_hi, xa_lo, (xh_done, xl_done, X["qkv"]), norm=0)
            with pe.Fori(0, 2) as i:
                for s in range(2):
                    tokens((C["v"] + s) % 2, C["v"] + s + 2 * i, T["v"] + 2 * s, xa_hi, xa_lo, per=4, i=i)

            def mask_later(out):
                return pe.matmul(out, ident_b[:, :], mask_b[:, :], start=False, stop=True)

            def diff_scores(par, half, comp):
                pe.wait_ge(stage_full[par][comp], 96 * (half + 1))
                own = slice(64 * comp, 64 * comp + 64)
                for i in range(QT):
                    n = 8 * par + 4 * comp + i
                    bank_ready(T["diff"] + n, 16, half)
                    b, q = ps[(T["diff"] + n) % 4], slice(P * i, P * i + P)
                    wide = max(P * (i + 1), 2 * P)
                    pe.matmul(b[:, 0:wide], stage[par][:, comp, 0, q], stage[par][:, comp, 1, 0:wide], start=True, stop=False)
                    pe.matmul(b[:, 0:wide], stage[par][own, comp, 0, q], stage_k_lo[par][own, 0:wide],
                              start=False, stop=False)
                    mask_later(b[:, q]).then_inc(tile_done, 1)

            def transposes(src, ready, n):
                for j, i in enumerate(TR_ORDER):
                    pe.wait_ge(*ready(j, i))
                    if j == 0 and not (isinstance(n, int) and n < 1):
                        pe.wait_ge(ptc_done, 4 * n)
                    elif j == 3:
                        pe.wait_ge(ptc_done, 4 * n + 1)
                    for kt in range(i + 1):
                        mm = pe.transpose(PT[i][:, kt * P:(kt + 1) * P],
                                          src[:, OFF[i] + kt * P:OFF[i] + (kt + 1) * P], ident[:, :])
                    mm.then_inc(tr_done, 1)

            def weighted(src, vals, head, n, taken):
                if not (isinstance(n, int) and n < 1):
                    pe.wait_ge(taken, n)
                for j, i in enumerate(TR_ORDER):
                    pe.wait_ge(ptc_done, 4 * n + j + 1)
                    for kt in range(i + 1):
                        mm = pe.matmul(O_PS[:, i * P:(i + 1) * P], src[:, OFF[i] + kt * P:OFF[i] + (kt + 1) * P],
                                       vals[:, kt, bass.ts(head, P)], start=(kt == 0), stop=(kt == i))
                mm.then_inc(o_done, 1)

            def turn(src, n, x_before):
                pe.wait_ge(on_done, n + 1)
                if not (isinstance(n, int) and n < 1):
                    pe.wait_ge(xl_done, x_before)
                for i in range(QT):
                    mm = pe.transpose(OT[:, i * P:(i + 1) * P], src[:, i, :], ident[:, :])
                mm.then_inc(ot_done, 1)

            def diff_step(par, half, first=0, scores=True):
                n = 2 * half + par
                if scores:
                    diff_scores(1 - par, half + par, 0)
                if first >= 3 and scores:
                    turn(o_raw[1 - par], n - 3, X["diff_o"] + n - 3)
                if first >= 1:
                    weighted(pT[1 - par], v_tok, n - 1, n - 1, oc_done)
                if not scores:
                    turn(o_raw[1 - par], n - 3, X["diff_o"] + n - 3)
                transposes(probs[par][:, 0, :], lambda j, i: (a_done, 4 * n + j + 1), n)
                if scores:
                    diff_scores(1 - par, half + par, 1)

            pe.wait_ge(dve_const, 5)
            diff_scores(0, 0, 0)
            diff_scores(0, 0, 1)
            for n in range(3):
                diff_step(n % 2, n // 2, first=n)
            with pe.Fori(1, HEADS // 2 - 1) as i:
                diff_step(1, i, first=3)
                diff_step(0, i + 1, first=3)
            diff_step(1, HEADS // 2 - 1, first=3, scores=False)
            weighted(pT[1], v_tok, HEADS - 1, HEADS - 1, oc_done)
            turn(o_raw[1], HEADS - 3, X["diff_o"] + HEADS - 3)

            def last_heads(k):
                if k in (2, 5):
                    n = HEADS - 2 if k == 2 else HEADS - 1
                    turn(o_raw[n % 2], n, X["diff_o"] + n)

            linear("wo_a", 2, xb_hi, xb_lo, (xh_done, xl_done, X["diff_o"]), hook=last_heads)
            mlp("mlp0", 1, xa_hi, xa_lo, xb_hi, xb_lo, X["mlp0"], 0)
            c, t = C["dkv"], T["dkv"]
            features(c % 2, c, t, xa_hi, xa_lo, fresh=(xh_done, xl_done, X["dkv"]))
            stat(2)
            features((c + 1) % 2, c + 1, t + 2, xa_hi, xa_lo, hook=lambda k: broadcast(2) if k == 4 else None)
            features(c % 2, c + 2, t + 4, xb_hi, xb_lo, fresh=(xh_done, xl_done, X["dq"]))
            features((c + 1) % 2, c + 3, t + 6, xb_hi, xb_lo, n=1)
            stat(3)
            c, t = C["ukv"], T["ukv"]
            features(c % 2, c, t, ckv_hi, ckv_lo, kt=2, cols=1024, n=8,
                     fresh=(xh_done, xl_done, X["ckv"]),
                     pair_hook=lambda a: broadcast(3) if a == 2 else None)
            pe.wait_ge(wlo_done, c + 2)
            stat(4)
            w_hi, w_lo = (w[(c + 1) % 2][:, :].rearrange("p (k m) -> p k m", k=2) for w in (whi, wlo))
            for q in range(QT):
                for half in range(2):
                    tt = t + 8 + 2 * q + half
                    bank_ready(tt)
                    for k in range(2):
                        rows, cols = slice(q * P, q * P + P), slice(512 * half, 512 * half + 512)
                        mm = products(ps[tt % 4][:, :], ckv_hi[:, k, rows], ckv_lo[:, k, rows],
                                      w_hi[:, k, cols], w_lo[:, k, cols], k == 0, k == 1)
                    mm.then_inc(tile_done, 1)
            broadcast(4)
            c, t = C["uq"], T["uq"]
            for u in range(3):
                features((c + u) % 2, c + u, t + 4 * u, cq_hi, cq_lo, kt=3, cols=512, n=4,
                         fresh=(xh_done, xl_done, X["cq"]) if u == 0 else None)

            def mla_scores(par, n, tiles):
                if 0 in tiles:
                    pe.wait_ge(mla_full[par], 80 * (n // 2 + 1) if isinstance(n, int) else 80 + 40 * (n - par))
                for i in tiles:
                    bank_ready(T["mla"] + i, 4, n)
                    b, w, q = ps[(T["mla"] + i) % 4], P * (i + 1), slice(P * i, P * i + P)
                    wide = max(w, 2 * P)
                    pe.matmul(b[:, 0:wide], mla_qr[par][:, q], mla_kr[:, 0:wide], start=True, stop=False)
                    pe.matmul(b[:, 0:wide], mla_qr[par][0:64, q], mla_kr_lo[0:64, 0:wide], start=False, stop=False)
                    pe.matmul(b[:, 0:w], mla_qn[par][:, q], k_nope[:, n, 0:w], start=False, stop=False)
                    mask_later(b[:, q]).then_inc(tile_done, 1)

            def mla_weighted(par, n):
                if not (isinstance(n, int) and n < 2):
                    pe.wait_ge(xl_done, X["mla_o"] + n - 1)
                pe.wait_ge(v_full[par], 16 * (n // 2 + 1) if isinstance(n, int) else 16 + 8 * (n - par))
                pe.wait_ge(ptc_done, 4 * (HEADS + n) + 4)
                for kt in range(QT):
                    mm = pe.matmul(MLA_O[par][:, P * kt:S], mla_v[par][:, kt, :], mla_pT[par][:, kt, P * kt:S],
                                   start=(kt == 0), stop=(kt == QT - 1))
                mm.then_inc(o_done, 1)

            def mla_step(par, n, scores=True):
                if scores:
                    mla_scores(1 - par, n + 1, (0, 1))
                transposes(mla_probs[par], lambda j, i: (pn_done, 4 * n + j + 1), HEADS + n)
                if scores:
                    mla_scores(1 - par, n + 1, (2, 3))
                mla_weighted(par, n)

            pe.wait_ge(kr_full, 96)
            mla_scores(0, 0, range(QT))
            mla_step(0, 0)
            with pe.Fori(0, HEADS // 2 - 1) as i:
                mla_step(1, 2 * i + 1)
                mla_step(0, 2 * i + 2)
            mla_step(1, HEADS - 1, scores=False)

            linear("wo_b", 2, xa_hi, xa_lo, (xh_done, xl_done, X["mla_o"]))
            mlp("mlp1", 5, xb_hi, xb_lo, xa_hi, xa_lo, X["mlp1"], 8 * ROUNDS, rows=True)
            c, t = C["w_in"], T["w_in"]
            features(c % 2, c, t, xb_hi, xb_lo, fresh=(xh_done, xl_done, X["w_in"]))
            pe.wait_ge(ssq_done, SSQ[7])
            for q in range(QT):
                for j, sums in enumerate((ssq, sq_tmp)):
                    mm = pe.matmul(STAT[:, 2 * q + j:2 * q + j + 1], sums[:, q * P:(q + 1) * P], ones[:, :],
                                   start=True, stop=True)
            mm.then_inc(stat_done, 1)

            def both_rstd(k):
                if k == 4:
                    pe.wait_ge(r12_done, 1)
                    broadcast(None, r12)

            features((c + 1) % 2, c + 1, t + 2, xb_hi, xb_lo, hook=both_rstd)
            def final_rstd(k):
                if k == 4:
                    pe.wait_ge(rstd_f_done, 7)
                    broadcast(6)

            features(c % 2, c + 2, t + 4, xb_hi, xb_lo, n=1, hook=final_rstd)
            features((c + 1) % 2, c + 3, t + 5, xb_hi, xb_lo)
            pe.wait_ge(bank_free[(t + 4) % 4], (t + 4) // 4 + 1)
            for q in range(QT):
                mm = pe.transpose(STAT[:, IDX_HEADS * q:IDX_HEADS * (q + 1)], ik_iw[64:64 + IDX_HEADS, q * P:(q + 1) * P],
                                  ident[64:64 + IDX_HEADS, 64:64 + IDX_HEADS])
            mm.then_inc(iwt_done, 1)
            def index_scores(i):
                for hd in range(IDX_HEADS):
                    tt = T_IDX[i] + hd
                    bank_ready(tt)
                    if i == 1 and hd == 0:
                        for tile in range(T["w_in"], T["w_in"] + 4):
                            pe.wait_ge(bank_free[tile % 4], tile // 4 + 1)
                        pe.wait_ge(ik_full, 16)
                    rows = slice(64 * (hd % 2), 64 * (hd % 2) + 64)
                    pe.matmul(ps[tt % 4][:, 0:P * (i + 1)], iq[rows, hd // 2, P * i:P * i + P],
                              (ik_iw, ik_odd)[hd % 2][rows, 0:P * (i + 1)], start=True, stop=True).then_inc(tile_done, 1)

            def scores2(jb, tiles):
                q, k, _, hd = JOBS[jb]
                rows = slice(64 * (hd % 2), 64 * (hd % 2) + 64)
                for i in tiles:
                    tt = T_JOB[jb] + i
                    bank_ready(tt)
                    if jb % 2 == 0 and i == 0:
                        for tile in Q_TILES[jb // 2]:
                            pe.wait_ge(bank_free[tile % 4], tile // 4 + 1)
                    out, chosen = ps[tt % 4][:, 0:P * (i + 1)], jb >= 4 and i >= 1
                    mm = pe.matmul(out, q[rows, hd // 2, P * i:P * i + P], k[rows, hd // 2, 0:P * (i + 1)],
                                   start=True, stop=not chosen)
                    if chosen:
                        pe.wait_ge(sel_done, i)
                        mm = pe.matmul(out, ident_b[:, :], sel[:, IDX_OFF[i]:IDX_OFF[i] + P * (i + 1)],
                                       start=False, stop=True)
                    mm.then_inc(tile_done, 1)

            def weighted2(jb):
                _, _, v, hd = JOBS[jb]
                n = 2 * HEADS + jb
                if jb in (0, 4):
                    for tile in V_TILES[jb // 4]:
                        pe.wait_ge(bank_free[tile % 4], tile // 4 + 1)
                pe.wait_ge(on_done, HEADS + jb)
                for j, i in enumerate(TR_ORDER):
                    pe.wait_ge(ptc_done, 4 * n + j + 1)
                    for kt in range(i + 1):
                        mm = pe.matmul(O_PS[:, i * 64:(i + 1) * 64],
                                       pT2[:, OFF[i] + kt * P:OFF[i] + (kt + 1) * P],
                                       v[:, kt, 64 * hd:64 * hd + 64], start=(kt == 0), stop=(kt == i))
                mm.then_inc(o_done, 1)

            def turn2(pair):
                pe.wait_ge(on_done, HEADS + 2 * pair + 2)
                if pair:
                    pe.wait_ge(xl_done, X["mix"] + MIX_PAIR[pair - 1] + 1)
                for i in range(QT):
                    mm = pe.transpose(OT[:, i * P:(i + 1) * P], o2[pair % 2][:, i, :], ident[:, :])
                mm.then_inc(ot_done, 1)

            c = C["w_in2"]
            index_scores(1)
            features(c % 2, c, T_CK, xb_hi, xb_lo)
            index_scores(2)
            tokens((c + 1) % 2, c + 1, T_CV, xb_hi, xb_lo)
            index_scores(3)
            features(c % 2, c + 2, T_DQ, xb_hi, xb_lo)
            features((c + 1) % 2, c + 3, T_DK, xb_hi, xb_lo)
            scores2(0, range(QT))
            tokens(c % 2, c + 4, T_DV, xb_hi, xb_lo)
            for jb in range(8):
                if jb < 7:
                    scores2(jb + 1, (0, 1))
                transposes(probs2[jb % 2], lambda j, i: (bank_free[(T_JOB[jb] + i) % 4], (T_JOB[jb] + i) // 4 + 1),
                           2 * HEADS + jb)
                if jb < 7:
                    scores2(jb + 1, (2, 3))
                weighted2(jb)
                if jb >= 2 and jb % 2 == 0:
                    turn2((jb - 2) // 2)
                if jb == 7:
                    pe.wait_ge(pool_d_done, 4)
                    pe.wait_ge(poolw_full, 16)
                    for a in range(2):
                        bank_ready(T_POOL + a)
                        pe.matmul(ps[(T_POOL + a) % 4][:, :], pool_w[:, a, :], pool_d[:, a, :], start=True, stop=True)\
                            .then_inc(tile_done, 1)
                u = C["att2"] + jb // 2
                features(u % 2, u, T_PROJ[jb], xb_hi, xb_lo, n=1, a_from=jb % 2)
            turn2(3)

            linear("w_out", 2, xa_hi, xa_lo, (xh_done, xl_done, X["mix"]))

            def proj(u, fresh):
                c, t = C[f"proj{u}"], T[f"proj{u}"]
                features(c % 2, c, t, p_hi, p_lo, kt=2, cols=512, fresh=fresh)
                stat(8 + 2 * u)
                features(c % 2, c, t + 2, p_hi, p_lo, kt=2, cols=512, a_from=2,
                         hook=lambda k: broadcast(8 + 2 * u) if k == 1 else None)

            proj(0, (xh_done, xl_done, X["p"]))

            def gate_up(r, n, first):
                c, t = C[f"gu{r}"], T[f"gu{r}"]
                if first:
                    features(c % 2, c, t, xb_hi, xb_lo, fresh=(xh_done, xl_done, X["ffn"]))
                    features((c + 1) % 2, c + 1, t + 2, xb_hi, xb_lo, hook=lambda k: late_rstd(9, k))
                with pe.Fori(1 if first else 0, n // 2) as i:
                    for s in range(2):
                        features((c + s) % 2, c + s + 2 * i, t + 2 * s, xb_hi, xb_lo, per=4, i=i)

            def down(r, n):
                c, t = C[f"dn{r}"], T[f"dn{r}"]
                for s in range(2):
                    features((c + s) % 2, c + s, t + 2 * s, xa_hi, xa_lo, kt=n,
                             fresh=(hid_hi, hid_lo, HID2 + 8 * r) if s == 0 else None)
                for s in range(2):
                    features((c + s) % 2, c + 2 + s, t + 4 + 2 * s, xa_hi, xa_lo, kt=n)

            for r, n in enumerate(GU_TILES):
                gate_up(r, n, r == 0)
                down(r, n)
            proj(1, None)

            linear("ple", 2, xb_hi, xb_lo, (xh_done, xl_done, X["ple"]), norm=11)

        @block.scalar
        def _(act):
            def hi(c0, j, t_before):
                slot = c0 % 2
                act.wait_ge(raw_full[slot], 16 * (c0 // 2 + 1) + 8 * j)
                if not isinstance(t_before, int) or t_before > 0:
                    act.wait_ge(tile_done, t_before)
                act.activation(whi[slot][:, :], raw[slot][:, :], ACT.Copy).then_inc(whi_done, 1)

            def bank_out(t, per=0, i=0):
                act.wait_ge(bank_free[t % 4], t // 4 + 1 + (per // 4) * i)

            def x_hi(dst, src, scale):
                act.activation(dst, src, ACT.Copy, scale=scale).then_inc(xh_done, 1)

            act.dma_start(gain[:, :], gains).then_inc(gain_loaded, 16)
            for i in range(4):
                act.dma_start(h[:, 2 * i:2 * i + 2, :], x_view[:, 2 * i:2 * i + 2, :]).then_inc(x_loaded[i], 16)
            def square0(k):
                act.activation(squares0[:, k, :], h[:, k, :], ACT.Square).then_inc(sq_done, 1)

            act.wait_ge(first_full, 16)
            act.activation(whi[0][:, FIRST], raw[0][:, FIRST], ACT.Copy).then_inc(first_hi, 1)
            act.wait_ge(gain_loaded, 16)
            for k in range(KD):
                if k == 2:
                    act.wait_ge(raw_full[0], 16)
                    act.activation(whi[0][:, SECOND], raw[0][:, SECOND], ACT.Copy).then_inc(whi_done, 1)
                act.wait_ge(x_loaded[k // 2], 16)
                x_hi(xa_hi[:, k, :], h[:, k, :], g("attn0", k))
                if k in (3, 5):
                    square0((k - 3) // 2)
            for k in range(2, 4):
                square0(k)
            hi(1, 0, 0)
            for k in range(4, KD):
                square0(k)

            c, t = C["qk"], T["qk"]
            act.wait_ge(lam_done, 2)
            act.activation(lam_ab[:, 2:4], lam_ab[:, 0:2], ACT.Exp).then_inc(lam_exp, 1)
            hi(c + 2, 0, t + 2)
            def split_hi_part(i, s):
                act.wait_ge(rope_done, 2 * i + s + 1)
                for hf in range(2):
                    act.activation(qk_split[hf][:, i, Q_HI + s, :], qk_raw[hf][:, i, 3 * s, :], ACT.Copy).then_inc(split_hi, 1)

            with act.Fori(1, 4) as i:
                for s in range(2):
                    hi(c + s + 1, 2 * i, t + 2 * s + 4 * i)
                    split_hi_part(i - 1, s)

            c, t = C["v"], T["v"]

            def v_pair(i, first=False):
                for s in range(2):
                    hi(c + s + 1, 2 * i, t + 2 * s + 4 * i)
                    if first and s == 0:
                        act.wait_ge(rstd_t_done, 1)
                        split_hi_part(3, 0)
                        split_hi_part(3, 1)
                    for u in range(2):
                        tt = t + 2 * s + u
                        act.wait_ge(tile_done, tt + 1 + 4 * i)
                        for half in range(2):
                            q = 2 * u + half
                            ins = act.activation(v_tok[:, q, bass.ds(256 * s + 512 * i, 256)],
                                                 ps[tt % 4][:, 256 * half:256 * half + 256],
                                                 ACT.Copy, scale=rstd_t[:, q:q + 1])
                        ins.then_inc(bank_free[tt % 4], 1)

            v_pair(0, first=True)
            with act.Fori(1, 2) as i:
                v_pair(i)

            def diff_exp(par, half, comp):
                n = 2 * half + par
                for i in range(QT):
                    j = 4 * comp + i
                    b = (T["diff"] + 8 * par + j) % 4
                    act.wait_ge(nm_done, 8 * n + j + 1)
                    if j == 0 and not (isinstance(half, int) and half < 1):
                        act.wait_ge(tr_done, 4 * (n - 1))
                    act.activation(probs[par][:, comp, OFF[i]:OFF[i] + P * (i + 1)], ps[b][:, 0:P * (i + 1)],
                                   ACT.Exp, bias=negmin[:, par, j:j + 1], scale=-1.0,
                                   accum_out=rowsum[:, par, j:j + 1]).then_inc(bank_free[b], 1)

            def copy_pT(pT, par, n):
                for j, i in enumerate(TR_ORDER):
                    act.wait_ge(tr_done, 4 * n + TR_BANK[j])
                    if j == 0 and not (isinstance(n, int) and n < 2):
                        act.wait_ge(o_done, n - 1)
                    act.activation(pT[par][:, OFF[i]:OFF[i] + P * (i + 1)], PT[i],
                                   ACT.Copy).then_inc(ptc_done, 1)

            def diff_copy_o(par, n):
                act.wait_ge(o_done, n + 1)
                if not (isinstance(n, int) and n < 2):
                    act.wait_ge(ot_done, n - 1)
                act.activation(o_raw[par][:, :, :].rearrange("p a b -> p (a b)"), O_PS[:, :],
                               ACT.Copy).then_inc(oc_done, 1)

            def diff_square(par, n):
                act.wait_ge(orstd_done, n)
                act.wait_ge(oc_done, n + 1)
                act.activation(o_sq[:, :], o_raw[par][:, :, :].rearrange("p a b -> p (a b)"), ACT.Square).then_inc(sqo_done, 1)

            def head_hi(dst, n, n0, scale):
                act.wait_ge(ot_done, n0 + n + 1)
                act.activation(dst[:, n, :], OT[:, :], ACT.Copy, scale=scale).then_inc(xh_done, 1)

            def diff_step(par, half, first=0, ahead=True):
                n = 2 * half + par
                if ahead:
                    diff_exp(1 - par, half + par, 0)
                if not ahead:
                    diff_copy_o(1 - par, n - 1)
                if first >= 3:
                    head_hi(xb_hi, n - 3, 0, gsub[:, 0:1])
                copy_pT(pT, par, n)
                if first >= 1 and ahead:
                    diff_copy_o(1 - par, n - 1)
                if ahead:
                    diff_exp(1 - par, half + par, 1)

            act.wait_ge(dve_const, 4)
            diff_exp(0, 0, 0)
            diff_exp(0, 0, 1)
            for n in range(3):
                diff_step(n % 2, n // 2, first=n)
            with act.Fori(1, HEADS // 2 - 1) as i:
                diff_step(1, i, first=3)
                diff_step(0, i + 1, first=3)
            diff_step(1, HEADS // 2 - 1, first=3, ahead=False)
            diff_square(0, HEADS - 2)
            diff_copy_o(1, HEADS - 1)
            head_hi(xb_hi, HEADS - 3, 0, gsub[:, 0:1])
            diff_square(1, HEADS - 1)
            for n in (HEADS - 2, HEADS - 1):
                head_hi(xb_hi, n, 0, gsub[:, 0:1])

            def residual(stage, dst, gname):
                c, t = C[stage], T[stage]
                for u in range(4):
                    hi(c + u + 1, 0, t + 2 * u)
                    for a in range(2):
                        bank_out(t + 2 * u + a)
                        x_hi(dst[:, 2 * u + a, :], h[:, 2 * u + a, :], gname(2 * u + a))

            def mlp(stage, hhi, dst, gname, rows=False):
                c, t = C[stage], T[stage]

                def one_round(r, first, last):
                    for u in range(4):
                        if not (first and u == 1):
                            hi(c + u + 1, 8 * r, t + 2 * u + 16 * r)
                        if first and u == 0:
                            hi(c + 2, 0, t + 2)
                        if first and u == 2 and rows:
                            act.wait_ge(rows_mm, 1)
                            act.activation(bias_rows[0:HEADS, :], ps[PT0][0:HEADS, 0:ROWS], ACT.Copy).then_inc(rows_done, 1)
                            act.wait_ge(rows_done, 1)
                            act.dma_start(rows_view, bias_rows[0:HEADS, :].unsqueeze(1).to_broadcast([HEADS, P, ROWS]))\
                                .then_inc(rows_stored, 16)
                        for a in range(2):
                            bank_out(t + 2 * u + a, 16, r)
                            act.activation(hhi[:, 2 * u + a, :], u_tmp[:, a, :], ACT.Square).then_inc(hid_hi, 1)
                    for d in range(4):
                        hi(c + d + 5, 8 * r, t + 8 + 2 * d + 16 * r)
                        if last:
                            for a in range(2):
                                k = 2 * d + a
                                bank_out(t + 8 + k, 16, r)
                                x_hi(dst[:, k, :], h[:, k, :], gname(k))
                                if rows:
                                    act.activation(squares[:, k, :], h[:, k, :], ACT.Square).then_inc(sq_done, 1)
                                    act.activation(squares_g[:, k, :], h[:, k, :], ACT.Square, scale=g("final", k))\
                                        .then_inc(sq_done, 1)

                one_round(0, True, False)
                with act.Fori(1, ROUNDS - 1) as r:
                    one_round(r, False, False)
                one_round(ROUNDS - 1, False, True)

            residual("wo_a", xa_hi, gains_of("mlp0"))
            mlp("mlp0", xb_hi, xa_hi, gains_of("kv_in"))
            c, t = C["dkv"], T["dkv"]
            hi(c + 1, 0, t)
            for k in range(KD):
                x_hi(xb_hi[:, k, :], h[:, k, :], g("attn1", k))
            hi(c + 2, 0, t + 2)
            for a in range(2):
                bank_out(t + a)
                x_hi(ckv_hi[:, a, :], ckv[:, a, :], g("kv", a))
            hi(c + 3, 0, t + 4)
            act.wait_ge(rope_done, 9)
            act.activation(k_eo_hi[0:32, :, :], k_eo[0:32, :, :], ACT.Copy).then_inc(rope_hi, 1)
            hi(c + 4, 0, t + 6)
            for a in range(3):
                bank_out(t + 4 + a)
                x_hi(cq_hi[:, a, :], cq_raw[:, a, :], g("q", a))
            c, t = C["ukv"], T["ukv"]
            hi(c + 1, 0, t)
            hi(c + 2, 0, t + 8)
            act.wait_ge(rstd_t_done, 4)
            for q in range(QT):
                for half in range(2):
                    tt = t + 8 + 2 * q + half
                    act.wait_ge(tile_done, tt + 1)
                    act.activation(v_tok2[:, q, 512 * half:512 * half + 512], ps[tt % 4][:, :], ACT.Copy,
                                   scale=rstd_t[:, 12 + q:13 + q]).then_inc(bank_free[tt % 4], 1)
            c, t = C["uq"], T["uq"]
            for u in range(3):
                hi(c + u + 1, 0, t + 4 * u)
                if u < 2:
                    act.wait_ge(rope_done, 10 + u)
                    for j in (2 * u, 2 * u + 1):
                        act.activation(qr_hi[j][:, :], qr_eo[:, j, :], ACT.Copy).then_inc(rope_hi, 1)

            def mla_exp(par, n, tiles=range(QT)):
                for i in tiles:
                    b = (T["mla"] + i) % 4
                    act.wait_ge(nm_done, NM_DIFF + 4 * n + i + 1)
                    if i == 0 and not (isinstance(n, int) and n < 2):
                        act.wait_ge(tr_done, 4 * (HEADS + n - 1))
                    act.activation(mla_probs[par][:, OFF[i]:OFF[i] + P * (i + 1)], ps[b][:, 0:P * (i + 1)],
                                   ACT.Exp, bias=negmin[:, par, i:i + 1], scale=-1.0,
                                   accum_out=rowsum[:, par, i:i + 1]).then_inc(bank_free[b], 1)

            def mla_copy_pT(par, n):
                for j, i in enumerate(TR_ORDER):
                    act.wait_ge(tr_done, 4 * (HEADS + n) + TR_BANK[j])
                    if j == 0 and not (isinstance(n, int) and n < 2):
                        act.wait_ge(o_done, HEADS + n - 1)
                    act.activation(mla_pT[par][:, 0:i + 1, P * i:P * i + P],
                                   PT[i].rearrange("p (a b) -> p a b", a=i + 1),
                                   ACT.Copy).then_inc(ptc_done, 1)

            def mla_hi(par, n):
                act.wait_ge(o_done, HEADS + n + 1)
                x_hi(xa_hi[:, n, :], MLA_O[par][:, :], 1.0)

            def mla_step(par, n, ahead=True, behind=True):
                if behind:
                    mla_hi(1 - par, n - 1)
                mla_copy_pT(par, n)
                if ahead:
                    mla_exp(1 - par, n + 1)

            mla_exp(0, 0)
            mla_step(0, 0, behind=False)
            with act.Fori(0, HEADS // 2 - 1) as i:
                mla_step(1, 2 * i + 1)
                mla_step(0, 2 * i + 2)
            mla_step(1, HEADS - 1, ahead=False)
            mla_hi(1, HEADS - 1)

            residual("wo_b", xb_hi, gains_of("mlp1"))
            mlp("mlp1", xa_hi, xb_hi, lambda k: g_x2[:, k:k + 1], rows=True)
            c, t = C["w_in"], T["w_in"]
            for u in range(4):
                hi(c + u + 1, 0, t + (0, 2, 4, 5)[u])
            def index_relu(i):
                for hd in range(IDX_HEADS):
                    j, tt = IDX_HEADS * (i - 1) + hd, T_IDX[i] + hd
                    act.wait_ge(tile_done, tt + 1)
                    if j >= 2:
                        act.wait_ge(idx_acc, j - 1)
                    act.activation(idx_relu[:, j % 2, 0:P * (i + 1)], ps[tt % 4][:, 0:P * (i + 1)], ACT.Relu)\
                        .then_inc(bank_free[tt % 4], 1)

            def take_tokens(dst, t):
                for u in range(2):
                    tt = t + u
                    act.wait_ge(tile_done, tt + 1)
                    for half in range(2):
                        q = 2 * u + half
                        ins = act.activation(dst[:, q, :], ps[tt % 4][:, 256 * half:256 * half + 256], ACT.Copy,
                                             scale=r12[:, q:q + 1])
                    ins.then_inc(bank_free[tt % 4], 1)

            def exp2(jb):
                for i in range(QT):
                    b, j = (T_JOB[jb] + i) % 4, 4 * jb + i
                    act.wait_ge(nm_done, NM_MLA + j + 1)
                    if i == 0 and jb >= 2:
                        act.wait_ge(tr_done, 4 * (2 * HEADS + jb - 1))
                    act.activation(probs2[jb % 2][:, OFF[i]:OFF[i] + P * (i + 1)], ps[b][:, 0:P * (i + 1)],
                                   ACT.Exp, bias=negmin[:, jb % 2, i:i + 1], scale=-1.0,
                                   accum_out=rowsum[:, jb % 2, i:i + 1]).then_inc(bank_free[b], 1)

            def copy_pT2(jb):
                n = 2 * HEADS + jb
                for j, i in enumerate(TR_ORDER):
                    act.wait_ge(tr_done, 4 * n + TR_BANK[j])
                    if j == 0 and jb:
                        act.wait_ge(o_done, n)
                    act.activation(pT2[:, OFF[i]:OFF[i] + P * (i + 1)], PT[i],
                                   ACT.Copy).then_inc(ptc_done, 1)

            def pair_hi(pair):
                act.wait_ge(ot_done, HEADS + pair + 1)
                x_hi(xa_hi[:, MIX_PAIR[pair], :], OT[:, :], 1.0)

            def conv_hi(a):
                act.wait_ge(conv_out, a + 1)
                x_hi(xa_hi[:, MIX_CONV[a], :], conv_y[:, a, :], 1.0)

            act.wait_ge(r12_done, 1)
            c = C["w_in2"]
            index_relu(1)
            hi(c + 1, 0, T["w_in2"])
            index_relu(2)
            hi(c + 2, 0, T_CK + 2)
            take_tokens(cv, T_CV)
            index_relu(3)
            hi(c + 3, 0, T_CV + 2)
            hi(c + 4, 0, T_DQ + 2)
            exp2(0)
            hi(c + 5, 0, T_DK + 2)
            take_tokens(dv, T_DV)
            c = C["att2"]
            for jb in range(8):
                copy_pT2(jb)
                if jb < 7:
                    exp2(jb + 1)
                if jb >= 2 and jb % 2 == 0:
                    pair_hi((jb - 2) // 2)
                if jb % 2 == 0:
                    hi(c + jb // 2 + 1, 0, T_PROJ[jb - 1] + 1 if jb else T_DV + 2)
            for a in range(2):
                act.wait_ge(tile_done, T_POOL + a + 1)
                x_hi(xa_hi[:, MIX_POOL[a], :], ps[(T_POOL + a) % 4][:, :], g("pool_scale", a))
            conv_hi(0)
            pair_hi(3)
            conv_hi(1)

            def take_copy(dst, tt, square=None):
                act.wait_ge(tile_done, tt + 1)
                if square is not None:
                    act.activation(square, ps[tt % 4][:, :], ACT.Square).then_inc(sq_done, 1)
                act.activation(dst, ps[tt % 4][:, :], ACT.Copy).then_inc(bank_free[tt % 4], 1)

            c, t = C["w_out"], T["w_out"]
            for u in range(4):
                hi(c + u + 1, 0, t + 2 * u)
                if u == 2:
                    act.wait_ge(p_full, 16)
                    for a in range(2):
                        x_hi(p_hi[:, a, :], p_raw[:, a, :], 1.0)
                for a in range(2):
                    take_copy(branch[:, 2 * u + a, :], t + 2 * u + a, square=squares2[:, 2 * u + a, :])

            def proj(u):
                hi(C[f"proj{u}"] + 1, 0, T[f"proj{u}"])
                for a in range(4):
                    take_copy(projected[:, 4 * u + a, :], T[f"proj{u}"] + a)

            def onto_residual(gname, n0, stage):
                def part(k):
                    done, order = (res_dve, RES_DVE) if k in RES_DVE else (res_pool, RES_POOL)
                    act.wait_ge(done, len(order) * n0 + order.index(k) + 1)
                    x_hi(xb_hi[:, k, :], h[:, k, :], g(gname, k))

                def square(k):
                    act.activation(squares2[:, k, :], h[:, k, :], ACT.Square).then_inc(sq_done, 1)

                squared = 0
                for k in range(KD):
                    part(k)
                    if k in (0, 2, 5):
                        square(squared)
                        squared += 1
                hi(C[stage] + 1, 0, T[stage])
                for k in range(squared, KD):
                    square(k)

            proj(0)
            onto_residual("ffn_pre", 0, "gu0")

            def gate_up(r, n):
                c, t = C[f"gu{r}"], T[f"gu{r}"]

                def pair(i, first=False):
                    for s in range(2):
                        if not first:
                            hi(c + s + 1, 2 * i, t + 2 * s + 4 * i)
                        if first and s == 0:
                            hi(c + 2, 0, t + 2)
                        act.wait_ge(bank_free[(t + 2 * s) % 4], (t + 2 * s) // 4 + 1 + i)
                        act.activation(silu_t[:, s, :], gate_t[:, s, :], ACT.Silu).then_inc(silu_done, 1)
                        act.wait_ge(hid_sq, HID2 + 8 * r + 2 * i + s + 1)
                        act.activation(xa_hi[:, 2 * i + s, :], hid_t[:, s, :], ACT.Copy).then_inc(hid_hi, 1)

                pair(0, first=(r == 0))
                with act.Fori(1, n // 2) as i:
                    pair(i)

            def down(r):
                c, t = C[f"dn{r}"], T[f"dn{r}"]
                for u in range(4):
                    hi(c + u + 1, 0, t + 2 * u)
                    for a in range(2):
                        if r == 0:
                            take_copy(branch[:, 2 * u + a, :], t + 2 * u + a)
                        elif r == len(GU_TILES) - 1:
                            bank_out(t + 2 * u + a)
                            act.activation(squares2[:, 2 * u + a, :], branch[:, 2 * u + a, :], ACT.Square).then_inc(sq_done, 1)

            for r, n in enumerate(GU_TILES):
                gate_up(r, n)
                down(r)
            proj(1)
            onto_residual("ple", 1, "ple")

            c, t = C["ple"], T["ple"]
            hi(c + 2, 0, t + 2)
            for u in range(4):
                if u == 1:
                    hi(c + 3, 0, t + 4)
                for a in range(2):
                    k = 2 * u + a
                    bank_out(t + k)
                    if u:
                        act.wait_ge(gated_done, k - 1)
                    act.activation(silu_t[:, a, :], gate_t[:, a, :], ACT.Sigmoid).then_inc(silu_done, 1)

        @block.vector
        def _(dve):
            def lo(c, slot):
                dve.wait_ge(whi_done, c + 1)
                dve.tensor_tensor(wlo[slot][:, :], raw[slot][:, :], whi[slot][:, :].bitcast(F32),
                                  ALU.subtract).then_inc(wlo_done, 1)

            def x_lo(dst, src, scale, dst_hi, n):
                dve.wait_ge(xh_done, n + 1)
                dve.scalar_tensor_tensor(out=dst, in0=src, scalar=scale, in1=dst_hi.bitcast(F32),
                                         op0=ALU.mult, op1=ALU.subtract).then_inc(xl_done, 1)

            def mean_square(n, dim):
                dve.wait_ge(stat_done, STATS[n] + 1)
                dve.tensor_scalar(ms_t[:, 4 * n:4 * n + 4], STAT[:, 0:QT], 1.0 / dim, EPS, ALU.mult, ALU.add).then_inc(ms_done, 1)

            def take_rstd(n, dst=None):
                dve.wait_ge(bc_done, n + 1)
                dve.tensor_copy((rstd_f if dst is None else dst)[:, :], BC[:, :]).then_inc(rstd_f_done, 1)
                dve.wait_ge(rstd_f_done, n + 1 - (n > 8) - (n > 10))

            def tile_ready(t, per=0, i=0):
                dve.wait_ge(tile_done, t + 1 + per * i)

            dve.memset(zeros[:, :], 0.0).then_inc(zeros_done, 1)
            dve.memset(ones[:, :], 1.0)
            dve.memset(half_neg[:, :], -0.5).then_inc(dve_const, 1)
            for part, done, made in ((FIRST, first_hi, first_lo), (SECOND, whi_done, wlo_done)):
                dve.wait_ge(done, 1)
                dve.tensor_tensor(wlo[0][:, part], raw[0][:, part], whi[0][:, part].bitcast(F32), ALU.subtract).then_inc(made, 1)
            dve.wait_ge(gain_loaded, 16)
            for k in range(KD):
                x_lo(xa_lo[:, k, :], h[:, k, :], g("attn0", k), xa_hi[:, k, :], X["qkv"] + k)
            lo(1, 1)
            dve.wait_ge(const_loaded, 16 * len(consts))
            for j in range(2):
                dve.tensor_tensor_reduce(out=lam_in[:, 2 * j, :], in0=lam_in[:, 2 * j, :],
                                         in1=lam_in[:, 2 * j + 1, :], scale=1.0, scalar=0.0, op0=ALU.mult,
                                         op1=ALU.add, accum_out=lam_ab[:, j:j + 1]).then_inc(lam_done, 1)
            dve.wait_ge(lam_exp, 1)
            dve.scalar_tensor_tensor(out=neg_lam[:, :], in0=lam_ab[:, 3:4], scalar=-LAMBDA_INIT, in1=lam_ab[:, 2:3],
                                     op0=ALU.add, op1=ALU.subtract).then_inc(dve_const, 1)
            dve.tensor_tensor(g_x2[:, :], gains_all("final"), gains_all("mix_pre"), ALU.mult).then_inc(dve_const, 1)
            dve.tensor_scalar(gsub[:, :], g("subln", 0), 1.0 - LAMBDA_INIT, None, ALU.mult).then_inc(dve_const, 1)
            dve.tensor_copy(ident_b[:, :], ident[:, :])
            dve.tensor_copy(mask_b[:, :], mask[:, :]).then_inc(dve_const, 1)

            def rope(t, dst1, dst2, cos_n, sin_n, rope_tmp, n_before, per=0, i=0):
                be, bo = ps[t % 4], ps[(t + 1) % 4]
                tile_ready(t + 1, per, i)
                if not (isinstance(n_before, int) and n_before < 1):
                    dve.wait_ge(rope_done, n_before)
                dve.tensor_tensor(dst1, be[:, :], cos_n[:, :], ALU.mult)
                dve.tensor_tensor(rope_tmp[:, 1, :], be[:, :], sin_n[:, :], ALU.mult).then_inc(bank_free[t % 4], 1)
                dve.tensor_tensor(rope_tmp[:, 0, :], bo[:, :], sin_n[:, :], ALU.mult)
                dve.tensor_tensor(dst2, bo[:, :], cos_n[:, :], ALU.mult).then_inc(bank_free[(t + 1) % 4], 1)

            c, t = C["qk"], T["qk"]
            mean_square(0, D)
            lo(c + 2, c % 2)
            take_rstd(0)
            def tables(cos_n, sin_n, scale, n_before):
                for dst, src in ((cos_n, cos_t), (sin_n, sin_t)):
                    dve.scalar_tensor_tensor(out=dst[:, :], in0=src[:, :], scalar=scale, in1=rstd_f[:, :],
                                             op0=ALU.mult, op1=ALU.mult).then_inc(table_done, 1)
                dve.wait_ge(table_done, n_before + 2)

            tables(cq, sq_, -DIFF_SCALE, 0)
            rope(t, qk_raw[0][:, 0, 0, :], qk_raw[1][:, 0, 0, :], cq, sq_, rope_tmp, 0)
            tables(ck, sk, 1.0, 2)
            rope(t + 2, qk_raw[0][:, 0, 3, :], qk_raw[1][:, 0, 3, :], ck, sk, rope_tmp, 1)
            def split_lo_part(i, s):
                dve.wait_ge(split_hi, 4 * i + 2 * s + 2)
                for hf in range(2):
                    dve.tensor_tensor(qk_split[hf][:, i, 3 * s, :], qk_raw[hf][:, i, 3 * s, :],
                                      qk_split[hf][:, i, Q_HI + s, :].bitcast(F32), ALU.subtract).then_inc(split_lo, 1)

            with dve.Fori(1, 4) as i:
                for s in range(2):
                    lo(c + s + 1 + 2 * i, (c + s + 1) % 2)
                    rope(t + 2 * s, qk_raw[0][:, i, 3 * s, :], qk_raw[1][:, i, 3 * s, :], (cq, ck)[s], (sq_, sk)[s],
                         rope_tmp, 2 * i + s, per=4, i=i)
                    split_lo_part(i - 1, s)

            c = C["v"]
            lo(c + 1, (c + 1) % 2)
            for s in range(2):
                split_lo_part(3, s)
            lo(c + 2, c % 2)
            with dve.Fori(1, 2) as i:
                for s in range(2):
                    lo(c + s + 1 + 2 * i, (c + s + 1) % 2)

            def diff_min(par, half, comp):
                for i in range(QT):
                    j = 4 * comp + i
                    b = ps[(T["diff"] + 8 * par + j) % 4]
                    tile_ready(T["diff"] + 8 * par + j, 16, half)
                    dve.tensor_reduce(negmin[:, par, j:j + 1], b[:, 0:P * (i + 1)], AX.X, ALU.min).then_inc(nm_done, 1)

            def diff_coefs(par, half):
                n = 2 * half + par
                s1, s2 = rowsum[:, par, 0:QT], rowsum[:, par, QT:2 * QT]
                b = (T["diff"] + 8 * par + 7) % 4
                dve.wait_ge(bank_free[b], (T["diff"] + 8 * par + 7) // 4 + 1 + 4 * half)
                dve.reciprocal(rinv[:, par, :], s2).then_inc(ri_done, 1)
                dve.wait_ge(ri_done, n + 1)
                dve.scalar_tensor_tensor(out=coef2[:, par, :], in0=rinv[:, par, :], scalar=neg_lam[:, 0:1], in1=s1,
                                         op0=ALU.mult, op1=ALU.mult).then_inc(rc_done, 1)
                dve.scalar_tensor_tensor(out=eps_o[:, n, :], in0=s1, scalar=SUBLN_EPS, in1=s1,
                                         op0=ALU.mult, op1=ALU.mult)
                dve.wait_ge(rc_done, n + 1)

            def diff_combine(par, half):
                for i in TR_ORDER:
                    w = slice(OFF[i], OFF[i] + P * (i + 1))
                    dve.scalar_tensor_tensor(out=probs[par][:, 0, w], in0=probs[par][:, 1, w],
                                             scalar=coef2[:, par, i:i + 1], in1=probs[par][:, 0, w],
                                             op0=ALU.mult, op1=ALU.add).then_inc(a_done, 1)

            def diff_mean_square(n):
                dve.wait_ge(sqo_done, n + 1)
                dve.tensor_reduce(o_ss[:, :], o_sq[:, :].rearrange("p (a b) -> p a b", a=QT), AX.X, ALU.add)\
                   .then_inc(oss_done, 1)
                dve.wait_ge(oss_done, n + 1)
                dve.scalar_tensor_tensor(out=o_ms[:, :], in0=o_ss[:, :], scalar=1.0 / P, in1=eps_o[:, n, :],
                                         op0=ALU.mult, op1=ALU.add).then_inc(oms_done, 1)

            def head_lo(dst, dst_hi, n, x0, scale):
                dve.wait_ge(xh_done, x0 + n + 1)
                dve.scalar_tensor_tensor(out=dst[:, n, :], in0=OT[:, :], scalar=scale,
                                         in1=dst_hi[:, n, :].bitcast(F32),
                                         op0=ALU.mult, op1=ALU.subtract).then_inc(xl_done, 1)

            def diff_step(par, half, first=0, ahead=True):
                n = 2 * half + par
                diff_coefs(par, half)
                if ahead:
                    diff_min(1 - par, half + par, 0)
                diff_combine(par, half)
                if first >= 3:
                    head_lo(xb_lo, xb_hi, n - 3, X["diff_o"], gsub[:, 0:1])
                if first >= 2:
                    diff_mean_square(n - 2)
                if ahead:
                    diff_min(1 - par, half + par, 1)

            dve.wait_ge(dve_const, 4)
            diff_min(0, 0, 0)
            diff_min(0, 0, 1)
            for n in range(3):
                diff_step(n % 2, n // 2, first=n)
            with dve.Fori(1, HEADS // 2 - 1) as i:
                diff_step(1, i, first=3)
                diff_step(0, i + 1, first=3)
            diff_step(1, HEADS // 2 - 1, first=3, ahead=False)
            diff_mean_square(HEADS - 2)
            head_lo(xb_lo, xb_hi, HEADS - 3, X["diff_o"], gsub[:, 0:1])
            diff_mean_square(HEADS - 1)
            for n in (HEADS - 2, HEADS - 1):
                head_lo(xb_lo, xb_hi, n, X["diff_o"], gsub[:, 0:1])

            def residual(stage, dst, dst_hi, gname, x0):
                c, t = C[stage], T[stage]
                for u in range(4):
                    lo(c + u + 1, (c + u + 1) % 2)
                    for a in range(2):
                        add_residual(2 * u + a, t + 2 * u + a)
                    for a in range(2):
                        k = 2 * u + a
                        x_lo(dst[:, k, :], h[:, k, :], gname(k), dst_hi[:, k, :], x0 + k)

            def add_residual(k, t, per=0, i=0):
                tile_ready(t, per, i)
                dve.tensor_tensor(h[:, k, :], ps[t % 4][:, :], h[:, k, :], ALU.add).then_inc(bank_free[t % 4], 1)

            def mlp(stage, norm, dst, dst_hi, gname, x0, hid0):
                c, t = C[stage], T[stage]

                def one_round(r, first, last):
                    for u in range(4):
                        if not (first and u == 1):
                            lo(c + u + 1 + 8 * r, (c + u + 1) % 2)
                        if first and u == 0:
                            lo(c + 2, c % 2)
                            mean_square(norm, D)
                            take_rstd(norm)
                        for a in range(2):
                            tt = t + 2 * u + a
                            tile_ready(tt, 16, r)
                            if not (first and u == 0 and hid0 == 0):
                                dve.wait_ge(hid_lo, hid0 + 8 * r + 2 * u + a - 1)
                            dve.scalar_tensor_tensor(out=u_tmp[:, a, :], in0=ps[tt % 4][:, :], scalar=0.0,
                                                     in1=rstd_f[:, :], op0=ALU.max, op1=ALU.mult)\
                               .then_inc(bank_free[tt % 4], 1)
                    for d in range(4):
                        lo(c + d + 5 + 8 * r, (c + d + 5) % 2)
                        for a in range(2):
                            add_residual(2 * d + a, t + 8 + 2 * d + a, 16, r)
                        if last:
                            for a in range(2):
                                k = 2 * d + a
                                x_lo(dst[:, k, :], h[:, k, :], gname(k), dst_hi[:, k, :], x0 + k)

                one_round(0, True, False)
                with dve.Fori(1, ROUNDS - 1) as r:
                    one_round(r, False, False)
                one_round(ROUNDS - 1, False, True)

            residual("wo_a", xa_lo, xa_hi, gains_of("mlp0"), X["mlp0"])
            mlp("mlp0", 1, xa_lo, xa_hi, gains_of("kv_in"), X["dkv"], 0)
            c, t = C["dkv"], T["dkv"]

            def take_scaled(dst, tt, scale=None):
                tile_ready(tt)
                if scale is None:
                    ins = dve.tensor_tensor(dst, ps[tt % 4][:, :], rstd_f[:, :], ALU.mult)
                else:
                    ins = dve.scalar_tensor_tensor(out=dst, in0=ps[tt % 4][:, :], scalar=scale, in1=rstd_f[:, :],
                                                   op0=ALU.mult, op1=ALU.mult)
                ins.then_inc(bank_free[tt % 4], 1)

            def rope_tables(n_before, scale):
                for j, src in enumerate((cos_t, sin_t)):
                    dve.scalar_tensor_tensor(out=table2[:, j, :], in0=src[:, :], scalar=scale, in1=rstd_f[:, :],
                                             op0=ALU.mult, op1=ALU.mult).then_inc(table_done, 1)
                dve.wait_ge(table_done, n_before + 2)

            lo(c + 1, (c + 1) % 2)
            for k in range(KD):
                x_lo(xb_lo[:, k, :], h[:, k, :], g("attn1", k), xb_hi[:, k, :], X["dq"] + k)
            mean_square(2, D)
            take_rstd(2)
            for a in range(2):
                take_scaled(ckv[:, a, :], t + a)
            lo(c + 2, c % 2)
            for a in range(2):
                x_lo(ckv_lo[:, a, :], ckv[:, a, :], g("kv", a), ckv_hi[:, a, :], X["ckv"] + a)
            rope_tables(4, 1.0)
            rope(t + 2, k_eo[:, 0, :], k_eo[:, 1, :], table2[:, 0, :], table2[:, 1, :], rope_tmp2, 8)
            lo(c + 3, (c + 1) % 2)
            dve.wait_ge(rope_hi, 1)
            dve.tensor_tensor(k_eo_lo[0:32, :, :], k_eo[0:32, :, :], k_eo_hi[0:32, :, :].bitcast(F32), ALU.subtract)\
               .then_inc(rope_lo, 1)
            for a in range(2):
                take_scaled(cq_raw[:, a, :], t + 4 + a)
            lo(c + 4, c % 2)
            take_scaled(cq_raw[:, 2, :], t + 6)
            for a in range(3):
                x_lo(cq_lo[:, a, :], cq_raw[:, a, :], g("q", a), cq_hi[:, a, :], X["cq"] + a)
            c, t = C["ukv"], T["ukv"]
            mean_square(3, 256)
            lo(c + 1, (c + 1) % 2)
            take_rstd(3)
            for a in range(8):
                take_scaled(k_nope[:, a, :], t + a)
            mean_square(4, 384)
            lo(c + 2, c % 2)
            take_rstd(4)
            c, t = C["uq"], T["uq"]
            rope_tables(6, -MLA_SCALE)
            lo(c + 1, (c + 1) % 2)
            for j in range(2):
                rope(t + 2 * j, qr_eo[:, 2 * j, :], qr_eo[:, 2 * j + 1, :], table2[:, 0, :], table2[:, 1, :],
                     rope_tmp2, 9 + j)
            for u in range(2):
                lo(c + u + 2, (c + u + 2) % 2)
                for a in range(4):
                    take_scaled(q_nope[:, 4 * u + a, :], t + 4 + 4 * u + a, -MLA_SCALE)
                for j in range(4 if u == 0 else 0):
                    dve.wait_ge(rope_hi, j + 2)
                    dve.tensor_tensor(qr_lo[:, j, :], qr_eo[:, j, :], qr_hi[j][:, :].bitcast(F32), ALU.subtract)\
                       .then_inc(rope_lo, 1)

            def mla_min(par, n, tiles):
                for i in tiles:
                    b = ps[(T["mla"] + i) % 4]
                    tile_ready(T["mla"] + i, 4, n)
                    dve.tensor_reduce(negmin[:, par, i:i + 1], b[:, 0:P * (i + 1)], AX.X, ALU.min)\
                       .then_inc(nm_done, 1)

            def mla_normalise(par, n):
                b = (T["mla"] + 3) % 4
                dve.wait_ge(bank_free[b], (T["mla"] + 3) // 4 + 1 + n)
                dve.reciprocal(rinv[:, par, 0:QT], rowsum[:, par, 0:QT]).then_inc(ri_done, 1)
                dve.wait_ge(ri_done, HEADS + n + 1)
                for i in TR_ORDER:
                    row = mla_probs[par][:, OFF[i]:OFF[i] + P * (i + 1)]
                    dve.tensor_scalar(row, row, rinv[:, par, i:i + 1], None, ALU.mult).then_inc(pn_done, 1)

            def mla_lo(par, n):
                x_lo(xa_lo[:, n, :], MLA_O[par][:, :], 1.0, xa_hi[:, n, :], X["mla_o"] + n)

            def mla_step(par, n, ahead=True, behind=True):
                mla_normalise(par, n)
                if ahead:
                    mla_min(1 - par, n + 1, (0, 1))
                if behind:
                    mla_lo(1 - par, n - 1)
                if ahead:
                    mla_min(1 - par, n + 1, (2, 3))

            mla_min(0, 0, range(QT))
            mla_step(0, 0, behind=False)
            with dve.Fori(0, HEADS // 2 - 1) as i:
                mla_step(1, 2 * i + 1)
                mla_step(0, 2 * i + 2)
            mla_step(1, HEADS - 1, ahead=False)
            mla_lo(1, HEADS - 1)

            residual("wo_b", xb_lo, xb_hi, gains_of("mlp1"), X["mlp1"])
            mlp("mlp1", 5, xb_lo, xb_hi, lambda k: g_x2[:, k:k + 1], X["w_in"], 8 * ROUNDS)
            c, t = C["w_in"], T["w_in"]
            for j in (1, 2):
                lo(c + j, (c + j) % 2)
            pairs = STAT[:, 0:2 * QT].rearrange("p (q b) -> p q b", b=2)
            dve.wait_ge(stat_done, STATS[6] + 1)
            dve.tensor_scalar(ms_t[:, 24:28], pairs[:, :, 0], 1.0 / D, EPS, ALU.mult, ALU.add).then_inc(ms_done, 1)
            dve.wait_ge(rstd_t_done, 7)
            dve.tensor_tensor(r1_sq[:, :], rstd_t[:, 24:28], rstd_t[:, 24:28], ALU.mult).then_inc(small_done, 1)
            dve.wait_ge(small_done, 1)
            dve.scalar_tensor_tensor(out=r1_ms[:, :], in0=pairs[:, :, 1], scalar=1.0 / D, in1=r1_sq[:, :],
                                     op0=ALU.mult, op1=ALU.mult).then_inc(small_done, 1)
            dve.wait_ge(small_done, 2)
            dve.tensor_scalar(ms_t[:, 28:32], r1_ms[:, :], EPS, None, ALU.add).then_inc(ms_done, 1)
            dve.wait_ge(rstd_t_done, 8)
            dve.tensor_tensor(r12[:, :], rstd_t[:, 24:28], rstd_t[:, 28:32], ALU.mult).then_inc(r12_done, 1)
            take_rstd(6)
            for a in range(2):
                take_scaled(iq[:, a, :], t + a)
            lo(c + 3, (c + 1) % 2)
            take_rstd(7, r1_f)
            for a in range(2):
                take_scaled(iq[:, 2 + a, :], t + 2 + a)
            dve.wait_ge(rows_stored, 16)
            take_scaled(ik_iw[:, :], t + 4)
            dve.wait_ge(nbias_full, 16)
            dve.tensor_tensor(nbias[:, :, P:2 * P], nbias[:, :, P:2 * P],
                              mask[:, :].unsqueeze(1).to_broadcast([P, HEADS, P]), ALU.add).then_inc(nb_masked, 1)
            for a in range(2):
                take_scaled(cq2[:, a, :], t + 5 + a, -HEAD_SCALE)
            dve.wait_ge(iwt_done, 1)
            dve.tensor_scalar(iw[:, :, :].rearrange("p a b -> p (a b)"), STAT[:, 0:IDX_HEADS * QT], IDX_SCALE, None,
                              ALU.mult).then_inc(small_done, 1)
            dve.wait_ge(small_done, 3)
            def index_sum(i):
                row = idx_score[:, IDX_OFF[i]:IDX_OFF[i] + P * (i + 1)]
                for hd in range(IDX_HEADS):
                    j, tt = IDX_HEADS * (i - 1) + hd, T_IDX[i] + hd
                    src = idx_relu[:, j % 2, 0:P * (i + 1)]
                    dve.wait_ge(bank_free[tt % 4], tt // 4 + 1)
                    if hd == 0:
                        dve.tensor_scalar(row, src, iw[:, i, 0:1], None, ALU.mult).then_inc(idx_acc, 1)
                    else:
                        dve.wait_ge(idx_acc, j)
                        dve.scalar_tensor_tensor(out=row, in0=src, scalar=iw[:, i, hd:hd + 1], in1=row,
                                                 op0=ALU.mult, op1=ALU.add).then_inc(idx_acc, 1)
                diag = idx_score[:, IDX_OFF[i] + P * i:IDX_OFF[i] + P * (i + 1)]
                dve.wait_ge(idx_acc, IDX_HEADS * i)
                dve.tensor_tensor(diag, diag, mask[:, :], ALU.subtract).then_inc(diag_done, 1)
                dve.wait_ge(diag_done, i)

            def top_rounds(first, last):
                for n in range(first, last):
                    i, rnd = 1 + n // ROUNDS_TOP, n % ROUNDS_TOP
                    row = idx_score[:, IDX_OFF[i]:IDX_OFF[i] + P * (i + 1)]
                    if n:
                        dve.wait_ge(top_done, 2 * n)
                    dve.max(top8[:, :], row).then_inc(top_done, 1)
                    dve.wait_ge(top_done, 2 * n + 1)
                    dve.match_replace(row, top8[:, :], row, TAKEN).then_inc(top_done, 1)
                    if rnd == ROUNDS_TOP - 1:
                        dve.wait_ge(top_done, 2 * n + 2)
                        dve.tensor_scalar(sel[:, IDX_OFF[i]:IDX_OFF[i] + P * (i + 1)], row, TAKEN / 2, BIG,
                                          ALU.is_gt, ALU.mult).then_inc(sel_done, 1)

            def min2(jb):
                head = NB_HEAD[jb]
                for i in range(QT):
                    tt, j = T_JOB[jb] + i, 4 * jb + i
                    b, w0 = ps[tt % 4], P * max(i - 1, 0)
                    tile_ready(tt)
                    dve.tensor_tensor(b[:, w0:P * (i + 1)], b[:, w0:P * (i + 1)],
                                      nbias[:, head, 2 * P - (P * (i + 1) - w0):2 * P], ALU.add).then_inc(mask_done, 1)
                    dve.wait_ge(mask_done, j + 1)
                    dve.tensor_reduce(negmin[:, jb % 2, i:i + 1], b[:, 0:P * (i + 1)], AX.X, ALU.min)\
                       .then_inc(nm_done, 1)

            def inverse2(jb):
                tt = T_JOB[jb] + 3
                dve.wait_ge(bank_free[tt % 4], tt // 4 + 1)
                dve.reciprocal(rinv[:, jb % 2, 0:QT], rowsum[:, jb % 2, 0:QT]).then_inc(ri_done, 1)

            def normalise2(jb):
                dve.wait_ge(o_done, 2 * HEADS + jb + 1)
                dve.wait_ge(ri_done, 2 * HEADS + jb + 1)
                pair = jb // 2
                if jb % 2 == 0 and pair >= 2:
                    dve.wait_ge(ot_done, HEADS + pair - 1)
                dve.tensor_tensor(o2[pair % 2][:, :, 64 * (jb % 2):64 * (jb % 2) + 64],
                                  O_PS[:, 0:256].rearrange("p (a b) -> p a b", a=QT),
                                  rinv[:, jb % 2, 0:QT].unsqueeze(2).to_broadcast([P, QT, 64]), ALU.mult)\
                   .then_inc(on_done, 1)

            def mix_lo(n, src, scale):
                x_lo(xa_lo[:, n, :], src, scale, xa_hi[:, n, :], X["mix"] + n)

            def convolve(a):
                x, y = conv_in[:, a, :], conv_y[:, a, :]
                dve.wait_ge(conv_x, a + 1)
                dve.tensor_scalar(y, x, g("conv", 4 + a), None, ALU.mult).then_inc(conv_step, 1)
                for tap in (1, 2):
                    dve.wait_ge(conv_step, 3 * a + tap)
                    dve.scalar_tensor_tensor(out=y[:, tap:S], in0=x[:, 0:S - tap],
                                             scalar=g("conv", 2 * (2 - tap) + a), in1=y[:, tap:S],
                                             op0=ALU.mult, op1=ALU.add).then_inc(conv_step, 1)

            def pool_mean(j):
                a, rows, src, w = POOL_GROUPS[j]
                s_ = pool_s[src]
                dve.wait_ge(pool_s_done, POOL_STEPS[j])
                dve.tensor_tensor(s_[rows, PAD:2 * PAD], s_[rows, PAD:2 * PAD], pool_fix[rows, a, :], ALU.mult)\
                    .then_inc(pool_fix_done, 1)
                dve.wait_ge(pool_fix_done, j + 1)
                dve.scalar_tensor_tensor(out=pool_d[rows, a, :], in0=s_[rows, PAD:PAD + S], scalar=1.0 / w,
                                         in1=pool_v[rows, a, PAD:PAD + S], op0=ALU.mult, op1=ALU.subtract)\
                    .then_inc(pool_d_done, 1)

            n_rounds = ROUNDS_TOP * (QT - 1)
            top_at = [0, 10, 20, 28, 33, 40, 43, 46, n_rounds]
            index_sum(1)
            top_rounds(top_at[0], top_at[1])
            for a in range(2):
                take_scaled(ck2[:, a, :], T_CK + a)
            index_sum(2)
            top_rounds(top_at[1], top_at[2])
            index_sum(3)
            top_rounds(top_at[2], top_at[3])
            for a in range(2):
                take_scaled(dq2[:, a, :], T_DQ + a, -HEAD_SCALE)
            dve.wait_ge(nb_masked, 1)
            top_rounds(top_at[3], top_at[4])
            for a in range(2):
                take_scaled(dk2[:, a, :], T_DK + a)
            min2(0)
            top_rounds(top_at[4], top_at[5])
            c = C["att2"]
            for jb in range(8):
                a = jb % 2
                inverse2(jb)
                if jb < 7:
                    min2(jb + 1)
                normalise2(jb)
                if jb < 3:
                    top_rounds(top_at[5 + jb], top_at[6 + jb])
                elif jb in (4, 5):
                    convolve(a)
                elif jb == 6:
                    for j in range(4):
                        pool_mean(j)
                if jb % 2 == 0 and jb:
                    if jb == 2:
                        dve.wait_ge(wlo_done, POOL_LO[1])
                    lo(c + jb // 2 + 1, (c + jb // 2 + 1) % 2)
                if jb >= 2 and jb % 2 == 0:
                    mix_lo(MIX_PAIR[(jb - 2) // 2], OT[:, :], 1.0)
                if jb < 2:
                    take_scaled(conv_in[:, a, :], T_PROJ[jb])
                elif jb < 4:
                    take_scaled(conv_gate[:, a, :], T_PROJ[jb])
                elif jb < 6:
                    take_scaled(pool_v[:, a, PAD:PAD + S], T_PROJ[jb])
                    if jb == 4:
                        dve.memset(pool_v[:, :, 0:PAD], 0.0).then_inc(pool_zero, 1)
                elif jb == 6:
                    take_scaled(conv_gate[:, 0, :], T_PROJ[jb])
            for a in range(2):
                mix_lo(MIX_POOL[a], ps[(T_POOL + a) % 4][:, :], g("pool_scale", a))
                dve.wait_ge(xl_done, X["mix"] + MIX_POOL[a] + 1)
                dve.sem_inc(bank_free[(T_POOL + a) % 4], 1)
            take_scaled(conv_gate[:, 1, :], T_PROJ[7])
            mix_lo(MIX_CONV[0], conv_y[:, 0, :], 1.0)
            mix_lo(MIX_PAIR[3], OT[:, :], 1.0)
            mix_lo(MIX_CONV[1], conv_y[:, 1, :], 1.0)
            for k in range(KD):
                ins = dve.scalar_tensor_tensor(out=h[:, k, :], in0=h[:, k, :], scalar=g("final", k), in1=r1_f[:, :],
                                               op0=ALU.mult, op1=ALU.mult)
            ins.then_inc(x2_done, 1)

            c, t = C["w_out"], T["w_out"]
            for u in range(4):
                lo(c + u + 1, (c + u + 1) % 2)
            for a in range(2):
                x_lo(p_lo[:, a, :], p_raw[:, a, :], 1.0, p_hi[:, a, :], X["p"] + a)

            def onto_residual(n, gname, gnext, x0, n0, c_next):
                mean_square(n, D)
                lo(c_next, c_next % 2)
                dve.wait_ge(bc_done, n + 1)

                def add(k):
                    dve.wait_ge(branch_done, KD * n0 + k + 1)
                    dve.tensor_tensor(h[:, k, :], h[:, k, :], branch[:, k, :], ALU.add).then_inc(res_dve, 1)

                for k in range(KD):
                    dve.scalar_tensor_tensor(out=branch[:, k, :], in0=branch[:, k, :], scalar=g(gname, k),
                                             in1=BC[:, :], op0=ALU.mult, op1=ALU.mult).then_inc(branch_done, 1)
                    if k in (0, 2, 7):
                        add(k)
                    elif k == 5:
                        add(4)
                for k in range(KD):
                    x_lo(xb_lo[:, k, :], h[:, k, :], g(gnext, k), xb_hi[:, k, :], x0 + k)

            dve.wait_ge(x2_done, 1)
            onto_residual(8, "mix_post", "ffn_pre", X["ffn"], 0, C["proj0"] + 1)

            def gate_up(r, n, first):
                c, t = C[f"gu{r}"], T[f"gu{r}"]

                def pair(i):
                    for s in range(2):
                        j = HID2 + 8 * r + 2 * i + s
                        if not (first and isinstance(i, int) and s == 1):
                            lo(c + s + 1 + 2 * i, (c + s + 1) % 2)
                        if first and isinstance(i, int) and s == 0:
                            lo(c + 2, c % 2)
                            mean_square(9, D)
                            take_rstd(9)
                        tt = t + 2 * s
                        tile_ready(tt, 4, i)
                        if not (first and isinstance(i, int)):
                            dve.wait_ge(hid_sq, j - 1)
                        dve.tensor_tensor(gate_t[:, s, :], ps[tt % 4][:, :], rstd_f[:, :], ALU.mult)\
                            .then_inc(bank_free[tt % 4], 1)
                        tile_ready(tt + 1, 4, i)
                        dve.tensor_tensor(up_t[:, s, :], ps[(tt + 1) % 4][:, :], rstd_f[:, :], ALU.mult)\
                            .then_inc(bank_free[(tt + 1) % 4], 1)

                pair(0)
                with dve.Fori(1, n // 2) as i:
                    pair(i)

            def down(r):
                c, t = C[f"dn{r}"], T[f"dn{r}"]
                for u in range(4):
                    lo(c + u + 1, (c + u + 1) % 2)
                    for a in range(2):
                        k, tt = 2 * u + a, t + 2 * u + a
                        if r == 0:
                            continue
                        tile_ready(tt)
                        if r == 1:
                            b0 = T["dn0"] + k
                            dve.wait_ge(bank_free[b0 % 4], b0 // 4 + 1)
                        dve.tensor_tensor(branch[:, k, :], ps[tt % 4][:, :], branch[:, k, :], ALU.add)\
                            .then_inc(bank_free[tt % 4], 1)

            for r, n in enumerate(GU_TILES):
                gate_up(r, n, r == 0)
                down(r)
            onto_residual(10, "ffn_post", "ple", X["ple"], 1, C["proj1"] + 1)

            c, t = C["ple"], T["ple"]

            def add_gated(k):
                dve.wait_ge(gated_done, k + 1)
                dve.tensor_tensor(h[:, k, :], h[:, k, :], projected[:, k, :], ALU.add).then_inc(y_done, 1)

            for j in (1, 2):
                lo(c + j, (c + j) % 2)
            mean_square(11, D)
            take_rstd(11)
            for u in range(4):
                for a in range(2):
                    k, tt = 2 * u + a, t + 2 * u + a
                    tile_ready(tt)
                    if u:
                        dve.wait_ge(silu_done, N_SILU + k - 1)
                    dve.tensor_tensor(gate_t[:, a, :], ps[tt % 4][:, :], rstd_f[:, :], ALU.mult)\
                        .then_inc(bank_free[tt % 4], 1)
                if u == 1:
                    lo(c + 3, (c + 3) % 2)
                if u:
                    for a in range(2):
                        add_gated(2 * u - 2 + a)
            for k in (KD - 2, KD - 1):
                dve.wait_ge(silu_done, N_SILU + k + 1)
                dve.tensor_tensor(projected[:, k, :], projected[:, k, :], silu_t[:, k % 2, :], ALU.mult)\
                    .then_inc(gated_done, 1)
                add_gated(k)

        @block.gpsimd
        def _(pool):
            def square_tile(src, k, n):
                if k == 0:
                    pool.tensor_tensor(ssq[:, :], src, src, ALU.mult).then_inc(sq_done, 1)
                else:
                    if k >= 2:
                        pool.wait_ge(ssq_done, SSQ[n] + k - 1)
                    pool.tensor_tensor(sq_tmp[:, :], src, src, ALU.mult).then_inc(sq_done, 1)
                    pool.wait_ge(sq_done, SQ[n] + k + 1)
                    pool.tensor_tensor(ssq[:, :], ssq[:, :], sq_tmp[:, :], ALU.add).then_inc(ssq_done, 1)

            def rstd(n):
                pool.wait_ge(ms_done, n + 1)
                pool.tensor_tensor(rstd_t[:, 4 * n:4 * n + 4], ms_t[:, 4 * n:4 * n + 4], half_neg[:, :], ALU.pow).then_inc(rstd_t_done, 1)

            def add_squares(squares, n):
                for k in range(1, KD):
                    pool.wait_ge(sq_done, SQ[n] + k + 1)
                    if k >= 2:
                        pool.wait_ge(ssq_done, SSQ[n] + k - 1)
                    pool.tensor_tensor(ssq[:, :], squares[:, 0, :] if k == 1 else ssq[:, :], squares[:, k, :],
                                       ALU.add).then_inc(ssq_done, 1)
                rstd(n)

            pool.wait_ge(dve_const, 1)
            add_squares(squares0, 0)

            def rope(t, dst1, dst2, rope_tmp, per=0, i=0):
                b = (t + 1) % 4
                pool.wait_ge(bank_free[b], (t + 1) // 4 + 1 + (per // 4) * i)
                pool.tensor_tensor(dst1, dst1, rope_tmp[:, 0, :], ALU.subtract)
                pool.tensor_tensor(dst2, dst2, rope_tmp[:, 1, :], ALU.add).then_inc(rope_done, 1)

            with pool.Fori(0, 4) as i:
                for s in range(2):
                    rope(T["qk"] + 2 * s, qk_raw[0][:, i, 3 * s, :], qk_raw[1][:, i, 3 * s, :], rope_tmp, 4, i)

            def diff_norm(par, n, square=True):
                pool.wait_ge(oc_done, n + 1)
                if square:
                    o = o_raw[par][:, :, :].rearrange("p a b -> p (a b)")
                    pool.tensor_tensor(o_sq[:, :], o, o, ALU.mult).then_inc(sqo_done, 1)
                else:
                    pool.wait_ge(on_done, n)
                pool.wait_ge(oms_done, n + 1)
                pool.tensor_tensor(o_rstd[:, :], o_ms[:, :], half_neg[:, :], ALU.pow).then_inc(orstd_done, 1)
                pool.wait_ge(orstd_done, n + 1)
                pool.tensor_tensor(o_raw[par][:, :, :], o_raw[par][:, :, :],
                                   o_rstd[:, :].unsqueeze(2).to_broadcast([P, QT, P]), ALU.mult).then_inc(on_done, 1)

            with pool.Fori(0, HEADS // 2 - 1) as half:
                for par in range(2):
                    diff_norm(par, 2 * half + par)
            for par in range(2):
                diff_norm(par, HEADS - 2 + par, square=False)

            def norm_tiles(t, n):
                for k in range(KD):
                    pool.wait_ge(bank_free[(t + k) % 4], (t + k) // 4 + 1)
                    square_tile(h[:, k, :], k, n)
                rstd(n)

            def hidden(t, hhi, hlo, hid0, r):
                for j in range(KD):
                    a = j % 2
                    tt = t + j
                    pool.wait_ge(bank_free[tt % 4], tt // 4 + 1 + 4 * r)
                    pool.tensor_tensor(u_sq[:, a, :], u_tmp[:, a, :], u_tmp[:, a, :], ALU.mult).then_inc(hid_sq, 1)
                    pool.wait_ge(hid_sq, hid0 + 8 * r + j + 1)
                    pool.wait_ge(hid_hi, hid0 + 8 * r + j + 1)
                    pool.tensor_tensor(hlo[:, j, :], u_sq[:, a, :], hhi[:, j, :].bitcast(F32), ALU.subtract)\
                        .then_inc(hid_lo, 1)

            norm_tiles(T["wo_a"], 1)
            with pool.Fori(0, ROUNDS) as r:
                hidden(T["mlp0"], xb_hi, xb_lo, 0, r)
            norm_tiles(T["mlp0"] + 56, 2)
            t = T["dkv"]
            for a in range(2):
                pool.wait_ge(bank_free[(t + a) % 4], (t + a) // 4 + 1)
                square_tile(ckv[:, a, :], a, 3)
            rope(t + 2, k_eo[:, 0, :], k_eo[:, 1, :], rope_tmp2)
            rstd(3)
            for a in range(3):
                pool.wait_ge(bank_free[(t + 4 + a) % 4], (t + 4 + a) // 4 + 1)
                square_tile(cq_raw[:, a, :], a, 4)
            rstd(4)
            for j in range(2):
                rope(T["uq"] + 2 * j, qr_eo[:, 2 * j, :], qr_eo[:, 2 * j + 1, :], rope_tmp2)
            norm_tiles(T["wo_b"], 5)
            with pool.Fori(0, ROUNDS) as r:
                hidden(T["mlp1"], xa_hi, xa_lo, 8 * ROUNDS, r)
            for k in range(1, KD):
                pool.wait_ge(sq_done, SQ[6] + 2 * k + 2)
                if k >= 2:
                    pool.wait_ge(ssq_done, SSQ[6] + 2 * k - 2)
                for sums, src in ((ssq, squares), (sq_tmp, squares_g)):
                    pool.tensor_tensor(sums[:, :], src[:, 0, :] if k == 1 else sums[:, :], src[:, k, :],
                                       ALU.add).then_inc(ssq_done, 1)
            rstd(6)
            rstd(7)

            for c in range(*POOL_LO):
                if c == POOL_LO[0]:
                    pool.wait_ge(wlo_done, c)
                pool.wait_ge(whi_done, c + 1)
                pool.tensor_tensor(wlo[c % 2][:, :], raw[c % 2][:, :], whi[c % 2][:, :].bitcast(F32),
                                   ALU.subtract).then_inc(wlo_done, 1)

            def window(dst, src, shift, low):
                pool.tensor_tensor(dst[:, low:PAD + S], src[:, low:PAD + S], src[:, low - shift:PAD + S - shift],
                                   ALU.add).then_inc(pool_s_done, 1)

            for a in range(2):
                tt = T_PROJ[2 + a]
                pool.wait_ge(bank_free[tt % 4], tt // 4 + 1)
                pool.tensor_tensor(conv_in[:, a, :], conv_in[:, a, :], conv_gate[:, a, :], ALU.mult).then_inc(conv_x, 1)
            pool.wait_ge(pool_zero, 1)
            steps = 0
            for a, windows in ((0, ((0, 1, 1), (1, 2, 3))), (1, ((2, 1, 1), (3, 2, 3), (2, 4, 7), (3, 8, 15)))):
                tt = T_PROJ[4 + a]
                pool.wait_ge(bank_free[tt % 4], tt // 4 + 1)
                src = pool_v[:, a, :]
                for dst, shift, low in windows:
                    if steps:
                        pool.wait_ge(pool_s_done, steps)
                    window(pool_s[dst], src, shift, low)
                    src = pool_s[dst]
                    steps += 1
            for a in range(2):
                tt = T_PROJ[6 + a]
                pool.wait_ge(bank_free[tt % 4], tt // 4 + 1)
                pool.wait_ge(conv_step, 3 * (a + 1))
                pool.tensor_tensor(conv_y[:, a, :], conv_y[:, a, :], conv_gate[:, a, :], ALU.mult).then_inc(conv_out, 1)

            def onto_residual(n0, n):
                for k in RES_POOL:
                    pool.wait_ge(branch_done, KD * n0 + k + 1)
                    pool.tensor_tensor(h[:, k, :], h[:, k, :], branch[:, k, :], ALU.add).then_inc(res_pool, 1)
                add_squares(squares2, n)

            add_squares(squares2, 8)
            onto_residual(0, 9)

            def gate_up(r, n):
                t = T[f"gu{r}"]

                def pair(i):
                    for s in range(2):
                        j = HID2 + 8 * r + 2 * i + s
                        tt = t + 2 * s + 1
                        pool.wait_ge(bank_free[tt % 4], tt // 4 + 1 + i)
                        pool.wait_ge(silu_done, j - HID2 + 1)
                        pool.wait_ge(hid_lo, j - 1)
                        pool.tensor_tensor(hid_t[:, s, :], silu_t[:, s, :], up_t[:, s, :], ALU.mult).then_inc(hid_sq, 1)
                        pool.wait_ge(hid_sq, j + 1)
                        pool.wait_ge(hid_hi, j + 1)
                        pool.tensor_tensor(xa_lo[:, 2 * i + s, :], hid_t[:, s, :],
                                           xa_hi[:, 2 * i + s, :].bitcast(F32), ALU.subtract).then_inc(hid_lo, 1)

                with pool.Fori(0, n // 2) as i:
                    pair(i)

            for r, n in enumerate(GU_TILES):
                gate_up(r, n)
            add_squares(squares2, 10)
            onto_residual(1, 11)

            for k in range(KD - 2):
                pool.wait_ge(silu_done, N_SILU + k + 1)
                pool.tensor_tensor(projected[:, k, :], projected[:, k, :], silu_t[:, k % 2, :], ALU.mult)\
                    .then_inc(gated_done, 1)


def pack_weights(inp):
    chunks = []

    def put(w, cols, k_tiles=KD):
        a = w[:, cols].reshape(k_tiles, P, len(cols)).transpose(1, 0, 2).reshape(P, -1)
        full = np.zeros((P, CHUNK), a.dtype)
        full[:, :a.shape[1]] = a
        chunks.append(full)

    def put_all(w, width=256):
        for n in range(0, w.shape[1], width):
            put(w, np.arange(n, n + width), w.shape[0] // P)

    def put_mlp(up, down):
        for r in range(ROUNDS):
            put_all(up[:, r * D:(r + 1) * D])
            put_all(down[r * D:(r + 1) * D])

    w = inp["w_qkv_a"][0]
    for j in range(4):
        for part in range(2):
            cols = [part * D + 64 * (4 * j + comp) + 32 * half + r
                    for half in range(2) for comp in range(4) for r in range(32)]
            put(w, np.array(cols))
    put_all(w[:, 2 * D:])
    put_all(inp["w_o_a"][0])
    put_mlp(inp["w_up"][0], inp["w_down"][0])
    dkv, ukv, dq, uq = inp["w_dkv"], inp["w_ukv"], inp["w_dq"][0], inp["w_uq"][0]
    put(dkv, np.arange(256))
    put(dkv, np.concatenate([np.tile(np.arange(256 + 32 * half, 288 + 32 * half), 4) for half in range(2)]))
    put(dq, np.arange(256))
    put(dq, np.concatenate([np.arange(256, 384)] * 2))
    heads = np.arange(HEADS)[:, None]
    for part in range(2):
        put(ukv, (256 * heads + 128 * part + np.arange(128)).ravel(), 2)
    put(uq, np.concatenate([(192 * heads[4 * j:4 * j + 4] + 128 + 32 * half + np.arange(32)).ravel()
                            for j in range(2) for half in range(2)]), 3)
    for part in range(2):
        put(uq, (192 * heads[4 * part:4 * part + 4] + np.arange(128)).ravel(), 3)
    put_all(inp["w_o_b"][0])
    put_mlp(inp["w_up"][1], inp["w_down"][1])
    w = inp["w_in_2"][0]
    at = dict(a_in=0, a_c=256, a_b=512, pv=768, cq=1024, ck=1280, cv=1536, iq=1792, ik=2304, iw=2368, dq=2376, dk=2632, dv=2888)
    put_all(w[:, at["iq"]:at["iq"] + 512])
    put(w, np.concatenate([at["ik"] + np.arange(64), at["iw"] + np.arange(IDX_HEADS), np.full(256 - 64 - IDX_HEADS, at["ik"])]))
    for name in ("cq", "ck", "cv", "dq", "dk", "dv", "a_in", "a_c", "pv", "a_b"):
        put(w, at[name] + np.arange(256))
    wo = inp["w_out_2"][0].reshape(KD, P, D)
    order = np.zeros(KD, int)
    for tiles, first in ((MIX_CONV, 0), (MIX_POOL, 2), (MIX_PAIR[2:], 4), (MIX_PAIR[:2], 6)):
        order[list(tiles)] = first, first + 1
    put_all(wo[order].reshape(D, D))
    proj, gate_up, down = inp["w_ple_proj_2"][0], inp["w_gate_up_2"][0], inp["w_down_2"][0]
    put(proj, np.arange(512), 2)
    tile0 = 0
    for n in GU_TILES:
        for j in range(tile0, tile0 + n):
            put(gate_up, np.concatenate([j * P + np.arange(P), down.shape[0] + j * P + np.arange(P)]))
        put_all(down[tile0 * P:(tile0 + n) * P])
        tile0 += n
    put(proj, 512 + np.arange(512), 2)
    put_all(inp["w_ple_gate_2"][0])
    assert len(chunks) == N_CHUNKS
    return np.stack(chunks)


def pack_gains(inp):
    vectors = [inp["attn_norm_g"][0], inp["attn_norm_g"][1], inp["kv_in_norm_g"], inp["mlp_norm_g"][0],
               inp["mlp_norm_g"][1], inp["final_norm_g"], inp["g_mix_pre_2"][0], inp["g_mix_post_2"][0],
               inp["g_ffn_pre_2"][0], inp["g_ffn_post_2"][0], inp["g_ple_2"][0], inp["kv_norm_g"],
               inp["q_norm_g"][0], inp["subln_g"][0], inp["pool_scale_2"][0], inp["conv_w_2"][0].reshape(-1)]
    return np.ascontiguousarray(np.concatenate([v.reshape(-1, P) for v in vectors]).T)


def rope_tables():
    inv_freq = np.float32(10000.0) ** (-np.arange(0, 64, 2, dtype=np.float32) / np.float32(64))
    ang = inv_freq[:, None] * np.arange(S, dtype=np.float32)[None, :]
    return np.tile(np.cos(ang), (4, 1)).astype(np.float32), np.tile(np.sin(ang), (4, 1)).astype(np.float32)


def distance_buckets():
    dist = np.maximum(2 * P - 1 - np.arange(ROWS), 0)
    exact = BUCKETS // 2
    large = exact + (np.log(np.maximum(dist, 1).astype(np.float32) / np.float32(exact))
                     / np.float32(np.log(MAX_DIST / exact)) * np.float32(BUCKETS - exact)).astype(np.int32)
    bucket = np.where(dist < exact, dist, np.minimum(large, BUCKETS - 1))
    eye = np.eye(BUCKETS, dtype=np.float32)
    out = eye[:, BUCKETS - 1:] - eye[:, bucket]
    out[:, 2 * P:] = 0.0
    return np.ascontiguousarray(out)


def pool_counts():
    out = np.ones((P, 2, PAD), np.float32)
    for a, rows, _, w in POOL_GROUPS:
        out[rows, a, :] = w / np.minimum(np.arange(PAD) + 1, w)
    return out.reshape(P, -1)


def pool_blocks(w):
    out = np.zeros((P, 2, P), w.dtype)
    for j in range(4):
        rows = slice(64 * (j % 2), 64 * (j % 2) + 64)
        out[rows, j // 2, rows] = w[j]
    return out.reshape(P, -1)


def lay_out(inp):
    cos, sin = rope_tables()
    return {
        "pT_in": np.ascontiguousarray(inp["p_2"][0, 0].T), "tab_in": np.ascontiguousarray(inp["rel_bias_2"].T),
        "buckets_in": distance_buckets(), "pool_w_in": pool_blocks(inp["pool_w_2"][0]), "pool_fix_in": pool_counts(),
        "wst": pack_weights(inp), "xT": np.ascontiguousarray(inp["x"][0].T), "gains": pack_gains(inp),
        "cos": cos, "sin": sin, "ident_in": np.eye(P, dtype=np.float32),
        "mask_in": np.triu(np.full((P, P), BIG, np.float32), 1),
        "lam": np.concatenate([inp["lambda_q1"], inp["lambda_k1"], inp["lambda_q2"], inp["lambda_k2"]], 1),
    }


def kernel(**inputs):
    from concourse import bacc
    from concourse.bass_utils import run_bass_kernel_spmd

    nc = bacc.Bacc("TRN2", target_bir_lowering=False, num_devices=1)
    arrays = lay_out({name: np.asarray(a) for name, a in inputs.items()})
    args = {name: nc.dram_tensor(name, a.shape, mybir.dt.from_np(a.dtype), kind="ExternalInput").ap()
            for name, a in arrays.items()}
    out = nc.dram_tensor("outT", (D, S), F32, kind="ExternalOutput").ap()
    build(nc, outT=out, **args)
    result = run_bass_kernel_spmd(nc, [arrays], core_ids=[0])
    return np.ascontiguousarray(result.results[0]["outT"].T)[None]
```
